# Optimizing a Trainium2 kernel written in Bass

```python
import jax, jax.numpy as jnp
from jax import lax
import numpy as np

D_MODEL = 1024
BATCH = 1
SEQ = 2048
DEPTH = 2

N_MIXERS = 2
N_META = 16
BLOCK = 128
N_PAD = BLOCK - N_META
BRANCH = D_MODEL
HG_DK = 128
HG_DV = 128
HG_HEADS = BRANCH // HG_DV
HG_CHUNK = BLOCK
HG_SUB = 16
N_SUB = HG_CHUNK // HG_SUB
SB_DH = 128
SB_HEADS = BRANCH // SB_DH
SB_SCALE = SB_DH ** -0.5
N_HGRN = (DEPTH + 1) // 2
N_SB = DEPTH // 2
EPS = 1e-6

kernel_name = "hybrid_hgrn2_stickbreaking_meta"

def _rmsnorm(x, w):
    xf = x.astype(jnp.float32)
    y = xf * lax.rsqrt(jnp.mean(xf * xf, axis=-1, keepdims=True) + EPS)
    return (y * w.astype(jnp.float32)).astype(x.dtype)

def _heads(t, n):
    b, l, _ = t.shape
    return t.reshape(b, l, n, -1).transpose(0, 2, 1, 3)

def _pad_front(t):
    return jnp.pad(t, ((0, 0), (0, 0), (N_PAD, 0), (0, 0)))

def _to_blocks(t):
    b, h, lp, d = t.shape
    return t.reshape(b, h, lp // BLOCK, BLOCK, d).transpose(2, 0, 1, 3, 4)

def _hgrn2_chunk(S, inp):
    q, k, v, g = inp
    bsz, h = q.shape[:2]
    b = jnp.cumsum(g, axis=2)
    o = jnp.einsum('bhtd,bhde->bhte', q * jnp.exp(b), S)
    qs = q.reshape(bsz, h, N_SUB, HG_SUB, HG_DK)
    ks = k.reshape(bsz, h, N_SUB, HG_SUB, HG_DK)
    vs = v.reshape(bsz, h, N_SUB, HG_SUB, HG_DV)
    bs = b.reshape(bsz, h, N_SUB, HG_SUB, HG_DK)
    tri = jnp.tril(jnp.ones((HG_SUB, HG_SUB), bool))[:, :, None]
    diff = bs[:, :, :, :, None, :] - bs[:, :, :, None, :, :]
    dec = jnp.exp(jnp.where(tri, diff, -jnp.inf))
    a_diag = jnp.einsum('bhntd,bhntsd,bhnsd->bhnts', qs, dec, ks)
    o_diag = jnp.einsum('bhnts,bhnse->bhnte', a_diag, vs)
    ref = jnp.concatenate([jnp.zeros_like(bs[:, :, :1, 0, :]), bs[:, :, :-1, -1, :]], axis=2)
    q_hat = qs * jnp.exp(bs - ref[:, :, :, None, :])
    lower = (jnp.arange(N_SUB)[None, :] < jnp.arange(N_SUB)[:, None])[:, :, None, None]
    expo = ref[:, :, :, None, None, :] - bs[:, :, None, :, :, :]
    k_hat = ks[:, :, None] * jnp.exp(jnp.where(lower, expo, -jnp.inf))
    a_off = jnp.einsum('bhitd,bhijsd->bhitjs', q_hat, k_hat)
    o_off = jnp.einsum('bhitjs,bhjse->bhite', a_off, vs)
    o = o + (o_diag + o_off).reshape(bsz, h, HG_CHUNK, HG_DV)
    b_last = b[:, :, -1, :]
    S = jnp.exp(b_last)[..., None] * S + jnp.einsum('bhsd,bhse->bhde', k * jnp.exp(b_last[:, :, None, :] - b), v)
    return S, o

def _hgrn2_mixer(y, w_in, lb, out_norm, w_out):
    bsz, l, _ = y.shape
    q, fz, v, gate = jnp.split(y @ w_in, 4, axis=-1)
    q, fz, v = (_heads(t, HG_HEADS).astype(jnp.float32) for t in (q, fz, v))
    lb = lb.reshape(1, HG_HEADS, 1, HG_DK)
    g = jnp.log(lb + (1.0 - lb) * jax.nn.sigmoid(fz))
    k = (1.0 - lb) * jax.nn.sigmoid(-fz)
    xs = tuple(_to_blocks(_pad_front(t)) for t in (q, k, v, g))
    s0 = jnp.zeros((bsz, HG_HEADS, HG_DK, HG_DV), jnp.float32)
    _, o = lax.scan(_hgrn2_chunk, s0, xs)
    nb = o.shape[0]
    o = o.transpose(1, 2, 0, 3, 4).reshape(bsz, HG_HEADS, nb * HG_CHUNK, HG_DV)[:, :, N_PAD:]
    o = _rmsnorm(o.transpose(0, 2, 1, 3), out_norm).reshape(bsz, l, BRANCH)
    return (o.astype(y.dtype) * jax.nn.silu(gate)) @ w_out

def _stick_breaking_mixer(y, w_in, w_out):
    bsz, l, _ = y.shape
    q, k, v, gate = jnp.split(y @ w_in, 4, axis=-1)
    q, k, v = (_pad_front(_heads(t, SB_HEADS).astype(jnp.float32)) for t in (q, k, v))
    lp = l + N_PAD
    s_pos = jnp.arange(lp)
    key_ok = s_pos >= N_PAD

    def block(args):
        qb, n = args
        t_pos = n * BLOCK + jnp.arange(BLOCK)
        valid = (s_pos[None, :] < t_pos[:, None]) & key_ok[None, :]
        z = jnp.einsum('bhtd,bhsd->bhts', qb, k) * SB_SCALE
        log_beta = jax.nn.log_sigmoid(z)
        log_keep = jnp.where(valid, log_beta - z, 0.0)
        later = lax.cumsum(log_keep, axis=3, reverse=True) - log_keep
        a = jnp.where(valid, jnp.exp(log_beta + later), 0.0)
        return jnp.einsum('bhts,bhse->bhte', a, v)

    o = lax.map(block, (_to_blocks(q), jnp.arange(lp // BLOCK)))
    o = o.transpose(1, 0, 3, 2, 4).reshape(bsz, lp, BRANCH)[:, N_PAD:]
    return (o.astype(y.dtype) * jax.nn.silu(gate)) @ w_out

def setup_inputs(seed: int = 0) -> dict:
    key = jax.random.key(seed)
    ks = jax.random.split(key, 11)
    f32 = jnp.float32
    x = jax.random.normal(ks[0], (BATCH, SEQ, D_MODEL), f32)
    meta_tokens = jax.random.normal(ks[1], (N_META, D_MODEL), f32)
    pre_norm = 1.0 + 0.05 * jax.random.normal(ks[2], (DEPTH, D_MODEL), f32)
    post_norm = 1.0 + 0.05 * jax.random.normal(ks[3], (DEPTH, D_MODEL), f32)
    hgrn_w_in = jax.random.normal(ks[4], (N_HGRN, D_MODEL, 4 * BRANCH), f32) * D_MODEL ** -0.5
    hgrn_lb = 0.5 * jax.random.normal(ks[5], (N_HGRN + 1, BRANCH), f32)
    hgrn_out_norm = 1.0 + 0.05 * jax.random.normal(ks[6], (N_HGRN, HG_DV), f32)
    hgrn_w_out = jax.random.normal(ks[7], (N_HGRN, BRANCH, D_MODEL), f32) * BRANCH ** -0.5
    sb_w_in = jax.random.normal(ks[8], (N_SB, D_MODEL, 4 * BRANCH), f32) * D_MODEL ** -0.5
    sb_w_out = jax.random.normal(ks[9], (N_SB, BRANCH, D_MODEL), f32) * BRANCH ** -0.5
    return {"x": x, "meta_tokens": meta_tokens, "pre_norm": pre_norm, "post_norm": post_norm,
            "hgrn_w_in": hgrn_w_in, "hgrn_lb": hgrn_lb, "hgrn_out_norm": hgrn_out_norm,
            "hgrn_w_out": hgrn_w_out, "sb_w_in": sb_w_in, "sb_w_out": sb_w_out}

def reference(x, meta_tokens, pre_norm, post_norm, hgrn_w_in, hgrn_lb, hgrn_out_norm, hgrn_w_out, sb_w_in, sb_w_out):
    bsz = x.shape[0]
    meta = jnp.broadcast_to(meta_tokens[None].astype(x.dtype), (bsz, N_META, D_MODEL))
    h = jnp.concatenate([meta, x], axis=1)
    lbs = jnp.cumsum(jax.nn.softmax(hgrn_lb.astype(jnp.float32), axis=0), axis=0)
    for i in range(DEPTH):
        y = _rmsnorm(h, pre_norm[i])
        j = i // N_MIXERS
        if i % N_MIXERS == 0:
            y = _hgrn2_mixer(y, hgrn_w_in[j], lbs[j], hgrn_out_norm[j], hgrn_w_out[j])
        else:
            y = _stick_breaking_mixer(y, sb_w_in[j], sb_w_out[j])
        h = h + _rmsnorm(y, post_norm[i])
    return h[:, N_META:]


_drawn_inputs = setup_inputs


def setup_inputs(seed=0):
    import zlib

    import numpy as np

    out = dict(_drawn_inputs(seed))
    spreads = {}
    factors = {}
    for name, (base, spread) in spreads.items():
        noise = np.random.default_rng([zlib.crc32(name.encode()), seed]).standard_normal(out[name].shape)
        drawn = base * np.exp(spread * noise) if base else spread * noise
        out[name] = __import__('jax').numpy.asarray(drawn.astype(out[name].dtype))
    for name, factor in factors.items():
        out[name] = (out[name] * factor).astype(out[name].dtype)
    return out
```

```python
from contextlib import ExitStack

import numpy as np

import concourse.bass as bass
from concourse import mybir

F32 = mybir.dt.float32
F32R = mybir.dt.float32r
ALU = mybir.AluOpType
ACT = mybir.ActivationFunctionType
AX_X = mybir.AxisListType.X

P = 128
D = 1024
KT = D // P
HEADS = D // P
SEQ = 2048
META = 16
TOK = META + SEQ
TILES = SEQ // P
EPS = 1e-6
SB_SCALE = float(P) ** -0.5


class Order:

    def __init__(self, sem, keys):
        self.sem, self.keys = sem, list(keys)

    def credit(self, engine):
        engine.sem_inc(self.sem, len(self.keys))

    def previous(self, key, rnd):
        return rnd * len(self.keys) + (self.keys.index(key) + 1)

    def done(self, key, rnd):
        return self.previous(key, rnd) + len(self.keys)


class Space:

    def __init__(self, nc, ctx, stage):
        self.nc, self.ctx, self.stage = nc, ctx, stage

    def sb(self, name, shape, dt=F32):
        return self.ctx.enter_context(self.nc.sbuf_tensor(f"{self.stage}_{name}", shape, dt))

    def ps(self, name, shape):
        return self.ctx.enter_context(self.nc.psum_tensor(f"{self.stage}_{name}", shape, F32))

    def sem(self, name):
        return self.ctx.enter_context(self.nc.semaphore(f"{self.stage}_{name}"))

    def order(self, name, keys):
        return Order(self.sem(name), keys)


class Common:

    def __init__(self, ident, apart):
        self.ident, self.apart = ident, apart

    def wait_apart(self, engine, sem, value):
        engine.wait_ge(sem, value)
        engine.sem_inc(self.apart, 1)


def row_to_all(row):
    return row.unsqueeze(0).broadcast_to([P, row.shape[0]])


META_BUF = 2


def credit(engine, *sems, by=1):
    for sem in sems:
        engine.sem_inc(sem, by)


def walk(engine, tile):
    tile(META_BUF, META, 0, 0)
    with engine.Fori(0, TILES // 2) as pair:
        for b in range(2):
            tile(b, P, pair * 2 + (1 + b), pair)


def walk_ahead(engine, start, finish):
    last = TILES // 2 - 1
    start(META_BUF, META, 0, 0)
    for b in range(2):
        start(b, P, 1 + b, 0)
    finish(META_BUF, META, 0, 0)
    with engine.Fori(0, last) as pair:
        for b in range(2):
            finish(b, P, pair * 2 + (1 + b), pair)
            start(b, P, pair * 2 + (3 + b), pair + 1)
    for b in range(2):
        finish(b, P, last * 2 + 1 + b, last)


def normalise(nc, stage, rows_meta, rows_seq, gain, common, yT_high, yT_low):
    with ExitStack() as ctx:
        s = Space(nc, ctx, stage)
        gain_all = s.sb("gain", [P, D])
        x = [s.sb(f"x{b}", [P, D]) for b in range(3)]
        y = [s.sb(f"y{b}", [P, D]) for b in range(3)]
        squares = [s.sb(f"squares{b}", [P, D]) for b in range(3)]
        sumsq, rms, rstd = (s.sb(n, [P, 4]) for n in ("sumsq", "rms", "rstd"))
        minus_half = s.sb("minus_half", [P, 1])
        yT = [s.ps(f"yT{b}", [P, KT, P]) for b in range(3)]
        gain_in = s.sem("gain_in")
        x_in = [s.sem(f"x_in{b}") for b in range(3)]
        sumsq_ready, rms_ready, rstd_ready, half_ready = (s.sem(n) for n in ("sumsq", "rms", "rstd", "half"))
        y_ready, yT_ready, high_done, low_done = (s.sem(n) for n in ("y", "yT", "high", "low"))
        block = ctx.enter_context(nc.Block())

        def columns(n, b):
            return slice(0, META) if b == 2 else bass.ds(n * P + (META - P), P)

        @block.sync
        def _(sp):
            sp.dma_start(gain_all[:, :], row_to_all(gain)).then_inc(gain_in, 16)
            sp.dma_start(x[2][0:META, :], rows_meta).then_inc(x_in[2], 16)
            with sp.Fori(0, TILES // 2) as pair:
                for b in range(2):
                    sp.wait_ge(y_ready, pair * 2 + (b + 1))
                    sp.dma_start(x[b][:, :], rows_seq[bass.ds(pair * (2 * P) + b * P, P), :]).then_inc(x_in[b], 16)

        @block.scalar
        def _(act):
            credit(act, sumsq_ready, high_done)

            def start(b, rows, n, pair):
                act.wait_ge(x_in[b], pair * 16 + 16)
                nc.scalar.activation(squares[b][0:rows, :], x[b][0:rows, :], ACT.Square,
                                     accum_out=sumsq[0:rows, b:b + 1]).then_inc(sumsq_ready, 1)

            def finish(b, rows, n, pair):
                common.wait_apart(act, yT_ready, n + 2)
                for half in range(2):
                    ks = slice(half * KT // 2, (half + 1) * KT // 2)
                    nc.scalar.activation(yT_high[:, ks, columns(n, b)], yT[b][:, ks, 0:rows], ACT.Copy).then_inc(high_done, 1)

            walk_ahead(act, start, finish)

        @block.gpsimd
        def _(pool):
            nc.gpsimd.memset(minus_half[:, :], -0.5).then_inc(half_ready, 1)
            pool.wait_ge(half_ready, 1)
            credit(pool, rms_ready, rstd_ready)

            def tile(b, rows, n, pair):
                common.wait_apart(pool, sumsq_ready, n + 2)
                nc.gpsimd.tensor_scalar(rms[0:rows, b:b + 1], sumsq[0:rows, b:b + 1], 1.0 / D, EPS,
                                        ALU.mult, ALU.add).then_inc(rms_ready, 1)
                pool.wait_ge(rms_ready, n + 2)
                nc.gpsimd.tensor_tensor(rstd[0:rows, b:b + 1], rms[0:rows, b:b + 1], minus_half[0:rows, :],
                                        ALU.pow).then_inc(rstd_ready, 1)

            walk(pool, tile)

        @block.vector
        def _(dve):
            dve.wait_ge(gain_in, 16)
            credit(dve, y_ready, low_done)

            def start(b, rows, n, pair):
                dve.wait_ge(rstd_ready, n + 2)
                nc.vector.scalar_tensor_tensor(y[b][0:rows, :], x[b][0:rows, :], rstd[0:rows, b:b + 1],
                                               gain_all[0:rows, :], ALU.mult, ALU.mult).then_inc(y_ready, 1)

            def finish(b, rows, n, pair):
                for half in range(2):
                    dve.wait_ge(high_done, n * 2 + (half + 2))
                    ks = slice(half * KT // 2, (half + 1) * KT // 2)
                    nc.vector.tensor_tensor(yT_low[:, ks, columns(n, b)], yT[b][:, ks, 0:rows],
                                            yT_high[:, ks, columns(n, b)].bitcast(F32), ALU.subtract).then_inc(low_done, 1)

            walk_ahead(dve, start, finish)

        @block.tensor
        def _(pe):
            credit(pe, yT_ready)

            def tile(b, rows, n, pair):
                pe.wait_ge(y_ready, n + 2)
                if b != META_BUF:
                    pe.wait_ge(low_done, pair * 4 + (2 * b + 1))
                for k in range(KT):
                    last = nc.tensor.transpose(yT[b][:, k, 0:rows], y[b][0:rows, k * P:(k + 1) * P], common.ident[0:rows, 0:rows])
                last.then_inc(yT_ready, 1)

            walk(pe, tile)


def project(nc, stage, w_in, yT_high, yT_low, proj):
    widths = [416, 416, 416, 416, 400]
    starts = [sum(widths[:g]) for g in range(len(widths))]
    assert sum(widths) == TOK
    G = len(widths)
    CT = 4 * HEADS
    with ExitStack() as ctx:
        s = Space(nc, ctx, stage)
        w = [s.sb(f"w{b}", [P, KT, P]) for b in range(2)]
        w_high = [s.sb(f"wh{b}", [P, KT, P], F32R) for b in range(2)]
        w_low = [s.sb(f"wl{b}", [P, KT, P], F32R) for b in range(2)]
        out_rows = [s.sb(f"out{b}", [P, TOK]) for b in range(2)]
        acc = [s.ps(f"acc{g}", [P, 512]) for g in range(G)]
        w_loaded = [s.sem(f"w_loaded{b}") for b in range(2)]
        stored = [s.sem(f"stored{b}") for b in range(2)]
        high_ready, low_ready = s.sem("high"), s.sem("low")
        products = s.order("products", [(b, g) for b in range(2) for g in range(G)])
        copied = s.order("copied", [(b, g) for b in range(2) for g in range(G)])
        w_cols = w_in.rearrange("(k p) n -> p k n", p=P)
        block = ctx.enter_context(nc.Block())

        @block.sync
        def _(sp):
            credit(sp, *stored, by=16)

            def load(b, pair):
                sp.dma_start(w[b][:, :, :], w_cols[:, :, bass.ds(pair * (2 * P) + b * P, P)]).then_inc(w_loaded[b], 16)

            def store(b, pair):
                sp.wait_ge(copied.sem, copied.done((b, G - 1), pair))
                sp.dma_start(proj[bass.ds(pair * 2 + b, 1), :, :].rearrange("c p t -> (c p) t"),
                             out_rows[b][:, :]).then_inc(stored[b], 16)

            for b in range(2):
                load(b, 0)
            with sp.Fori(0, CT // 2 - 1) as pair:
                for b in range(2):
                    sp.wait_ge(low_ready, pair * 2 + (b + 2))
                    load(b, pair + 1)
                    store(b, pair)
            for b in range(2):
                store(b, CT // 2 - 1)
            for b in range(2):
                sp.wait_ge(stored[b], 16 * (CT // 2) + 16)

        @block.scalar
        def _(act):
            copied.credit(act)

            def split(b, pair):
                act.wait_ge(w_loaded[b], pair * 16 + 16)
                nc.scalar.activation(w_high[b][:, :, :], w[b][:, :, :], ACT.Copy).then_inc(high_ready, 1)

            def read_out(b, pair):
                act.wait_ge(stored[b], pair * 16 + 16)
                for g in range(G):
                    act.wait_ge(products.sem, products.done((b, g), pair))
                    nc.scalar.activation(out_rows[b][:, starts[g]:starts[g] + widths[g]], acc[g][:, 0:widths[g]],
                                         ACT.Copy).then_inc(copied.sem, 1)

            for b in range(2):
                split(b, 0)
            with act.Fori(0, CT // 2 - 1) as pair:
                for b in range(2):
                    read_out(b, pair)
                    split(b, pair + 1)
            for b in range(2):
                read_out(b, CT // 2 - 1)

        @block.vector
        def _(dve):
            credit(dve, low_ready)
            with dve.Fori(0, CT // 2) as pair:
                for b in range(2):
                    dve.wait_ge(high_ready, pair * 2 + (b + 1))
                    dve.wait_ge(products.sem, products.previous((b, G - 1), pair))
                    nc.vector.tensor_tensor(w_low[b][:, :, :], w[b][:, :, :], w_high[b][:, :, :].bitcast(F32),
                                            ALU.subtract).then_inc(low_ready, 1)

        @block.tensor
        def _(pe):
            products.credit(pe)
            with pe.Fori(0, CT // 2) as pair:
                for b in range(2):
                    pe.wait_ge(low_ready, pair * 2 + (b + 2))
                    for g in range(G):
                        if b == 0:
                            pe.wait_ge(copied.sem, copied.previous((1, g), pair))
                        else:
                            pe.wait_ge(copied.sem, copied.done((0, g), pair))
                        t = slice(starts[g], starts[g] + widths[g])
                        for k in range(KT):
                            for n, (wp, yp) in enumerate(((w_high, yT_high), (w_high, yT_low), (w_low, yT_high))):
                                last = nc.tensor.matmul(acc[g][:, 0:widths[g]], wp[b][:, k, :], yp[:, k, t],
                                                        start=(k == 0 and n == 0), stop=(k == KT - 1 and n == 2))
                        last.then_inc(products.sem, 1)


def contract(nc, common, stage, mixed, rstd_rows, w_out, gain, res_meta, res_seq, out_meta, out_seq):
    with ExitStack() as ctx:
        s = Space(nc, ctx, stage)
        HALF = D // 2
        wo_high, wo_low = (s.sb(n, [P, KT, D], F32R) for n in ("wo_high", "wo_low"))
        wo = [s.sb(f"wo{b}", [P, D]) for b in range(2)]
        gain_all = s.sb("gain", [P, D])
        minus_half = s.sb("minus_half", [P, 1])
        m = [s.sb(f"m{b}", [P, KT, P]) for b in range(3)]
        r = [s.sb(f"r{b}", [P, KT, P]) for b in range(3)] if rstd_rows is not None else None
        m_high = [s.sb(f"mh{b}", [P, KT, P], F32R) for b in range(3)]
        m_low = [s.sb(f"ml{b}", [P, KT, P], F32R) for b in range(3)]
        res = [s.sb(f"res{b}", [P, D]) for b in range(3)]
        normed = [s.sb(f"normed{b}", [P, D]) for b in range(3)]
        squares = [s.sb(f"squares{b}", [P, D]) for b in range(3)]
        sumsq, rms, rstd = (s.sb(n, [P, 4]) for n in ("sumsq", "rms", "rstd"))
        acc = [s.ps(f"acc{b}", [P, 2, HALF]) for b in range(3)]
        wo_in = [s.sem(f"wo_in{b}") for b in range(2)]
        m_in = [s.sem(f"m_in{b}") for b in range(3)]
        res_in = [s.sem(f"res_in{b}") for b in range(3)]
        stored = [s.sem(f"stored{b}") for b in range(3)]
        names = ("scaled", "wo_high", "wo_low", "gain_in", "m_high", "m_low", "product", "sumsq", "rms", "rstd", "half",
                 "normed", "summed")
        (scaled_ready, wo_high_ready, wo_low_ready, gain_in, high_ready, low_ready, product, sumsq_ready, rms_ready, rstd_ready,
         half_ready, normed_ready, summed) = (s.sem(n) for n in names)
        block = ctx.enter_context(nc.Block())
        with_meta = out_meta is not None

        def steps(engine, raised, start, finish):
            last = TILES // 2 - 1
            credit(engine, *raised, by=1 if with_meta else 2)
            if with_meta:
                start(META_BUF, META, 0, 0)
            for b in range(2):
                start(b, P, 1 + b, 0)
            if with_meta:
                finish(META_BUF, META, 0, 0)
            with engine.Fori(0, last) as pair:
                for b in range(2):
                    finish(b, P, pair * 2 + (1 + b), pair)
                    start(b, P, pair * 2 + (3 + b), pair + 1)
            for b in range(2):
                finish(b, P, last * 2 + 1 + b, last)

        def nothing(b, rows, n, pair):
            pass

        @block.sync
        def _(sp):
            sp.dma_start(gain_all[:, :], row_to_all(gain)).then_inc(gain_in, 16)
            for k in range(KT):
                if k >= 2:
                    sp.wait_ge(wo_low_ready, k - 1)
                sp.dma_start(wo[k % 2][:, :], w_out[k * P:(k + 1) * P, :]).then_inc(wo_in[k % 2], 16)
            def load(b, n, rows, cols):
                sp.dma_start(m[b][:, :, 0:rows], mixed[:, :, cols].rearrange("k p t -> p k t")).then_inc(m_in[b], 16)
                if r is not None:
                    tile = rstd_rows[:, n:n + 1, 0:rows] if b == META_BUF else rstd_rows[:, bass.ds(n, 1), 0:rows]
                    sp.dma_start(r[b][:, :, 0:rows], tile.rearrange("k n t -> n k t").broadcast_to([P, KT, rows])
                                 ).then_inc(m_in[b], 16)

            def load_residual(b, rows, pair):
                rows_in = res_meta if b == META_BUF else res_seq[bass.ds(pair * (2 * P) + b * P, P), :]
                sp.dma_start(res[b][0:rows, :], rows_in).then_inc(res_in[b], 16)

            def load_tile(b, pair):
                load(b, pair * 2 + (1 + b), P, bass.ds(pair * (2 * P) + (META + b * P), P))

            def store(b, rows, n, pair):
                sp.wait_ge(summed, n + 2)
                to = out_meta if b == META_BUF else out_seq[bass.ds(pair * (2 * P) + b * P, P), :]
                sp.dma_start(to, res[b][0:rows, :]).then_inc(stored[b], 16)

            credit(sp, *stored, by=16)
            last = TILES // 2 - 1
            if with_meta:
                load(META_BUF, 0, META, slice(0, META))
                load_residual(META_BUF, META, 0)
            for b in range(2):
                load_tile(b, 0)
                load_residual(b, P, 0)
            if with_meta:
                store(META_BUF, META, 0, 0)
            with sp.Fori(0, last) as pair:
                for b in range(2):
                    n = pair * 2 + (1 + b)
                    sp.wait_ge(low_ready, n + 2)
                    load_tile(b, pair + 1)
                    store(b, P, n, pair)
                    sp.wait_ge(stored[b], pair * 16 + 32)
                    load_residual(b, P, pair + 1)
            for b in range(2):
                store(b, P, last * 2 + 1 + b, last)
            for b in range(2 + with_meta):
                sp.wait_ge(stored[b], 32 if b == META_BUF else 16 * (TILES // 2) + 16)

        @block.scalar
        def _(act):
            for k in range(KT):
                act.wait_ge(wo_in[k % 2], 16 * (k // 2 + 1))
                nc.scalar.activation(wo_high[:, k, :], wo[k % 2][:, :], ACT.Copy).then_inc(wo_high_ready, 1)

            def start(b, rows, n, pair):
                if r is None:
                    act.wait_ge(m_in[b], pair * 16 + 16)
                else:
                    act.wait_ge(scaled_ready, n + 2)
                nc.scalar.activation(m_high[b][:, :, 0:rows], m[b][:, :, 0:rows], ACT.Copy).then_inc(high_ready, 1)

            def finish(b, rows, n, pair):
                act.wait_ge(product, n + 2)
                nc.scalar.activation(squares[b][0:rows, :], acc[b][0:rows, :, :].rearrange("p h n -> p (h n)"), ACT.Square,
                                     accum_out=sumsq[0:rows, b:b + 1]).then_inc(sumsq_ready, 1)

            steps(act, (high_ready, sumsq_ready), start, finish)

        @block.gpsimd
        def _(pool):
            nc.gpsimd.memset(minus_half[:, :], -0.5).then_inc(half_ready, 1)
            pool.wait_ge(half_ready, 1)

            def tile(b, rows, n, pair):
                common.wait_apart(pool, sumsq_ready, n + 2)
                nc.gpsimd.tensor_scalar(rms[0:rows, b:b + 1], sumsq[0:rows, b:b + 1], 1.0 / D, EPS,
                                        ALU.mult, ALU.add).then_inc(rms_ready, 1)
                pool.wait_ge(rms_ready, n + 2)
                nc.gpsimd.tensor_tensor(rstd[0:rows, b:b + 1], rms[0:rows, b:b + 1], minus_half[0:rows, :],
                                        ALU.pow).then_inc(rstd_ready, 1)
                pool.wait_ge(res_in[b], pair * 16 + 16)
                pool.wait_ge(normed_ready, n + 2)
                nc.gpsimd.tensor_tensor(res[b][0:rows, :], normed[b][0:rows, :], res[b][0:rows, :],
                                        ALU.add).then_inc(summed, 1)

            steps(pool, (rms_ready, rstd_ready, summed), nothing, tile)

        @block.vector
        def _(dve):
            for k in range(KT):
                dve.wait_ge(wo_high_ready, k + 1)
                nc.vector.tensor_tensor(wo_low[:, k, :], wo[k % 2][:, :], wo_high[:, k, :].bitcast(F32),
                                        ALU.subtract).then_inc(wo_low_ready, 1)
            dve.wait_ge(gain_in, 16)

            def start(b, rows, n, pair):
                if r is not None:
                    dve.wait_ge(m_in[b], pair * 32 + 32)
                    nc.vector.tensor_tensor(m[b][:, :, 0:rows], m[b][:, :, 0:rows], r[b][:, :, 0:rows], ALU.mult
                                            ).then_inc(scaled_ready, 1)
                dve.wait_ge(high_ready, n + 2)
                if b != META_BUF:
                    dve.wait_ge(product, pair * 2 + (b + 1))
                nc.vector.tensor_tensor(m_low[b][:, :, 0:rows], m[b][:, :, 0:rows], m_high[b][:, :, 0:rows].bitcast(F32),
                                        ALU.subtract).then_inc(low_ready, 1)

            def finish(b, rows, n, pair):
                dve.wait_ge(rstd_ready, n + 2)
                if b != META_BUF:
                    dve.wait_ge(summed, pair * 2 + (b + 1))
                nc.vector.scalar_tensor_tensor(normed[b][0:rows, :], acc[b][0:rows, :, :].rearrange("p h n -> p (h n)"),
                                               rstd[0:rows, b:b + 1], gain_all[0:rows, :],
                                               ALU.mult, ALU.mult).then_inc(normed_ready, 1)

            steps(dve, (low_ready, normed_ready, scaled_ready), start, finish)

        @block.tensor
        def _(pe):
            pe.wait_ge(wo_low_ready, KT)

            def tile(b, rows, n, pair):
                pe.wait_ge(low_ready, n + 2)
                if b != META_BUF:
                    pe.wait_ge(normed_ready, pair * 2 + (b + 1))
                for k in range(KT):
                    for mp, wps in ((m_high, (wo_high, wo_low)), (m_low, (wo_high,))):
                        for half in range(2):
                            cols = slice(half * HALF, (half + 1) * HALF)
                            for wp in wps:
                                last = nc.tensor.matmul(acc[b][0:rows, half, :], mp[b][:, k, 0:rows], wp[:, k, cols],
                                                        start=(k == 0 and mp is m_high and wp is wo_high),
                                                        stop=(k == KT - 1 and mp is m_low))
                last.then_inc(product, 1)

            steps(pe, (product,), nothing, tile)


UNITS = ("m", 0, 1, 2, 3)
GROUP = 4 * P
SMALL = (1, 2, 4, 8, 16)
SLOT = {"m": 0, 0: 0, 1: 1, 2: 0, 3: 1}


def width(u):
    return META if u == "m" else P


def tokens(u):
    return META if u == "m" else GROUP


def halves(u):
    return [h for h in (1, 2, 4, 8, 16, 32, 64) if h < width(u)]


def recurrence_steps():
    def levels(us, h, *then):
        return [("level", u, h) for u in us] + list(then)

    a, b = (0, 1), (2, 3)
    return ([("gates", "m"), ("turn_v", "m"), ("gates", 0), ("gates", 1)]
            + [("level", "m", h) for h in halves("m")] + [("mask", "m"), ("turn_v", 0), ("turn_v", 1)]
            + levels(a, 1, ("turn_k", "m")) + levels(a, 2, ("carry", "m")) + levels(a, 4, ("out", "m"))
            + levels(a, 8, ("norm", "m"), ("gates", 2), ("gates", 3)) + levels(a, 16, ("mask", 0), ("mask", 1))
            + levels(a, 32) + levels(a, 64, ("spread", 0), ("spread", 1), ("turn_v", 2), ("turn_v", 3))
            + levels(b, 1, ("turn_k", 0)) + levels(b, 2, ("carry", 0), ("turn_k", 1)) + levels(b, 4, ("out", 0), ("carry", 1))
            + levels(b, 8, ("norm", 0), ("out", 1)) + levels(b, 16, ("norm", 1), ("mask", 2), ("mask", 3))
            + levels(b, 32) + levels(b, 64, ("spread", 2), ("spread", 3))
            + [(name, u) for name in ("turn_k", "carry") for u in b] + [(name, u) for u in b for name in ("out", "norm")]
            + [("rms", "all")])


def recurrence(nc, common, stage, proj, lb_logits, out_norm, level_masks, mixed, rstd_rows):
    steps = recurrence_steps()

    def keys(name):
        return [step[1:] if len(step) > 2 else step[1] for step in steps if step[0] == name]

    with ExitStack() as ctx:
        s = Space(nc, ctx, stage)
        q_i, f_i, v_i, g_i = range(4)

        def each(name, shape, dt=F32):
            return {u: s.sb(f"{name}_{u}", shape(u), dt) for u in UNITS}

        raw = each("raw", lambda u: [P, 4, tokens(u)])
        sig = each("sig", lambda u: [P, 2, tokens(u)])
        decay = each("decay", lambda u: [P, tokens(u)])
        gate_sig = each("gate_sig", lambda u: [P, tokens(u)])
        gate = each("gate", lambda u: [P, tokens(u)])
        dq = each("dq", lambda u: [P, tokens(u)])
        dk = each("dk", lambda u: [P, tokens(u)])
        totals = each("totals", lambda u: [P, GROUP])
        v = each("v", lambda u: [P, tokens(u) // width(u), P])
        kT = each("kT", lambda u: [P, tokens(u) // width(u), P])
        state = {u: s.sb(f"state_{u}", [P, 4, P]) for u in (0, 1, 2, 3)}
        scores = each("scores", lambda u: [P, 4, P])
        masked = [s.sb(f"masked{i}", [P, 6, 4, 32]) for i in range(2)]
        diag = each("diag", lambda u: [P, 4, 32])
        squares = each("squares", lambda u: [P, tokens(u)])
        ms = s.sb("ms", [P, 1 + TILES])
        rstd = s.sb("rstd", [P, 1 + TILES])
        rstd_turned = s.sb("rstd_turned", [1 + TILES, P])
        result = each("result", lambda u: [P, tokens(u)])
        mask_rows = s.sb("masks", [P, 6 * 32 + 4])
        masks = mask_rows[:, 0:6 * 32].rearrange("p (l t) -> p l t", t=32)
        own_32 = mask_rows[:, 6 * 32:6 * 32 + 4]
        mean_of = s.sb("mean_of", [P, 1])
        minus_half = s.sb("minus_half", [P, 1 + TILES])
        out_gain = s.sb("out_gain", [P, 1])
        logits = s.sb("logits", [P, 2, HEADS])
        lb_work = s.sb("lb_work", [P, 6, HEADS])
        lb, one_less_lb = s.sb("lb", [P, HEADS]), s.sb("one_less_lb", [P, HEADS])
        lb_now = s.sb("lb_now", [P, 2])

        small = [s.ps(f"small{i}", [P, 8, 4, 32]) for i in range(2)]
        turned_v, turned_k = s.ps("turned_v", [P, 4, P]), s.ps("turned_k", [P, 4, P])
        added = s.ps("added", [P, GROUP])
        o = s.ps("o", [P, GROUP])

        raw_in = {u: s.sem(f"raw_in_{u}") for u in UNITS}
        left = {u: s.sem(f"left_{u}") for u in UNITS}
        consts_in, set_up, exps_made, lb_steps = (s.sem(n) for n in ("consts_in", "set_up", "exps_made", "lb_steps"))
        sig_made = s.order("sig_made", keys("gates"))
        gates_made = s.order("gates_made", keys("gates"))
        silu_made = s.order("silu_made", keys("gates"))
        q_at = s.order("q_at", [k for st in steps if st[0] in ("gates", "level")
                                for k in ([(st[1], 1)] if st[0] == "gates" else [(st[1], 2 * st[2])])])
        total_at = s.order("total_at", [(u, 2 * h) for u, h in keys("level")])
        k_at = s.order("k_at", [(u, 2 * h) for u, h in keys("level")])
        scored = s.order("scored", keys("level"))
        masked_at = s.order("masked_at", [(u, n) for u in keys("mask") for n in range(2)])
        placed = s.order("placed", [u for u in keys("mask") if u != "m"])
        spread = s.order("spread", keys("spread"))
        v_turned, k_turned = s.order("v_turned", keys("turn_v")), s.order("k_turned", keys("turn_k"))
        v_made, k_made = s.order("v_made", keys("turn_v")), s.order("k_made", keys("turn_k"))
        k_added = s.order("k_added", keys("carry"))
        states = s.order("states", [(u, n) for u in keys("carry") for n in range(1 if u == "m" else 4)])
        read, meaned = s.order("read", keys("out")), s.order("meaned", keys("norm"))
        squared = s.order("squared", keys("out"))
        ms_made = s.order("ms_made", keys("norm"))
        mixed_at = s.order("mixed_at", keys("out"))
        rstd_made = s.order("rstd_made", ["all"])
        rstd_on_psum = s.order("rstd_on_psum", ["all"])
        rstd_copied = s.order("rstd_copied", ["all"])
        rstd_left = s.sem("rstd_left")
        head_lb = s.order("head_lb", ["lb"])

        users = [st for st in steps if st[0] in ("carry", "norm", "rms")]
        added_users = {}
        for at, st in enumerate(users):
            name, u = users[at - 1]
            order, key = {"carry": (states, (u, 0 if u == "m" else 3)), "norm": (ms_made, u),
                          "rms": (rstd_copied, "all")}[name]
            added_users[st] = [lambda h, order=order, key=key, at=at:
                               (order, order.done(key, h) if at else order.previous(key, h))]

        proj_h = proj.rearrange("(a h) p t -> h p a t", a=4)

        def span(u):
            return slice(0, META) if u == "m" else slice(META + u * GROUP, META + (u + 1) * GROUP)

        def blocks(u):
            w = width(u)
            return [(i, slice(i * w, (i + 1) * w)) for i in range(tokens(u) // w)]

        def by_halves(tile, u, h):
            return tile[u][:, 0:tokens(u)].rearrange("p (m two h) -> p m two h", two=2, h=h)

        def total(u, h):
            n = tokens(u) // h
            t = decay[u][:, 0:n] if h == 1 else totals[u][:, GROUP - 2 * GROUP // h:GROUP - 2 * GROUP // h + n]
            return t.rearrange("p (m two) -> p m two", two=2) if n > 1 and h < width(u) else t

        with nc.Block() as prologue:
            @prologue.sync
            def _(sp):
                sp.dma_start(mask_rows[:, :], level_masks).then_inc(consts_in, 16)
                sp.dma_start(out_gain[:, :], out_norm.unsqueeze(1)).then_inc(consts_in, 16)
                sp.dma_start(logits[:, :, :], lb_logits).then_inc(consts_in, 16)
                sp.wait_ge(consts_in, 48)

            @prologue.gpsimd
            def _(pool):
                nc.gpsimd.memset(minus_half[:, :], -0.5).then_inc(set_up, 1)
                nc.gpsimd.memset(mean_of[:, :], 1.0 / P).then_inc(set_up, 1)
                nc.gpsimd.memset(ms[:, :], 1.0).then_inc(set_up, 1)
                pool.wait_ge(set_up, 3)

            @prologue.vector
            def _(dve):
                made = 0

                def chained(op):
                    nonlocal made
                    made += 1
                    op.then_inc(lb_steps, 1)
                    dve.wait_ge(lb_steps, made)

                w = lb_work
                dve.wait_ge(consts_in, 48)
                chained(nc.vector.tensor_tensor(w[:, 0, :], logits[:, 0, :], logits[:, 1, :], ALU.max))
                chained(nc.vector.tensor_tensor(w[:, 1, :], logits[:, 0, :], w[:, 0, :], ALU.subtract))
                chained(nc.vector.tensor_tensor(w[:, 2, :], logits[:, 1, :], w[:, 0, :], ALU.subtract))
                dve.wait_ge(exps_made, 1)
                chained(nc.vector.tensor_tensor(w[:, 5, :], w[:, 3, :], w[:, 4, :], ALU.add))
                chained(nc.vector.reciprocal(w[:, 0, :], w[:, 5, :]))
                chained(nc.vector.tensor_tensor(lb[:, :], w[:, 3, :], w[:, 0, :], ALU.mult))
                chained(nc.vector.tensor_scalar(one_less_lb[:, :], lb[:, :], -1.0, 1.0, ALU.mult, ALU.add))

            @prologue.scalar
            def _(act):
                act.wait_ge(lb_steps, 3)
                nc.scalar.activation(lb_work[:, 3:5, :], lb_work[:, 1:3, :], ACT.Exp).then_inc(exps_made, 1)

        block = ctx.enter_context(nc.Block())

        @block.sync
        def _(sp):
            def store_rstd(h):
                sp.wait_ge(rstd_copied.sem, rstd_copied.done("all", h))
                sp.dma_start(rstd_rows[bass.ds(h, 1), :, :].rearrange("h n t -> (h n) t"), rstd_turned[:, :]
                             ).then_inc(rstd_left, 16)

            def load(u, h):
                sp.dma_start(raw[u][:, :, :], proj_h[bass.ds(h, 1), :, :, span(u)].rearrange("h p a t -> (h p) a t")
                             ).then_inc(raw_in[u], 16)

            def store(u, h):
                sp.wait_ge(mixed_at.sem, mixed_at.done(u, h))
                sp.dma_start(mixed[bass.ds(h, 1), :, span(u)].rearrange("h p t -> (h p) t"), result[u][:, :]).then_inc(left[u], 16)

            for u in UNITS:
                load(u, 0)
            with sp.Fori(0, HEADS - 1) as h:
                for u in UNITS:
                    store(u, h)
                    load(u, h + 1)
                store_rstd(h)
            for u in UNITS:
                store(u, HEADS - 1)
            store_rstd(HEADS - 1)
            sp.wait_ge(rstd_left, 16 * HEADS + 16)
            for u in UNITS:
                sp.wait_ge(left[u], 16 * HEADS + 16)

        @block.scalar
        def _(act):
            for x in (sig_made, gates_made, spread, v_made, k_made, squared):
                x.credit(act)
            with act.Fori(0, HEADS) as h:
                act.wait_ge(head_lb.sem, head_lb.done("lb", h))
                for step in steps:
                    name, u = step[0:2]
                    if name == "gates":
                        act.wait_ge(raw_in[u], h * 16 + 16)
                        act.wait_ge(mixed_at.sem, mixed_at.previous(u, h))
                        act.wait_ge(total_at.sem, total_at.previous((u, 2 * halves(u)[-1]), h))
                        act.wait_ge(k_at.sem, k_at.previous((u, 2 * halves(u)[-1]), h))
                        act.wait_ge(k_turned.sem, k_turned.previous(u, h))
                        nc.scalar.activation(sig[u][:, 0, :], raw[u][:, f_i, :], ACT.Sigmoid)
                        nc.scalar.activation(sig[u][:, 1, :], raw[u][:, f_i, :], ACT.Sigmoid, scale=-1.0).then_inc(sig_made.sem, 1)
                        nc.scalar.activation(gate_sig[u][:, :], raw[u][:, g_i, :], ACT.Sigmoid)
                        act.wait_ge(sig_made.sem, sig_made.done(u, h))
                        nc.scalar.activation(decay[u][:, :], sig[u][:, 0, :], ACT.Identity, bias=lb_now[:, 0:1],
                                             scale=lb_now[:, 1:2])
                        nc.scalar.activation(dk[u][:, :], sig[u][:, 1, :], ACT.Copy, scale=lb_now[:, 1:2]
                                             ).then_inc(gates_made.sem, 1)
                    elif name == "turn_v":
                        act.wait_ge(v_turned.sem, v_turned.done(u, h))
                        act.wait_ge(read.sem, read.previous(u, h))
                        act.wait_ge(k_added.sem, k_added.previous(u, h))
                        w, n = width(u), tokens(u) // width(u)
                        nc.scalar.activation(v[u][0:w, :, :], turned_v[0:w, 0:n, :], ACT.Copy).then_inc(v_made.sem, 1)
                    elif name == "turn_k":
                        act.wait_ge(k_turned.sem, k_turned.done(u, h))
                        act.wait_ge(k_added.sem, k_added.previous(u, h))
                        w, n = width(u), tokens(u) // width(u)
                        nc.scalar.activation(kT[u][0:w, :, :], turned_k[0:w, 0:n, :], ACT.Copy).then_inc(k_made.sem, 1)
                    elif name == "spread":
                        act.wait_ge(scored.sem, scored.done((u, 64), h))
                        act.wait_ge(placed.sem, placed.done(u, h))
                        ps = small[SLOT[u]]
                        for p0 in (0, 64):
                            nc.scalar.activation(scores[u][p0:p0 + 32, :, p0 + 32:p0 + 64], ps[p0:p0 + 32, 6, :, :], ACT.Copy)
                        nc.scalar.activation(scores[u][0:64, :, 64:128],
                                             ps[0:64, 0:2, :, :].rearrange("p a b t -> p (a b t)").rearrange("p (b t) -> p b t", t=64),
                                             ACT.Copy).then_inc(spread.sem, 1)
                    elif name == "out":
                        act.wait_ge(read.sem, read.done(u, h))
                        nc.scalar.activation(squares[u][:, :], o[:, 0:tokens(u)], ACT.Square).then_inc(squared.sem, 1)

        @block.gpsimd
        def _(pool):
            for x in (silu_made, k_at, placed, rstd_made):
                x.credit(pool)
            with pool.Fori(0, HEADS) as h:
                for step in steps:
                    name, u = step[0:2]
                    if name == "gates":
                        pool.wait_ge(gates_made.sem, gates_made.done(u, h))
                        nc.gpsimd.tensor_tensor(gate[u][:, :], raw[u][:, g_i, :], gate_sig[u][:, :], ALU.mult
                                                ).then_inc(silu_made.sem, 1)
                    elif name == "level":
                        half = step[2]
                        pool.wait_ge(scored.sem, scored.done((u, half), h))
                        if half > 1:
                            pool.wait_ge(total_at.sem, total_at.done((u, half), h))
                            pool.wait_ge(k_at.sem, k_at.done((u, half), h))
                        left_half = by_halves(dk, u, half)[:, :, 0, :]
                        right_total = total(u, half)[:, :, 1:2].broadcast_to(list(left_half.shape))
                        nc.gpsimd.tensor_tensor(left_half, left_half, right_total, ALU.mult).then_inc(k_at.sem, 1)
                    elif name == "mask" and u != "m":
                        pool.wait_ge(masked_at.sem, masked_at.done((u, 1), h))
                        pool.wait_ge(read.sem, read.previous(u, h))
                        nc.gpsimd.tensor_tensor(scores[u][:, :, :].rearrange("p b (i t) -> p b i t", t=32),
                                                diag[u][:, :, :].unsqueeze(2).broadcast_to([P, 4, 4, 32]),
                                                own_32[:, :].unsqueeze(1).unsqueeze(3).broadcast_to([P, 4, 4, 32]),
                                                ALU.mult).then_inc(placed.sem, 1)
                    elif name == "rms":
                        pool.wait_ge(ms_made.sem, ms_made.done(3, h))
                        pool.wait_ge(rstd_on_psum.sem, rstd_on_psum.previous("all", h))
                        nc.gpsimd.tensor_tensor(rstd[:, :], ms[:, :], minus_half[:, :], ALU.pow).then_inc(rstd_made.sem, 1)

        @block.vector
        def _(dve):
            for x in (q_at, total_at, masked_at, states, ms_made, mixed_at, rstd_copied, head_lb):
                x.credit(dve)
            for sem in (*left.values(), rstd_left):
                dve.sem_inc(sem, 16)

            def head_bound(rnd, when):
                nc.vector.tensor_copy(lb_now[:, 0:1], lb[:, bass.ds(when, 1)])
                nc.vector.tensor_copy(lb_now[:, 1:2], one_less_lb[:, bass.ds(when, 1)]).then_inc(head_lb.sem, 1)

            with dve.Fori(0, HEADS) as h:
                dve.wait_ge(gates_made.sem, gates_made.previous(3, h))
                head_bound(h, h)
                for step in steps:
                    name, u = step[0:2]
                    n = 0 if u == "all" else tokens(u)
                    if name == "gates":
                        dve.wait_ge(gates_made.sem, gates_made.done(u, h))
                        nc.vector.tensor_tensor(dq[u][:, :], raw[u][:, q_i, :], decay[u][:, :], ALU.mult).then_inc(q_at.sem, 1)
                    elif name == "level":
                        half = step[2]
                        pairs = total(u, half)
                        if half > 1:
                            dve.wait_ge(total_at.sem, total_at.done((u, half), h))
                        dve.wait_ge(k_at.sem, k_at.previous((u, halves(u)[-1] * 2), h))
                        wide = total(u, 2 * half)
                        out = wide if len(wide.shape) == 2 else wide.rearrange("p m two -> p (m two)")
                        nc.vector.tensor_tensor(out.unsqueeze(2), pairs[:, :, 0:1], pairs[:, :, 1:2], ALU.mult
                                                ).then_inc(total_at.sem, 1)
                        dve.wait_ge(scored.sem, scored.done((u, half), h))
                        dve.wait_ge(q_at.sem, q_at.done((u, half), h))
                        right_half = by_halves(dq, u, half)[:, :, 1, :]
                        nc.vector.tensor_tensor(right_half, right_half, pairs[:, :, 0:1].broadcast_to(list(right_half.shape)),
                                                ALU.mult).then_inc(q_at.sem, 1)
                    elif name == "mask":
                        last_small = min(16, halves(u)[-1])
                        dve.wait_ge(scored.sem, scored.done((u, last_small), h))
                        levels = 1 + len([x for x in halves(u) if x <= 16])
                        w, nb = min(32, width(u)), n // width(u)
                        rows = slice(0, P if u != "m" else w)
                        nc.vector.tensor_tensor(masked[SLOT[u]][rows, 0:levels, 0:nb, 0:w], small[SLOT[u]][rows, 0:levels, 0:nb, 0:w],
                                                masks[rows, 0:levels, 0:w].unsqueeze(2).broadcast_to([rows.stop, levels, nb, w]),
                                                ALU.mult).then_inc(masked_at.sem, 1)
                        dve.wait_ge(masked_at.sem, masked_at.done((u, 0), h))
                        if u == "m":
                            dve.wait_ge(read.sem, read.previous(u, h))
                        else:
                            dve.wait_ge(placed.sem, placed.previous(u, h))
                        nc.vector.tensor_reduce(diag[u][rows, 0:nb, 0:w],
                                                masked[SLOT[u]][rows, 0:levels, 0:nb, 0:w].rearrange("p l b t -> p b t l"),
                                                AX_X, ALU.add).then_inc(masked_at.sem, 1)
                    elif name == "carry":
                        dve.wait_ge(k_added.sem, k_added.done(u, h))
                        if u == "m":
                            dve.wait_ge(read.sem, read.previous(0, h))
                            nc.vector.tensor_copy(state[0][:, 0, :], added[:, 0:P]).then_inc(states.sem, 1)
                        else:
                            dve.wait_ge(total_at.sem, total_at.done((u, P), h))
                            if u < 3:
                                dve.wait_ge(read.sem, read.previous(u + 1, h))
                            for i in range(4):
                                if u == 3 and i == 3:
                                    dve.sem_inc(states.sem, 1)
                                    continue
                                before = (u, i - 1) if i else (("m", 0) if u == 0 else (u - 1, 3))
                                dve.wait_ge(states.sem, states.done(before, h))
                                to = state[u][:, i + 1, :] if i < 3 else state[u + 1][:, 0, :]
                                nc.vector.scalar_tensor_tensor(to, state[u][:, i, :], total(u, P)[:, i:i + 1],
                                                               added[:, i * P:(i + 1) * P], ALU.mult, ALU.add
                                                               ).then_inc(states.sem, 1)
                    elif name == "norm":
                        dve.wait_ge(meaned.sem, meaned.done(u, h))
                        dve.wait_ge(rstd_made.sem, rstd_made.previous("all", h))
                        nb, first = n // width(u), 0 if u == "m" else 1 + 4 * u
                        nc.vector.tensor_scalar(ms[0:width(u), first:first + nb], added[0:width(u), 0:nb], EPS, None, ALU.add
                                                ).then_inc(ms_made.sem, 1)
                    elif name == "out":
                        dve.wait_ge(read.sem, read.done(u, h))
                        dve.wait_ge(squared.sem, squared.done(u, h))
                        dve.wait_ge(silu_made.sem, silu_made.done(u, h))
                        dve.wait_ge(left[u], h * 16 + 16)
                        nc.vector.scalar_tensor_tensor(result[u][:, :], o[:, 0:n], out_gain[:, 0:1], gate[u][:, :],
                                                       ALU.mult, ALU.mult).then_inc(mixed_at.sem, 1)
                    elif name == "rms":
                        dve.wait_ge(rstd_on_psum.sem, rstd_on_psum.done("all", h))
                        dve.wait_ge(rstd_left, h * 16 + 16)
                        nc.vector.tensor_copy(rstd_turned[:, :], added[0:1 + TILES, 0:P]).then_inc(rstd_copied.sem, 1)


        @block.tensor
        def _(pe):
            for x in (scored, v_turned, k_turned, k_added, read, meaned, rstd_on_psum):
                x.credit(pe)
            vs, ks, os = keys("turn_v"), keys("turn_k"), keys("out")

            def wait_apart(order, value):
                common.wait_apart(pe, order.sem, value)

            def before(order, ring, u, rnd):
                at = ring.index(u)
                return order.done(ring[at - 1], rnd) if at else order.previous(ring[-1], rnd)

            with pe.Fori(0, HEADS) as h:
                for step in steps:
                    name, u = step[0:2]
                    w = 0 if u == "all" else width(u)
                    if name == "turn_v":
                        common.wait_apart(pe, raw_in[u], h * 16 + 16)
                        wait_apart(v_made, v_made.previous(vs[-1], h) if u == vs[0] else v_made.done(vs[vs.index(u) - 1], h))
                        for i, cols in blocks(u):
                            last = nc.tensor.transpose(turned_v[0:w, i, :], raw[u][:, v_i, cols], common.ident[:, :])
                        last.then_inc(v_turned.sem, 1)
                    elif name == "level":
                        half, ps = step[2], small[SLOT[u]]
                        if half == 1:
                            wait_apart(q_at, q_at.done((u, 1), h))
                            if u == "m":
                                wait_apart(spread, spread.previous(2, h))
                            elif u == 0:
                                wait_apart(masked_at, masked_at.done(("m", 1), h))
                            elif u == 1:
                                wait_apart(spread, spread.previous(3, h))
                            else:
                                wait_apart(spread, spread.done(u - 2, h))
                        else:
                            wait_apart(q_at, q_at.done((u, half), h))
                            wait_apart(k_at, k_at.done((u, half), h))
                        if half == 32:
                            wait_apart(masked_at, masked_at.done((u, 0), h))
                        if half == 64:
                            half64 = ps[0:64, 0:2, :, :].rearrange("p a b t -> p (a b t)").rearrange("p (b t) -> p b t", t=64)
                        for i, cols in blocks(u):
                            c = cols.start
                            if half == 64:
                                last = nc.tensor.matmul(half64[:, i, :], dk[u][:, c:c + 64], dq[u][:, c + 64:c + 128],
                                                        start=True, stop=True)
                            elif half == 32:
                                for p0 in (0, 64):
                                    last = nc.tensor.matmul(ps[p0:p0 + 32, 6, i, :], dk[u][:, c + p0:c + p0 + 32],
                                                            dq[u][:, c + p0 + 32:c + p0 + 64], start=True, stop=True)
                            else:
                                level = half.bit_length()
                                for p0 in range(0, w, 32):
                                    n = min(32, w)
                                    part = slice(c + p0, c + p0 + n)
                                    if half == 1:
                                        nc.tensor.matmul(ps[p0:p0 + n, 0, i, 0:n], dk[u][:, part], raw[u][:, q_i, part],
                                                         start=True, stop=True)
                                    last = nc.tensor.matmul(ps[p0:p0 + n, level, i, 0:n], dk[u][:, part], dq[u][:, part],
                                                            start=True, stop=True)
                        last.then_inc(scored.sem, 1)
                    elif name == "turn_k":
                        wait_apart(k_at, k_at.done((u, w), h))
                        wait_apart(k_made, k_made.previous(ks[-1], h) if u == ks[0] else k_made.done(ks[ks.index(u) - 1], h))
                        for i, cols in blocks(u):
                            last = nc.tensor.transpose(turned_k[0:w, i, :], dk[u][:, cols], common.ident[:, :])
                        last.then_inc(k_turned.sem, 1)
                    elif name == "carry":
                        wait_apart(v_made, v_made.done(u, h))
                        wait_apart(k_made, k_made.done(u, h))
                        for prior in added_users[("carry", u)]:
                            wait_apart(*prior(h))
                        for i, cols in blocks(u):
                            last = nc.tensor.matmul(added[:, i * P:(i + 1) * P], kT[u][0:w, i, :], v[u][0:w, i, :],
                                                    start=True, stop=True)
                        last.then_inc(k_added.sem, 1)
                    elif name == "out":
                        wait_apart(mixed_at, mixed_at.previous(os[-1], h) if u == os[0]
                                   else mixed_at.done(os[os.index(u) - 1], h))
                        if u == "m":
                            wait_apart(masked_at, masked_at.done((u, 1), h))
                            last = nc.tensor.matmul(o[:, 0:w], v[u][0:w, 0, :], diag[u][0:w, 0, 0:w], start=True, stop=True)
                        else:
                            wait_apart(placed, placed.done(u, h))
                            wait_apart(spread, spread.done(u, h))
                            wait_apart(states, states.done((u, 2), h))
                            for i, cols in blocks(u):
                                nc.tensor.matmul(o[:, cols], v[u][:, i, :], scores[u][:, i, :], start=True, stop=False)
                                last = nc.tensor.matmul(o[:, cols], state[u][:, i, :], dq[u][:, cols], start=False, stop=True)
                        last.then_inc(read.sem, 1)
                    elif name == "norm":
                        wait_apart(squared, squared.done(u, h))
                        for prior in added_users[("norm", u)]:
                            wait_apart(*prior(h))
                        for i, cols in blocks(u):
                            last = nc.tensor.matmul(added[0:w, i:i + 1], squares[u][:, cols], mean_of[:, 0:1],
                                                    start=True, stop=True)
                        last.then_inc(meaned.sem, 1)
                    elif name == "rms":
                        wait_apart(rstd_made, rstd_made.done("all", h))
                        for prior in added_users[("rms", "all")]:
                            wait_apart(*prior(h))
                        nc.tensor.transpose(added[0:1 + TILES, 0:P], rstd[:, :], common.ident[:, :]
                                            ).then_inc(rstd_on_psum.sem, 1)


LEAD = 6


def attention_steps():
    score, values = [], []
    for g in range(4):
        for c in [*range(g, -1, -1), "m"]:
            parts = [0] if c == "m" else range(4)
            score += [("score", g, c, i) for i in parts]
            values += [(g, c, j) for j in parts]
    steps = []

    def add_score(n):
        if n < len(score):
            _, g, c, i = score[n]
            if c == g and i == 0:
                steps.append(("prepare", g))
            steps.append(score[n])

    steps.append(("prepare", "m"))
    for n in range(LEAD):
        add_score(n)
    steps.append(("turn",) + values[0])
    for n, at in enumerate(values):
        add_score(n + LEAD)
        if n + 1 < len(values):
            steps.append(("turn",) + values[n + 1])
        steps.append(("multiply",) + at)
        if at[1] == "m":
            steps.append(("finish", at[0]))
    return steps


def last_user(users, slot_of):
    before = {}
    for n, user in enumerate(users):
        same = [m for m in range(len(users)) if slot_of(users[m]) == slot_of(user)]
        at = same.index(n)
        before[user] = (users[same[at - 1]], at == 0)
    return before


def attention(nc, common, stage, proj, mixed):
    steps = attention_steps()

    def keys(name):
        return [step[1:] if len(step) > 2 else step[1] for step in steps if step[0] == name]

    CHUNKS = ("m", 0, 1, 2, 3)
    with ExitStack() as ctx:
        s = Space(nc, ctx, stage)
        q_i, k_i, v_i, g_i = range(4)
        raw = s.sb("raw", [P, 4, TOK])
        k_high, k_low, q_high, q_low = (s.sb(n, [P, TOK], F32R) for n in ("k_high", "k_low", "q_high", "q_low"))
        v = s.sb("v", [P, 1 + TILES, P])
        gate_sig, gate = s.sb("gate_sig", [P, TOK]), s.sb("gate", [P, TOK])
        keep = [s.sb(f"keep{i}", [P, 4, 512]) for i in range(2)]
        beta = [s.sb(f"beta{i}", [P, 4, 512]) for i in range(2)]
        a = [s.sb(f"a{i}", [P, 4, 512]) for i in range(3)]
        left_over = s.sb("left_over", [P, 4, TOK + 1])
        aT = [s.sb(f"aT{i}", [P, 512]) for i in range(2)]
        result = [s.sb(f"result{i}", [P, 512]) for i in range(2)]
        z = [s.ps(f"z{i}", [P, 512]) for i in range(4)]
        turned = [s.ps(f"turned{i}", [P, 4, P]) for i in range(2)]
        o = [s.ps(f"o{i}", [P, 512]) for i in range(2)]

        raw_in = {c: s.sem(f"raw_in_{c}") for c in CHUNKS}
        stored = [s.sem(f"stored{i}") for i in range(2)]
        high_made, v_made, gate_sig_made, low_made, gate_made = (
            s.order(n, keys("prepare")) for n in ("high", "v_made", "gate_sig", "low", "gate"))
        v_turned = s.order("v_turned", keys("prepare"))
        scored = s.order("scored", keys("score"))
        keep_made, beta_made = s.order("keep_made", keys("score")), s.order("beta_made", keys("score"))
        diagonal = [(g, c, i) for g, c, i in keys("score") if c == g]
        cut_off = s.order("cut_off", diagonal)
        scanned = s.order("scanned", keys("score"))
        a_made = s.order("a_made", keys("score"))
        a_turned = s.order("a_turned", keys("turn"))
        aT_made = s.order("aT_made", keys("turn"))
        multiplied = s.order("multiplied", keys("multiply"))
        finished = s.order("finished", keys("finish"))

        units = [(g, c) for g, c, i in keys("score") if i == 0]
        unit_no = {u: n for n, u in enumerate(units)}

        def tiles_of(c):
            return (0,) if c == "m" else range(4)

        def last_of(c):
            return 0 if c == "m" else 3

        turns = [st for st in steps if st[0] in ("prepare", "turn")]
        turned_slot = {st: n % 2 for n, st in enumerate(turns)}
        turned_before = last_user(turns, lambda st: turned_slot[st])
        aT_slot = {k: n % 2 for n, k in enumerate(keys("turn"))}
        aT_before = last_user(keys("turn"), lambda k: aT_slot[k])
        z_before = last_user(keys("score"), lambda k: k[2])
        sig_before = last_user(units, lambda u: unit_no[u] % 2)
        a_before = last_user(units, lambda u: unit_no[u] % 3)
        o_before = last_user([g for g in range(4)], lambda g: g % 2)
        row_before = last_user(keys("score"), lambda k: (k[1], k[2]))

        proj_h = proj.rearrange("(a h) p t -> h p a t", a=4)
        block = ctx.enter_context(nc.Block())

        def span(c):
            return slice(0, META) if c == "m" else slice(META + c * 512, META + (c + 1) * 512)

        def value(order, key, before, rnd):
            return order.previous(key, rnd) if before else order.done(key, rnd)

        @block.sync
        def _(sp):
            def load(c, h):
                sp.dma_start(raw[:, :, span(c)], proj_h[bass.ds(h, 1), :, :, span(c)].rearrange("h p a t -> (h p) a t")
                             ).then_inc(raw_in[c], 16)

            def reload(c, h):
                for order in (high_made, low_made, v_made) + (() if c == "m" else (gate_made,)):
                    sp.wait_ge(order.sem, order.done(c, h))
                load(c, h + 1)

            def store(g, h):
                sp.wait_ge(finished.sem, finished.done(g, h))
                sp.dma_start(mixed[bass.ds(h, 1), :, span(g)].rearrange("h p t -> (h p) t"), result[g % 2][:, :]
                             ).then_inc(stored[g % 2], 16)

            for c in CHUNKS:
                load(c, 0)
            with sp.Fori(0, HEADS - 1) as h:
                for st in steps:
                    if st[0] == "prepare":
                        reload(st[1], h)
                    elif st[0] == "finish":
                        store(st[1], h)
            for g in range(4):
                store(g, HEADS - 1)
            for i in range(2):
                sp.wait_ge(stored[i], 16 * 2 * HEADS + 16)

        @block.scalar
        def _(act):
            for x in (high_made, v_made, gate_sig_made, keep_made, beta_made):
                x.credit(act)
            with act.Fori(0, HEADS) as h:
                for st in steps:
                    if st[0] == "prepare":
                        c = st[1]
                        cols = span(c)
                        act.wait_ge(raw_in[c], h * 16 + 16)
                        act.wait_ge(scored.sem, scored.previous((3, c, last_of(c)), h))
                        if c != "m":
                            act.wait_ge(finished.sem, finished.previous(c, h))
                            nc.scalar.activation(q_high[:, cols], raw[:, q_i, cols], ACT.Copy)
                            nc.scalar.activation(gate_sig[:, cols], raw[:, g_i, cols], ACT.Sigmoid)
                        nc.scalar.activation(k_high[:, cols], raw[:, k_i, cols], ACT.Copy).then_inc(high_made.sem, 1)
                        act.wait_ge(v_turned.sem, v_turned.done(c, h))
                        act.wait_ge(multiplied.sem, multiplied.previous((3, c, last_of(c)), h))
                        ps = turned[turned_slot[st]]
                        if c == "m":
                            nc.scalar.activation(v[0:META, 0, :], ps[0:META, 0, :], ACT.Copy).then_inc(v_made.sem, 1)
                        else:
                            nc.scalar.activation(v[:, 1 + 4 * c:5 + 4 * c, :], ps[:, :, :], ACT.Copy).then_inc(v_made.sem, 1)
                    elif st[0] == "score":
                        _, g, c, i = st
                        key = (g, c, i)
                        act.wait_ge(scored.sem, scored.done(key, h))
                        (pg, pc), wrapped = sig_before[(g, c)]
                        act.wait_ge(a_made.sem, value(a_made, (pg, pc, 0 if pc == "m" else (i if c != "m" else 3)), wrapped, h))
                        n = unit_no[(g, c)] % 2
                        if c == "m":
                            zi, to_keep, to_beta = z[0][:, 0:4 * META], keep[n][:, :, 0:META], beta[n][:, :, 0:META]
                            zi = zi.rearrange("p (i s) -> p i s", s=META)
                        else:
                            nk = P * (i + 1) if c == g else 512
                            zi, to_keep, to_beta = z[i][:, 0:nk], keep[n][:, i, 0:nk], beta[n][:, i, 0:nk]
                        nc.scalar.activation(to_keep, zi, ACT.Sigmoid, scale=-SB_SCALE).then_inc(keep_made.sem, 1)
                        nc.scalar.activation(to_beta, zi, ACT.Sigmoid, scale=SB_SCALE).then_inc(beta_made.sem, 1)

        @block.gpsimd
        def _(pool):
            for x in (gate_made, cut_off, a_made):
                x.credit(pool)
            with pool.Fori(0, HEADS) as h:
                for st in steps:
                    if st[0] == "prepare" and st[1] != "m":
                        c = st[1]
                        pool.wait_ge(high_made.sem, high_made.done(c, h))
                        pool.wait_ge(finished.sem, finished.previous(c, h))
                        nc.gpsimd.tensor_tensor(gate[:, span(c)], raw[:, g_i, span(c)], gate_sig[:, span(c)], ALU.mult
                                                ).then_inc(gate_made.sem, 1)
                    elif st[0] == "prepare":
                        pool.sem_inc(gate_made.sem, 1)
                    elif st[0] == "score":
                        _, g, c, i = st
                        key = (g, c, i)
                        n, unit = unit_no[(g, c)] % 2, unit_no[(g, c)]
                        if c == g:
                            own = slice(i * P, (i + 1) * P)
                            common.wait_apart(pool, beta_made.sem, beta_made.done(key, h))
                            for tile, fill in ((keep, 1.0), (beta, 0.0)):
                                last = nc.gpsimd.affine_select(out=tile[n][:, i, own], in_=tile[n][:, i, own],
                                                               compare_op=ALU.is_gt, fill=fill, base=0,
                                                               pattern=[[-1, P]], channel_multiplier=1)
                            last.then_inc(cut_off.sem, 1)
                            pool.wait_ge(cut_off.sem, cut_off.done(key, h))
                        else:
                            pool.wait_ge(beta_made.sem, beta_made.done(key, h))
                        pool.wait_ge(scanned.sem, scanned.done(key, h))
                        (pg, pc), wrapped = a_before[(g, c)]
                        pool.wait_ge(a_turned.sem, value(a_turned, (pg, pc, last_of(pc)), wrapped, h))
                        if c == "m":
                            nc.gpsimd.tensor_tensor(a[unit % 3][:, :, 0:META], beta[n][:, :, 0:META],
                                                    left_over[:, :, 1:1 + META], ALU.mult).then_inc(a_made.sem, 1)
                        else:
                            nk, first = (P * (i + 1) if c == g else 512), span(c).start
                            nc.gpsimd.tensor_tensor(a[unit % 3][:, i, 0:nk], beta[n][:, i, 0:nk],
                                                    left_over[:, i, first + 1:first + 1 + nk], ALU.mult
                                                    ).then_inc(a_made.sem, 1)

        @block.vector
        def _(dve):
            for x in (low_made, scanned, aT_made, finished):
                x.credit(dve)
            for sem in stored:
                dve.sem_inc(sem, 16)
            with dve.Fori(0, HEADS) as h:
                for st in steps:
                    if st[0] == "prepare":
                        c = st[1]
                        cols = span(c)
                        dve.wait_ge(high_made.sem, high_made.done(c, h))
                        if c != "m":
                            nc.vector.tensor_tensor(q_low[:, cols], raw[:, q_i, cols], q_high[:, cols].bitcast(F32), ALU.subtract)
                        nc.vector.tensor_tensor(k_low[:, cols], raw[:, k_i, cols], k_high[:, cols].bitcast(F32), ALU.subtract
                                                ).then_inc(low_made.sem, 1)
                    elif st[0] == "score":
                        _, g, c, i = st
                        key = (g, c, i)
                        n, first = unit_no[(g, c)] % 2, span(c).start
                        prior, wrapped = row_before[key]
                        dve.wait_ge(a_made.sem, value(a_made, prior, wrapped, h))
                        if c == g:
                            nk = P * (i + 1)
                            nc.vector.memset(left_over[:, i, first + nk:first + nk + 1], 1.0)
                            dve.wait_ge(cut_off.sem, cut_off.done(key, h))
                        else:
                            nk = META if c == "m" else 512
                            dve.wait_ge(keep_made.sem, keep_made.done(key, h))
                            later = (g, 0 if c == "m" else c + 1, 3 if c == "m" else i)
                            dve.wait_ge(scanned.sem, scanned.done(later, h))
                        for t in (range(4) if c == "m" else (i,)):
                            row = left_over[:, t, first:first + nk]
                            data = keep[n][:, t, 0:nk]
                            start = 1.0 if c == g else left_over[:, t, first + nk:first + nk + 1]
                            last = nc.vector.tensor_tensor_scan(row[:, ::-1], data[:, ::-1], data[:, ::-1], start,
                                                                ALU.mult, ALU.bypass)
                        last.then_inc(scanned.sem, 1)
                    elif st[0] == "turn":
                        _, g, c, j = st
                        key = (g, c, j)
                        dve.wait_ge(a_turned.sem, a_turned.done(key, h))
                        prior, wrapped = aT_before[key]
                        dve.wait_ge(multiplied.sem, value(multiplied, prior, wrapped, h))
                        i0 = j if c == g else 0
                        rows = slice(0, META if c == "m" else P)
                        nc.vector.tensor_copy(aT[aT_slot[key]][rows, i0 * P:512],
                                              turned[turned_slot[st]][rows, i0:4, :].rearrange("p i t -> p (i t)")
                                              ).then_inc(aT_made.sem, 1)
                    elif st[0] == "finish":
                        g = st[1]
                        dve.wait_ge(multiplied.sem, multiplied.done((g, "m", 0), h))
                        dve.wait_ge(gate_made.sem, gate_made.done(g, h))
                        dve.wait_ge(stored[g % 2], h * 32 + (16 + 16 * (g // 2)))
                        nc.vector.tensor_tensor(result[g % 2][:, :], o[g % 2][:, :], gate[:, span(g)], ALU.mult
                                                ).then_inc(finished.sem, 1)

        @block.tensor
        def _(pe):
            for x in (v_turned, scored, a_turned, multiplied):
                x.credit(pe)

            def wait_turned(st, h):
                prior, wrapped = turned_before[st]
                order = v_made if prior[0] == "prepare" else aT_made
                key = prior[1] if prior[0] == "prepare" else prior[1:]
                common.wait_apart(pe, order.sem, value(order, key, wrapped, h))

            with pe.Fori(0, HEADS) as h:
                for st in steps:
                    if st[0] == "prepare":
                        c = st[1]
                        common.wait_apart(pe, raw_in[c], h * 16 + 16)
                        wait_turned(st, h)
                        ps = turned[turned_slot[st]]
                        w, cols = (META if c == "m" else P), span(c)
                        for j in tiles_of(c):
                            last = nc.tensor.transpose(ps[0:w, j, :], raw[:, v_i, cols.start + j * P:cols.start + j * P + w],
                                                       common.ident[:, :])
                        last.then_inc(v_turned.sem, 1)
                    elif st[0] == "score":
                        _, g, c, i = st
                        for chunk in (g, c):
                            common.wait_apart(pe, low_made.sem, low_made.done(chunk, h))
                        prior, wrapped = z_before[(g, c, i)]
                        common.wait_apart(pe, beta_made.sem, value(beta_made, prior, wrapped, h))
                        nk = META if c == "m" else P * (i + 1) if c == g else 512
                        ks = slice(span(c).start, span(c).start + nk)
                        for t in (range(4) if c == "m" else (i,)):
                            qs = slice(span(g).start + t * P, span(g).start + (t + 1) * P)
                            to = z[0][:, t * META:(t + 1) * META] if c == "m" else z[i][:, 0:nk]
                            nc.tensor.matmul(to, q_high[:, qs], k_high[:, ks], start=True, stop=False)
                            nc.tensor.matmul(to, q_high[:, qs], k_low[:, ks], start=False, stop=False)
                            last = nc.tensor.matmul(to, q_low[:, qs], k_high[:, ks], start=False, stop=True)
                        last.then_inc(scored.sem, 1)
                    elif st[0] == "turn":
                        _, g, c, j = st
                        common.wait_apart(pe, a_made.sem, a_made.done((g, c, last_of(c)), h))
                        wait_turned(st, h)
                        unit, w = unit_no[(g, c)], (META if c == "m" else P)
                        for i in range(j if c == g else 0, 4):
                            last = nc.tensor.transpose(turned[turned_slot[st]][0:w, i, :], a[unit % 3][:, i, j * P:j * P + w],
                                                       common.ident[:, :])
                        last.then_inc(a_turned.sem, 1)
                    elif st[0] == "multiply":
                        _, g, c, j = st
                        key = (g, c, j)
                        common.wait_apart(pe, aT_made.sem, aT_made.done(key, h))
                        common.wait_apart(pe, v_made.sem, v_made.done(c, h))
                        if c == g and j == 0:
                            prior, wrapped = o_before[g]
                            common.wait_apart(pe, finished.sem, value(finished, prior, wrapped, h))
                        i0, w = (j if c == g else 0), (META if c == "m" else P)
                        tile = 0 if c == "m" else 1 + 4 * c + j
                        nc.tensor.matmul(o[g % 2][:, i0 * P:512], v[0:w, tile, :], aT[aT_slot[key]][0:w, i0 * P:512],
                                         start=(c == g and j == 0), stop=(c == "m")).then_inc(multiplied.sem, 1)


def program(nc, x, meta_tokens, pre_norm, post_norm, hgrn_w_in, hgrn_lb, hgrn_out_norm, hgrn_w_out, sb_w_in, sb_w_out, level_masks, out):
    proj = nc.dram_tensor("proj", (4 * HEADS, P, TOK), F32, kind="Internal").ap()
    mixed = nc.dram_tensor("mixed", (HEADS, P, TOK), F32, kind="Internal").ap()
    h1 = nc.dram_tensor("h1", (TOK, D), F32, kind="Internal").ap()
    rstd_rows = nc.dram_tensor("rstd_rows", (HEADS, 1 + TILES, P), F32, kind="Internal").ap()
    rows = x[0]
    with ExitStack() as ctx:
        s = Space(nc, ctx, "all")
        ident = s.sb("ident", [P, P])
        made = s.sem("made")
        with nc.Block() as block:
            @block.gpsimd
            def _(pool):
                nc.gpsimd.memset(ident[:, :], 1.0).then_inc(made, 1)
                pool.wait_ge(made, 1)
                nc.gpsimd.affine_select(out=ident[:, :], in_=ident[:, :], compare_op=ALU.is_equal, fill=0.0,
                                        base=0, pattern=[[-1, P]], channel_multiplier=1).then_inc(made, 1)
                pool.wait_ge(made, 2)

        common = Common(ident, s.sem("apart"))
        with ExitStack() as yctx:
            y = Space(nc, yctx, "y0")
            yT_high, yT_low = (y.sb(n, [P, KT, TOK], F32R) for n in ("high", "low"))
            normalise(nc, "n0", meta_tokens, rows, pre_norm[0], common, yT_high, yT_low)
            project(nc, "p0", hgrn_w_in[0], yT_high, yT_low, proj)
        recurrence(nc, common, "r0", proj, hgrn_lb, hgrn_out_norm[0], level_masks, mixed, rstd_rows)
        contract(nc, common, "c0", mixed, rstd_rows, hgrn_w_out[0], post_norm[0], meta_tokens, rows, h1[0:META, :], h1[META:TOK, :])
        with ExitStack() as yctx:
            y = Space(nc, yctx, "y1")
            yT_high, yT_low = (y.sb(n, [P, KT, TOK], F32R) for n in ("high", "low"))
            normalise(nc, "n1", h1[0:META, :], h1[META:TOK, :], pre_norm[1], common, yT_high, yT_low)
            project(nc, "p1", sb_w_in[0], yT_high, yT_low, proj)
        attention(nc, common, "a1", proj, mixed)
        contract(nc, common, "c1", mixed, None, sb_w_out[0], post_norm[1], None, h1[META:TOK, :], None, out[0])


OUT_SHAPE = (1, SEQ, D)
INPUTS = ("x", "meta_tokens", "pre_norm", "post_norm", "hgrn_w_in", "hgrn_lb", "hgrn_out_norm", "hgrn_w_out",
          "sb_w_in", "sb_w_out")


def small_level_masks():
    s, t = np.arange(P)[:, None, None] % 32, np.arange(32)[None, None, :]
    size = 2 ** np.arange(1, 6)[None, :, None]
    level = (s // size == t // size) & (s % size < size // 2) & (t % size >= size // 2)
    own = np.arange(P)[:, None] // 32 == np.arange(4)[None, :]
    return np.concatenate([np.concatenate([s == t, level], axis=1).reshape(P, 6 * 32), own], axis=1).astype(np.float32)


def kernel(**inputs):
    import concourse.bacc as bacc
    from concourse.bass_utils import run_bass_kernel_spmd

    nc = bacc.Bacc("TRN2", target_bir_lowering=False, num_devices=1)
    arrays, args = {}, []
    for name in INPUTS:
        a = np.ascontiguousarray(inputs[name])
        if name == "hgrn_lb":
            a = np.ascontiguousarray(a.reshape(2, HEADS, P).transpose(2, 0, 1))
        arrays[f"in_{name}"] = a
        args.append(nc.dram_tensor(f"in_{name}", a.shape, F32, kind="ExternalInput").ap())
    arrays["level_masks"] = small_level_masks()
    args.append(nc.dram_tensor("level_masks", (P, 6 * 32 + 4), F32, kind="ExternalInput").ap())
    args.append(nc.dram_tensor("out_h", OUT_SHAPE, F32, kind="ExternalOutput").ap())
    program(nc, *args)
    return run_bass_kernel_spmd(nc, [arrays], core_ids=[0]).results[0]["out_h"]
```

```python
from contextlib import ExitStack

import numpy as np

import concourse.bass as bass
from concourse import mybir

F32 = mybir.dt.float32
F32R = mybir.dt.float32r
ALU = mybir.AluOpType
ACT = mybir.ActivationFunctionType
AX_X = mybir.AxisListType.X

P = 128
D = 1024
KT = D // P
HEADS = D // P
SEQ = 2048
META = 16
TOK = META + SEQ
TILES = SEQ // P
EPS = 1e-6
SB_SCALE = float(P) ** -0.5


class Order:

    def __init__(self, sem, keys):
        self.sem, self.keys = sem, list(keys)

    def credit(self, engine):
        engine.sem_inc(self.sem, len(self.keys))

    def previous(self, key, rnd):
        return rnd * len(self.keys) + (self.keys.index(key) + 1)

    def done(self, key, rnd):
        return self.previous(key, rnd) + len(self.keys)


class AheadOrder:

    def __init__(self, orders):
        self.orders = orders

    def of(self, key):
        return next(order for order in self.orders if key in order.keys)

    def credit(self, engine):
        for order in self.orders:
            order.credit(engine)

    def sem(self, key):
        return self.of(key).sem

    def previous(self, key, rnd):
        return self.of(key).sem, self.of(key).previous(key, rnd)

    def done(self, key, rnd):
        return self.of(key).sem, self.of(key).done(key, rnd)


class Space:

    def __init__(self, nc, ctx, stage):
        self.nc, self.ctx, self.stage = nc, ctx, stage

    def sb(self, name, shape, dt=F32):
        return self.ctx.enter_context(self.nc.sbuf_tensor(f"{self.stage}_{name}", shape, dt))

    def ps(self, name, shape):
        return self.ctx.enter_context(self.nc.psum_tensor(f"{self.stage}_{name}", shape, F32))

    def sem(self, name):
        return self.nc.alloc_semaphore(f"{self.stage}_{name}")

    def order(self, name, keys):
        return Order(self.sem(name), keys)

    def ahead_order(self, name, keys):
        return AheadOrder([self.order(f"{name}{of}", [key for ahead, key in keys if ahead == flag])
                           for flag, of in ((1, "_ahead"), (0, "")) if any(ahead == flag for ahead, key in keys)])


class Common:

    def __init__(self, ident, apart):
        self.ident, self.apart = ident, apart

    def wait_apart(self, engine, sem, value):
        engine.wait_ge(sem, value)
        engine.sem_inc(self.apart, 1)


def row_to_all(row):
    return row.unsqueeze(0).broadcast_to([P, row.shape[0]])


META_BUF = 2


def credit(engine, *sems, by=1):
    for sem in sems:
        engine.sem_inc(sem, by)


def walk(engine, tile):
    tile(META_BUF, META, 0, 0)
    with engine.Fori(0, TILES // 2) as pair:
        for b in range(2):
            tile(b, P, pair * 2 + (1 + b), pair)


def walk_ahead(engine, start, finish):
    last = TILES // 2 - 1
    start(META_BUF, META, 0, 0)
    for b in range(2):
        start(b, P, 1 + b, 0)
    finish(META_BUF, META, 0, 0)
    with engine.Fori(0, last) as pair:
        for b in range(2):
            finish(b, P, pair * 2 + (1 + b), pair)
            start(b, P, pair * 2 + (3 + b), pair + 1)
    for b in range(2):
        finish(b, P, last * 2 + 1 + b, last)


def normalise(nc, stage, rows_meta, rows_seq, gain, common, yT_high, yT_low):
    with ExitStack() as ctx:
        s = Space(nc, ctx, stage)
        gain_all = s.sb("gain", [P, D])
        x = [s.sb(f"x{b}", [P, D]) for b in range(3)]
        y = [s.sb(f"y{b}", [P, D]) for b in range(3)]
        squares = [s.sb(f"squares{b}", [P, D]) for b in range(3)]
        sumsq, rms, rstd = (s.sb(n, [P, 4]) for n in ("sumsq", "rms", "rstd"))
        minus_half = s.sb("minus_half", [P, 1])
        yT = [s.ps(f"yT{b}", [P, KT, P]) for b in range(3)]
        gain_in = s.sem("gain_in")
        x_in = [s.sem(f"x_in{b}") for b in range(3)]
        sumsq_ready, rms_ready, rstd_ready, half_ready = (s.sem(n) for n in ("sumsq", "rms", "rstd", "half"))
        y_ready, yT_ready, high_done, low_done = (s.sem(n) for n in ("y", "yT", "high", "low"))
        block = ctx.enter_context(nc.Block())

        def columns(n, b):
            return slice(0, META) if b == 2 else bass.ds(n * P + (META - P), P)

        @block.sync
        def _(sp):
            sp.dma_start(gain_all[:, :], row_to_all(gain)).then_inc(gain_in, 16)
            sp.dma_start(x[2][0:META, :], rows_meta).then_inc(x_in[2], 16)
            with sp.Fori(0, TILES // 2) as pair:
                for b in range(2):
                    sp.wait_ge(y_ready, pair * 2 + (b + 1))
                    sp.dma_start(x[b][:, :], rows_seq[bass.ds(pair * (2 * P) + b * P, P), :]).then_inc(x_in[b], 16)

        @block.scalar
        def _(act):
            credit(act, sumsq_ready, high_done)

            def start(b, rows, n, pair):
                act.wait_ge(x_in[b], pair * 16 + 16)
                nc.scalar.activation(squares[b][0:rows, :], x[b][0:rows, :], ACT.Square,
                                     accum_out=sumsq[0:rows, b:b + 1]).then_inc(sumsq_ready, 1)

            def finish(b, rows, n, pair):
                common.wait_apart(act, yT_ready, n + 2)
                for half in range(2):
                    ks = slice(half * KT // 2, (half + 1) * KT // 2)
                    nc.scalar.activation(yT_high[:, ks, columns(n, b)], yT[b][:, ks, 0:rows], ACT.Copy).then_inc(high_done, 1)

            walk_ahead(act, start, finish)

        @block.gpsimd
        def _(pool):
            nc.gpsimd.memset(minus_half[:, :], -0.5).then_inc(half_ready, 1)
            pool.wait_ge(half_ready, 1)
            credit(pool, rms_ready, rstd_ready)

            def tile(b, rows, n, pair):
                common.wait_apart(pool, sumsq_ready, n + 2)
                nc.gpsimd.tensor_scalar(rms[0:rows, b:b + 1], sumsq[0:rows, b:b + 1], 1.0 / D, EPS,
                                        ALU.mult, ALU.add).then_inc(rms_ready, 1)
                pool.wait_ge(rms_ready, n + 2)
                nc.gpsimd.tensor_tensor(rstd[0:rows, b:b + 1], rms[0:rows, b:b + 1], minus_half[0:rows, :],
                                        ALU.pow).then_inc(rstd_ready, 1)

            walk(pool, tile)

        @block.vector
        def _(dve):
            dve.wait_ge(gain_in, 16)
            credit(dve, y_ready, low_done)

            def start(b, rows, n, pair):
                dve.wait_ge(rstd_ready, n + 2)
                nc.vector.scalar_tensor_tensor(y[b][0:rows, :], x[b][0:rows, :], rstd[0:rows, b:b + 1],
                                               gain_all[0:rows, :], ALU.mult, ALU.mult).then_inc(y_ready, 1)

            def finish(b, rows, n, pair):
                for half in range(2):
                    dve.wait_ge(high_done, n * 2 + (half + 2))
                    ks = slice(half * KT // 2, (half + 1) * KT // 2)
                    nc.vector.tensor_tensor(yT_low[:, ks, columns(n, b)], yT[b][:, ks, 0:rows],
                                            yT_high[:, ks, columns(n, b)].bitcast(F32), ALU.subtract).then_inc(low_done, 1)

            walk_ahead(dve, start, finish)

        @block.tensor
        def _(pe):
            credit(pe, yT_ready)

            def tile(b, rows, n, pair):
                pe.wait_ge(y_ready, n + 2)
                if b != META_BUF:
                    pe.wait_ge(low_done, pair * 4 + (2 * b + 1))
                for k in range(KT):
                    last = nc.tensor.transpose(yT[b][:, k, 0:rows], y[b][0:rows, k * P:(k + 1) * P], common.ident[0:rows, 0:rows])
                last.then_inc(yT_ready, 1)

            walk(pe, tile)


def project(nc, stage, w_in, yT_high, yT_low, proj):
    widths = [416, 416, 416, 416, 400]
    starts = [sum(widths[:g]) for g in range(len(widths))]
    assert sum(widths) == TOK
    G = len(widths)
    CT = 4 * HEADS
    with ExitStack() as ctx:
        s = Space(nc, ctx, stage)
        w = [s.sb(f"w{b}", [P, KT, P]) for b in range(2)]
        w_high = [s.sb(f"wh{b}", [P, KT, P], F32R) for b in range(2)]
        w_low = [s.sb(f"wl{b}", [P, KT, P], F32R) for b in range(2)]
        out_rows = [s.sb(f"out{b}", [P, TOK]) for b in range(2)]
        acc = [s.ps(f"acc{g}", [P, 512]) for g in range(G)]
        w_loaded = [s.sem(f"w_loaded{b}") for b in range(2)]
        stored = [s.sem(f"stored{b}") for b in range(2)]
        high_ready, low_ready = s.sem("high"), s.sem("low")
        products = s.order("products", [(b, g) for b in range(2) for g in range(G)])
        copied = s.order("copied", [(b, g) for b in range(2) for g in range(G)])
        w_cols = w_in.rearrange("(k p) n -> p k n", p=P)
        block = ctx.enter_context(nc.Block())

        @block.sync
        def _(sp):
            credit(sp, *stored, by=16)

            def load(b, pair):
                sp.dma_start(w[b][:, :, :], w_cols[:, :, bass.ds(pair * (2 * P) + b * P, P)]).then_inc(w_loaded[b], 16)

            def store(b, pair):
                sp.wait_ge(copied.sem, copied.done((b, G - 1), pair))
                sp.dma_start(proj[bass.ds(pair * 2 + b, 1), :, :].rearrange("c p t -> (c p) t"),
                             out_rows[b][:, :]).then_inc(stored[b], 16)

            for b in range(2):
                load(b, 0)
            with sp.Fori(0, CT // 2 - 1) as pair:
                for b in range(2):
                    sp.wait_ge(low_ready, pair * 2 + (b + 2))
                    load(b, pair + 1)
                    store(b, pair)
            for b in range(2):
                store(b, CT // 2 - 1)
            for b in range(2):
                sp.wait_ge(stored[b], 16 * (CT // 2) + 16)

        @block.scalar
        def _(act):
            copied.credit(act)

            def split(b, pair):
                act.wait_ge(w_loaded[b], pair * 16 + 16)
                nc.scalar.activation(w_high[b][:, :, :], w[b][:, :, :], ACT.Copy).then_inc(high_ready, 1)

            def read_out(b, pair):
                act.wait_ge(stored[b], pair * 16 + 16)
                for g in range(G):
                    act.wait_ge(products.sem, products.done((b, g), pair))
                    nc.scalar.activation(out_rows[b][:, starts[g]:starts[g] + widths[g]], acc[g][:, 0:widths[g]],
                                         ACT.Copy).then_inc(copied.sem, 1)

            for b in range(2):
                split(b, 0)
            with act.Fori(0, CT // 2 - 1) as pair:
                for b in range(2):
                    read_out(b, pair)
                    split(b, pair + 1)
            for b in range(2):
                read_out(b, CT // 2 - 1)

        @block.vector
        def _(dve):
            credit(dve, low_ready)
            with dve.Fori(0, CT // 2) as pair:
                for b in range(2):
                    dve.wait_ge(high_ready, pair * 2 + (b + 1))
                    dve.wait_ge(products.sem, products.previous((b, G - 1), pair))
                    nc.vector.tensor_tensor(w_low[b][:, :, :], w[b][:, :, :], w_high[b][:, :, :].bitcast(F32),
                                            ALU.subtract).then_inc(low_ready, 1)

        @block.tensor
        def _(pe):
            products.credit(pe)
            with pe.Fori(0, CT // 2) as pair:
                for b in range(2):
                    pe.wait_ge(low_ready, pair * 2 + (b + 2))
                    for g in range(G):
                        if b == 0:
                            pe.wait_ge(copied.sem, copied.previous((1, g), pair))
                        else:
                            pe.wait_ge(copied.sem, copied.done((0, g), pair))
                        t = slice(starts[g], starts[g] + widths[g])
                        for k in range(KT):
                            for n, (wp, yp) in enumerate(((w_high, yT_high), (w_high, yT_low), (w_low, yT_high))):
                                last = nc.tensor.matmul(acc[g][:, 0:widths[g]], wp[b][:, k, :], yp[:, k, t],
                                                        start=(k == 0 and n == 0), stop=(k == KT - 1 and n == 2))
                        last.then_inc(products.sem, 1)


def contract(nc, common, stage, mixed, rstd_rows, w_out, gain, res_meta, res_seq, out_meta, out_seq):
    with ExitStack() as ctx:
        s = Space(nc, ctx, stage)
        HALF = D // 2
        wo_high, wo_low = (s.sb(n, [P, KT, D], F32R) for n in ("wo_high", "wo_low"))
        wo = [s.sb(f"wo{b}", [P, D]) for b in range(2)]
        gain_all = s.sb("gain", [P, D])
        minus_half = s.sb("minus_half", [P, 1])
        m = [s.sb(f"m{b}", [P, KT, P]) for b in range(3)]
        r = [s.sb(f"r{b}", [P, KT, P]) for b in range(3)] if rstd_rows is not None else None
        m_high = [s.sb(f"mh{b}", [P, KT, P], F32R) for b in range(3)]
        m_low = [s.sb(f"ml{b}", [P, KT, P], F32R) for b in range(3)]
        res = [s.sb(f"res{b}", [P, D]) for b in range(3)]
        normed = [s.sb(f"normed{b}", [P, D]) for b in range(3)]
        squares = [s.sb(f"squares{b}", [P, D]) for b in range(3)]
        sumsq, rms, rstd = (s.sb(n, [P, 4]) for n in ("sumsq", "rms", "rstd"))
        acc = [s.ps(f"acc{b}", [P, 2, HALF]) for b in range(3)]
        wo_in = [s.sem(f"wo_in{b}") for b in range(2)]
        m_in = [s.sem(f"m_in{b}") for b in range(3)]
        res_in = [s.sem(f"res_in{b}") for b in range(3)]
        stored = [s.sem(f"stored{b}") for b in range(3)]
        names = ("scaled", "wo_high", "wo_low", "gain_in", "m_high", "m_low", "product", "sumsq", "rms", "rstd", "half",
                 "normed", "summed")
        (scaled_ready, wo_high_ready, wo_low_ready, gain_in, high_ready, low_ready, product, sumsq_ready, rms_ready, rstd_ready,
         half_ready, normed_ready, summed) = (s.sem(n) for n in names)
        block = ctx.enter_context(nc.Block())
        with_meta = out_meta is not None

        def steps(engine, raised, start, finish):
            last = TILES // 2 - 1
            credit(engine, *raised, by=1 if with_meta else 2)
            if with_meta:
                start(META_BUF, META, 0, 0)
            for b in range(2):
                start(b, P, 1 + b, 0)
            if with_meta:
                finish(META_BUF, META, 0, 0)
            with engine.Fori(0, last) as pair:
                for b in range(2):
                    finish(b, P, pair * 2 + (1 + b), pair)
                    start(b, P, pair * 2 + (3 + b), pair + 1)
            for b in range(2):
                finish(b, P, last * 2 + 1 + b, last)

        def nothing(b, rows, n, pair):
            pass

        @block.sync
        def _(sp):
            sp.dma_start(gain_all[:, :], row_to_all(gain)).then_inc(gain_in, 16)
            for k in range(KT):
                if k >= 2:
                    sp.wait_ge(wo_low_ready, k - 1)
                sp.dma_start(wo[k % 2][:, :], w_out[k * P:(k + 1) * P, :]).then_inc(wo_in[k % 2], 16)
            def load(b, n, rows, cols):
                sp.dma_start(m[b][:, :, 0:rows], mixed[:, :, cols].rearrange("k p t -> p k t")).then_inc(m_in[b], 16)
                if r is not None:
                    tile = rstd_rows[:, n:n + 1, 0:rows] if b == META_BUF else rstd_rows[:, bass.ds(n, 1), 0:rows]
                    sp.dma_start(r[b][:, :, 0:rows], tile.rearrange("k n t -> n k t").broadcast_to([P, KT, rows])
                                 ).then_inc(m_in[b], 16)

            def load_residual(b, rows, pair):
                rows_in = res_meta if b == META_BUF else res_seq[bass.ds(pair * (2 * P) + b * P, P), :]
                sp.dma_start(res[b][0:rows, :], rows_in).then_inc(res_in[b], 16)

            def load_tile(b, pair):
                load(b, pair * 2 + (1 + b), P, bass.ds(pair * (2 * P) + (META + b * P), P))

            def store(b, rows, n, pair):
                sp.wait_ge(summed, n + 2)
                to = out_meta if b == META_BUF else out_seq[bass.ds(pair * (2 * P) + b * P, P), :]
                sp.dma_start(to, res[b][0:rows, :]).then_inc(stored[b], 16)

            credit(sp, *stored, by=16)
            last = TILES // 2 - 1
            if with_meta:
                load(META_BUF, 0, META, slice(0, META))
                load_residual(META_BUF, META, 0)
            for b in range(2):
                load_tile(b, 0)
                load_residual(b, P, 0)
            if with_meta:
                store(META_BUF, META, 0, 0)
            with sp.Fori(0, last) as pair:
                for b in range(2):
                    n = pair * 2 + (1 + b)
                    sp.wait_ge(low_ready, n + 2)
                    load_tile(b, pair + 1)
                    store(b, P, n, pair)
                    sp.wait_ge(stored[b], pair * 16 + 32)
                    load_residual(b, P, pair + 1)
            for b in range(2):
                store(b, P, last * 2 + 1 + b, last)
            for b in range(2 + with_meta):
                sp.wait_ge(stored[b], 32 if b == META_BUF else 16 * (TILES // 2) + 16)

        @block.scalar
        def _(act):
            for k in range(KT):
                act.wait_ge(wo_in[k % 2], 16 * (k // 2 + 1))
                nc.scalar.activation(wo_high[:, k, :], wo[k % 2][:, :], ACT.Copy).then_inc(wo_high_ready, 1)

            def start(b, rows, n, pair):
                if r is None:
                    act.wait_ge(m_in[b], pair * 16 + 16)
                else:
                    act.wait_ge(scaled_ready, n + 2)
                nc.scalar.activation(m_high[b][:, :, 0:rows], m[b][:, :, 0:rows], ACT.Copy).then_inc(high_ready, 1)

            def finish(b, rows, n, pair):
                act.wait_ge(product, n + 2)
                nc.scalar.activation(squares[b][0:rows, :], acc[b][0:rows, :, :].rearrange("p h n -> p (h n)"), ACT.Square,
                                     accum_out=sumsq[0:rows, b:b + 1]).then_inc(sumsq_ready, 1)

            steps(act, (high_ready, sumsq_ready), start, finish)

        @block.gpsimd
        def _(pool):
            nc.gpsimd.memset(minus_half[:, :], -0.5).then_inc(half_ready, 1)
            pool.wait_ge(half_ready, 1)

            def tile(b, rows, n, pair):
                common.wait_apart(pool, sumsq_ready, n + 2)
                nc.gpsimd.tensor_scalar(rms[0:rows, b:b + 1], sumsq[0:rows, b:b + 1], 1.0 / D, EPS,
                                        ALU.mult, ALU.add).then_inc(rms_ready, 1)
                pool.wait_ge(rms_ready, n + 2)
                nc.gpsimd.tensor_tensor(rstd[0:rows, b:b + 1], rms[0:rows, b:b + 1], minus_half[0:rows, :],
                                        ALU.pow).then_inc(rstd_ready, 1)
                pool.wait_ge(res_in[b], pair * 16 + 16)
                pool.wait_ge(normed_ready, n + 2)
                nc.gpsimd.tensor_tensor(res[b][0:rows, :], normed[b][0:rows, :], res[b][0:rows, :],
                                        ALU.add).then_inc(summed, 1)

            steps(pool, (rms_ready, rstd_ready, summed), nothing, tile)

        @block.vector
        def _(dve):
            for k in range(KT):
                dve.wait_ge(wo_high_ready, k + 1)
                nc.vector.tensor_tensor(wo_low[:, k, :], wo[k % 2][:, :], wo_high[:, k, :].bitcast(F32),
                                        ALU.subtract).then_inc(wo_low_ready, 1)
            dve.wait_ge(gain_in, 16)

            def start(b, rows, n, pair):
                if r is not None:
                    dve.wait_ge(m_in[b], pair * 32 + 32)
                    nc.vector.tensor_tensor(m[b][:, :, 0:rows], m[b][:, :, 0:rows], r[b][:, :, 0:rows], ALU.mult
                                            ).then_inc(scaled_ready, 1)
                dve.wait_ge(high_ready, n + 2)
                if b != META_BUF:
                    dve.wait_ge(product, pair * 2 + (b + 1))
                nc.vector.tensor_tensor(m_low[b][:, :, 0:rows], m[b][:, :, 0:rows], m_high[b][:, :, 0:rows].bitcast(F32),
                                        ALU.subtract).then_inc(low_ready, 1)

            def finish(b, rows, n, pair):
                dve.wait_ge(rstd_ready, n + 2)
                if b != META_BUF:
                    dve.wait_ge(summed, pair * 2 + (b + 1))
                nc.vector.scalar_tensor_tensor(normed[b][0:rows, :], acc[b][0:rows, :, :].rearrange("p h n -> p (h n)"),
                                               rstd[0:rows, b:b + 1], gain_all[0:rows, :],
                                               ALU.mult, ALU.mult).then_inc(normed_ready, 1)

            steps(dve, (low_ready, normed_ready, scaled_ready), start, finish)

        @block.tensor
        def _(pe):
            pe.wait_ge(wo_low_ready, KT)

            def tile(b, rows, n, pair):
                pe.wait_ge(low_ready, n + 2)
                if b != META_BUF:
                    pe.wait_ge(normed_ready, pair * 2 + (b + 1))
                for k in range(KT):
                    for mp, wps in ((m_high, (wo_high, wo_low)), (m_low, (wo_high,))):
                        for half in range(2):
                            cols = slice(half * HALF, (half + 1) * HALF)
                            for wp in wps:
                                last = nc.tensor.matmul(acc[b][0:rows, half, :], mp[b][:, k, 0:rows], wp[:, k, cols],
                                                        start=(k == 0 and mp is m_high and wp is wo_high),
                                                        stop=(k == KT - 1 and mp is m_low))
                last.then_inc(product, 1)

            steps(pe, (product,), nothing, tile)


UNITS = ("m", 0, 1, 2, 3)
GROUP = 4 * P
SMALL = (1, 2, 4, 8, 16)
SLOT = {0: 0, 1: 1, 2: 0, 3: 1}


def width(u):
    return META if u == "m" else P


def tokens(u):
    return META if u == "m" else GROUP


def added_blocks(u):
    return 1 if u == "m" else 3 if u == 3 else 4


def halves(u):
    return [h for h in (1, 2, 4, 8, 16, 32, 64) if h < width(u)]


def recurrence_steps():
    def own(*steps):
        return [(0,) + step for step in steps]

    def ahead(*steps):
        return [(1,) + step for step in steps]

    def level(us, h):
        return [("level", u, h) for u in us]

    late, early = (2, 3), (0, 1)
    return (ahead(("load", "m"), ("load", 0), ("load", 1)) + own(*level(late, 1), ("turn_k", 0))
            + own(*level(late, 2), ("carry", 0), ("turn_k", 1)) + ahead(("bound", "lb"), ("gates", "m"))
            + own(*level(late, 4), ("out", 0), ("carry", 1)) + ahead(("gates", 0))
            + own(*level(late, 8), ("norm", 0), ("out", 1)) + ahead(("product", "m"), ("turn_v", "m"))
            + own(*level(late, 16), ("norm", 1)) + ahead(("gates", 1)) + own(("mask", 2), ("mask", 3))
            + ahead(("product", 0)) + own(("sum", 2), ("sum", 3)) + ahead(("turn_v", 0))
            + own(*level(late, 32)) + ahead(("product", 1), ("turn_v", 1))
            + own(*level(late, 64), ("spread", 2), ("spread", 3)) + ahead(("load", 2), ("load", 3))
            + ahead(*level(early, 1)) + own(("turn_k", 2)) + ahead(("level", "m", 1))
            + ahead(*level(early, 2)) + own(("carry", 2), ("turn_k", 3)) + ahead(("level", "m", 2))
            + ahead(*level(early, 4)) + own(("out", 2), ("carry", 3)) + ahead(("gates", 2), ("level", "m", 4))
            + ahead(*level(early, 8)) + own(("norm", 2), ("out", 3)) + ahead(("level", "m", 8), ("gates", 3))
            + ahead(*level(early, 16)) + own(("norm", 3)) + ahead(("mask", 0), ("mask", 1), ("product", 2), ("mask", "m"))
            + ahead(("sum", 0), ("sum", 1), ("sum", "m"), ("turn_k", "m"))
            + ahead(*level(early, 32)) + own(("rms", "all")) + ahead(("product", 3), ("turn_v", 2), ("carry", "m"))
            + ahead(*level(early, 64), ("spread", 0), ("spread", 1), ("out", "m"), ("turn_v", 3), ("norm", "m")))


def recurrence(nc, common, stage, proj, lb_logits, out_norm, level_masks, mixed, rstd_rows):
    steps = recurrence_steps()

    first_steps = [step[1:] for step in steps if step[0]]
    last_steps = [step[1:] for step in steps if not step[0]]

    def keys(name):
        return [(step[0], step[2:] if len(step) > 3 else step[2]) for step in steps if step[1] == name]

    with ExitStack() as ctx:
        s = Space(nc, ctx, stage)
        q_i, f_i, v_i, g_i = range(4)

        def each(name, shape, dt=F32):
            return {u: s.sb(f"{name}_{u}", shape(u), dt) for u in UNITS}

        raw = each("raw", lambda u: [P, 4, tokens(u)])
        sig = each("sig", lambda u: [P, 2, tokens(u)])
        decay = each("decay", lambda u: [P, tokens(u)])
        gate_sig = each("gate_sig", lambda u: [P, tokens(u)])
        gate = each("gate", lambda u: [P, tokens(u)])
        dq = each("dq", lambda u: [P, tokens(u)])
        dk = each("dk", lambda u: [P, tokens(u)])
        totals = each("totals", lambda u: [P, GROUP])
        v = each("v", lambda u: [P, tokens(u) // width(u), P])
        kT = each("kT", lambda u: [P, tokens(u) // width(u), P])
        state = {u: s.sb(f"state_{u}", [P, 4, P]) for u in (0, 1, 2, 3)}
        scores = each("scores", lambda u: [P, 4, P])
        masked = {i: s.sb(f"masked{i}", [P, 6, 4, 32]) for i in (0, 1)}
        masked["m"] = s.sb("masked_m", [META, 5, 1, META])
        diag = each("diag", lambda u: [P, 4, 32])
        squares = each("squares", lambda u: [P, tokens(u)])
        ms = s.sb("ms", [P, 1 + TILES])
        rstd = s.sb("rstd", [P, 1 + TILES])
        rstd_turned = s.sb("rstd_turned", [1 + TILES, P])
        result = each("result", lambda u: [P, tokens(u)])
        mask_rows = s.sb("masks", [P, 6 * 32 + 4])
        masks = mask_rows[:, 0:6 * 32].rearrange("p (l t) -> p l t", t=32)
        own_32 = mask_rows[:, 6 * 32:6 * 32 + 4]
        mean_of = s.sb("mean_of", [P, 1])
        minus_half = s.sb("minus_half", [P, 1 + TILES])
        out_gain = s.sb("out_gain", [P, 1])
        logits = s.sb("logits", [P, 2, HEADS])
        lb_work = s.sb("lb_work", [P, 6, HEADS])
        lb, one_less_lb = s.sb("lb", [P, HEADS]), s.sb("one_less_lb", [P, HEADS])
        lb_now = s.sb("lb_now", [P, 2])

        small = [s.ps(f"small{i}", [P, 8, 4, 32]) for i in range(2)]
        turned_v, turned_k = s.ps("turned_v", [P, 4, P]), s.ps("turned_k", [P, 4, P])
        meta_small = turned_v[:, 0, 0:5 * META].rearrange("p (l b t) -> p l b t", b=1, t=META)
        added = s.ps("added", [P, GROUP])
        o = s.ps("o", [P, GROUP])

        raw_in = {u: s.sem(f"raw_in_{u}") for u in UNITS}
        left = {u: s.sem(f"left_{u}") for u in UNITS}
        consts_in, set_up, exps_made, lb_steps = (s.sem(n) for n in ("consts_in", "set_up", "exps_made", "lb_steps"))
        sig_made = s.ahead_order("sig_made", keys("gates"))
        gates_made = s.ahead_order("gates_made", keys("gates"))
        silu_made = s.ahead_order("silu_made", keys("product"))
        q_at = s.ahead_order("q_at", [(st[0], (st[2], 1) if st[1] == "product" else (st[2], 2 * st[3]))
                                      for st in steps if st[1] in ("product", "level")])
        total_at = s.ahead_order("total_at", [(ahead, (u, 2 * h)) for ahead, (u, h) in keys("level")])
        k_at = s.ahead_order("k_at", [(ahead, (u, 2 * h)) for ahead, (u, h) in keys("level")])
        scored = s.ahead_order("scored", keys("level"))
        masked_at = s.ahead_order("masked_at", keys("mask"))
        summed = s.ahead_order("summed", keys("sum"))
        placed = s.ahead_order("placed", [(ahead, u) for ahead, u in keys("sum") if u != "m"])
        spread = s.ahead_order("spread", keys("spread"))
        v_turned, k_turned = s.ahead_order("v_turned", keys("turn_v")), s.ahead_order("k_turned", keys("turn_k"))
        v_made, k_made = s.ahead_order("v_made", keys("turn_v")), s.ahead_order("k_made", keys("turn_k"))
        k_added = s.ahead_order("k_added", keys("carry"))
        states = s.ahead_order("states", [(ahead, (u, n)) for ahead, u in keys("carry") for n in range(added_blocks(u))])
        read, meaned = s.ahead_order("read", keys("out")), s.ahead_order("meaned", keys("norm"))
        squared = s.ahead_order("squared", keys("out"))
        ms_made = s.ahead_order("ms_made", keys("norm"))
        mixed_at = s.ahead_order("mixed_at", keys("out"))
        rstd_made = s.ahead_order("rstd_made", keys("rms"))
        rstd_on_psum = s.ahead_order("rstd_on_psum", keys("rms"))
        rstd_copied = s.ahead_order("rstd_copied", keys("rms"))
        rstd_left = s.sem("rstd_left")
        head_lb = s.ahead_order("head_lb", keys("bound"))

        users = [st for st in first_steps + last_steps if st[0] in ("carry", "norm", "rms")]
        added_users = {}
        for at, st in enumerate(users):
            name, u = users[at - 1]
            order, key = {"carry": (states, (u, added_blocks(u) - 1)), "norm": (ms_made, u),
                          "rms": (rstd_copied, "all")}[name]
            added_users[st] = [lambda h, order=order, key=key, at=at:
                               (order.done if at else order.previous)(key, h)]

        proj_h = proj.rearrange("(a h) p t -> h p a t", a=4)

        def span(u):
            return slice(0, META) if u == "m" else slice(META + u * GROUP, META + (u + 1) * GROUP)

        def blocks(u):
            w = width(u)
            return [(i, slice(i * w, (i + 1) * w)) for i in range(tokens(u) // w)]

        def by_halves(tile, u, h):
            return tile[u][:, 0:tokens(u)].rearrange("p (m two h) -> p m two h", two=2, h=h)

        def total(u, h):
            n = tokens(u) // h
            t = decay[u][:, 0:n] if h == 1 else totals[u][:, GROUP - 2 * GROUP // h:GROUP - 2 * GROUP // h + n]
            return t.rearrange("p (m two) -> p m two", two=2) if n > 1 and h < width(u) else t

        with nc.Block() as prologue:
            @prologue.sync
            def _(sp):
                sp.dma_start(mask_rows[:, :], level_masks).then_inc(consts_in, 16)
                sp.dma_start(out_gain[:, :], out_norm.unsqueeze(1)).then_inc(consts_in, 16)
                sp.dma_start(logits[:, :, :], lb_logits).then_inc(consts_in, 16)
                sp.wait_ge(consts_in, 48)

            @prologue.gpsimd
            def _(pool):
                nc.gpsimd.memset(minus_half[:, :], -0.5).then_inc(set_up, 1)
                nc.gpsimd.memset(mean_of[:, :], 1.0 / P).then_inc(set_up, 1)
                nc.gpsimd.memset(ms[:, :], 1.0).then_inc(set_up, 1)
                pool.wait_ge(set_up, 3)

            @prologue.vector
            def _(dve):
                made = 0

                def chained(op):
                    nonlocal made
                    made += 1
                    op.then_inc(lb_steps, 1)
                    dve.wait_ge(lb_steps, made)

                w = lb_work
                dve.wait_ge(consts_in, 48)
                chained(nc.vector.tensor_tensor(w[:, 0, :], logits[:, 0, :], logits[:, 1, :], ALU.max))
                chained(nc.vector.tensor_tensor(w[:, 1, :], logits[:, 0, :], w[:, 0, :], ALU.subtract))
                chained(nc.vector.tensor_tensor(w[:, 2, :], logits[:, 1, :], w[:, 0, :], ALU.subtract))
                dve.wait_ge(exps_made, 1)
                chained(nc.vector.tensor_tensor(w[:, 5, :], w[:, 3, :], w[:, 4, :], ALU.add))
                chained(nc.vector.reciprocal(w[:, 0, :], w[:, 5, :]))
                chained(nc.vector.tensor_tensor(lb[:, :], w[:, 3, :], w[:, 0, :], ALU.mult))
                chained(nc.vector.tensor_scalar(one_less_lb[:, :], lb[:, :], -1.0, 1.0, ALU.mult, ALU.add))

            @prologue.scalar
            def _(act):
                act.wait_ge(lb_steps, 3)
                nc.scalar.activation(lb_work[:, 3:5, :], lb_work[:, 1:3, :], ACT.Exp).then_inc(exps_made, 1)

        block = ctx.enter_context(nc.Block())

        @block.sync
        def _(sp):
            def store_rstd(h):
                common.wait_apart(sp, *rstd_copied.done("all", h))
                sp.dma_start(rstd_rows[bass.ds(h, 1), :, :].rearrange("h n t -> (h n) t"), rstd_turned[:, :]
                             ).then_inc(rstd_left, 16)

            def load(u, h):
                sp.dma_start(raw[u][:, :, :], proj_h[bass.ds(h, 1), :, :, span(u)].rearrange("h p a t -> (h p) a t")
                             ).then_inc(raw_in[u], 16)

            def store(u, h):
                common.wait_apart(sp, *mixed_at.done(u, h))
                sp.dma_start(mixed[bass.ds(h, 1), :, span(u)].rearrange("h p t -> (h p) t"), result[u][:, :]).then_inc(left[u], 16)

            def step(st, h):
                name, u = st[0:2]
                if name == "load":
                    common.wait_apart(sp, *scored.previous((u, 1), h))
                    common.wait_apart(sp, *v_turned.previous(u, h))
                    common.wait_apart(sp, *silu_made.previous(u, h))
                    load(u, h)
                elif name == "out":
                    store(u, h)
                elif name == "rms":
                    store_rstd(h)

            for st in first_steps:
                step(st, 0)
            with sp.Fori(0, HEADS - 1) as h:
                for ahead, *st in steps:
                    step(st, h + 1 if ahead else h)
            for st in last_steps:
                step(st, HEADS - 1)
            sp.wait_ge(rstd_left, 16 * HEADS + 16)
            for u in UNITS:
                sp.wait_ge(left[u], 16 * HEADS + 16)

        @block.scalar
        def _(act):
            for x in (sig_made, gates_made, spread, v_made, k_made, squared):
                x.credit(act)
            def step(st, h):
                name, u = st[0:2]
                if name == "gates":
                    act.wait_ge(*head_lb.done("lb", h))
                    act.wait_ge(raw_in[u], h * 16 + 16)
                    act.wait_ge(*silu_made.previous(u, h))
                    act.wait_ge(*total_at.previous((u, 2 * halves(u)[-1]), h))
                    act.wait_ge(*k_at.previous((u, 2 * halves(u)[-1]), h))
                    act.wait_ge(*k_turned.previous(u, h))
                    nc.scalar.activation(sig[u][:, 0, :], raw[u][:, f_i, :], ACT.Sigmoid)
                    nc.scalar.activation(sig[u][:, 1, :], raw[u][:, f_i, :], ACT.Sigmoid, scale=-1.0).then_inc(sig_made.sem(u), 1)
                    nc.scalar.activation(gate_sig[u][:, :], raw[u][:, g_i, :], ACT.Sigmoid)
                    act.wait_ge(*sig_made.done(u, h))
                    nc.scalar.activation(decay[u][:, :], sig[u][:, 0, :], ACT.Identity, bias=lb_now[:, 0:1],
                                         scale=lb_now[:, 1:2])
                    nc.scalar.activation(dk[u][:, :], sig[u][:, 1, :], ACT.Copy, scale=lb_now[:, 1:2]
                                         ).then_inc(gates_made.sem(u), 1)
                elif name == "turn_v":
                    act.wait_ge(*v_turned.done(u, h))
                    act.wait_ge(*read.previous(u, h))
                    act.wait_ge(*k_added.previous(u, h))
                    w, n = width(u), tokens(u) // width(u)
                    nc.scalar.activation(v[u][0:w, :, :], turned_v[0:w, 0:n, :], ACT.Copy).then_inc(v_made.sem(u), 1)
                elif name == "turn_k":
                    act.wait_ge(*k_turned.done(u, h))
                    act.wait_ge(*k_added.previous(u, h))
                    w, n = width(u), tokens(u) // width(u)
                    nc.scalar.activation(kT[u][0:w, :, :], turned_k[0:w, 0:n, :], ACT.Copy).then_inc(k_made.sem(u), 1)
                elif name == "spread":
                    act.wait_ge(*scored.done((u, 64), h))
                    act.wait_ge(*placed.done(u, h))
                    ps = small[SLOT[u]]
                    for p0 in (0, 64):
                        nc.scalar.activation(scores[u][p0:p0 + 32, :, p0 + 32:p0 + 64], ps[p0:p0 + 32, 6, :, :], ACT.Copy)
                    nc.scalar.activation(scores[u][0:64, :, 64:128],
                                         ps[0:64, 0:2, :, :].rearrange("p a b t -> p (a b t)").rearrange("p (b t) -> p b t", t=64),
                                         ACT.Copy).then_inc(spread.sem(u), 1)
                elif name == "out":
                    act.wait_ge(*read.done(u, h))
                    nc.scalar.activation(squares[u][:, :], o[:, 0:tokens(u)], ACT.Square).then_inc(squared.sem(u), 1)

            for st in first_steps:
                step(st, 0)
            with act.Fori(0, HEADS - 1) as h:
                for ahead, *st in steps:
                    step(st, h + 1 if ahead else h)
            for st in last_steps:
                step(st, HEADS - 1)

        @block.gpsimd
        def _(pool):
            for x in (silu_made, k_at, placed, rstd_made):
                x.credit(pool)
            def step(st, h):
                name, u = st[0:2]
                if name == "product":
                    pool.wait_ge(*gates_made.done(u, h))
                    pool.wait_ge(*mixed_at.previous(u, h))
                    nc.gpsimd.tensor_tensor(gate[u][:, :], raw[u][:, g_i, :], gate_sig[u][:, :], ALU.mult
                                            ).then_inc(silu_made.sem(u), 1)
                elif name == "level":
                    half = st[2]
                    pool.wait_ge(*scored.done((u, half), h))
                    if half > 1:
                        pool.wait_ge(*total_at.done((u, half), h))
                        pool.wait_ge(*k_at.done((u, half), h))
                    left_half = by_halves(dk, u, half)[:, :, 0, :]
                    right_total = total(u, half)[:, :, 1:2].broadcast_to(list(left_half.shape))
                    nc.gpsimd.tensor_tensor(left_half, left_half, right_total, ALU.mult).then_inc(k_at.sem((u, 2 * half)), 1)
                elif name == "sum" and u != "m":
                    pool.wait_ge(*summed.done(u, h))
                    pool.wait_ge(*read.previous(u, h))
                    nc.gpsimd.tensor_tensor(scores[u][:, :, :].rearrange("p b (i t) -> p b i t", t=32),
                                            diag[u][:, :, :].unsqueeze(2).broadcast_to([P, 4, 4, 32]),
                                            own_32[:, :].unsqueeze(1).unsqueeze(3).broadcast_to([P, 4, 4, 32]),
                                            ALU.mult).then_inc(placed.sem(u), 1)
                elif name == "rms":
                    pool.wait_ge(*ms_made.done(3, h))
                    pool.wait_ge(*rstd_on_psum.previous("all", h))
                    nc.gpsimd.tensor_tensor(rstd[:, :], ms[:, :], minus_half[:, :], ALU.pow).then_inc(rstd_made.sem("all"), 1)

            for st in first_steps:
                step(st, 0)
            with pool.Fori(0, HEADS - 1) as h:
                for ahead, *st in steps:
                    step(st, h + 1 if ahead else h)
            for st in last_steps:
                step(st, HEADS - 1)

        @block.vector
        def _(dve):
            for x in (q_at, total_at, masked_at, summed, states, ms_made, mixed_at, rstd_copied, head_lb):
                x.credit(dve)
            for sem in (*left.values(), rstd_left):
                dve.sem_inc(sem, 16)

            def step(st, h):
                name, u = st[0:2]
                n = 0 if u in ("all", "lb") else tokens(u)
                if name == "bound":
                    dve.wait_ge(*gates_made.previous(3, h))
                    nc.vector.tensor_copy(lb_now[:, 0:1], lb[:, bass.ds(h, 1)])
                    nc.vector.tensor_copy(lb_now[:, 1:2], one_less_lb[:, bass.ds(h, 1)]).then_inc(head_lb.sem("lb"), 1)
                elif name == "product":
                    dve.wait_ge(*gates_made.done(u, h))
                    dve.wait_ge(*read.previous(u, h))
                    nc.vector.tensor_tensor(dq[u][:, :], raw[u][:, q_i, :], decay[u][:, :], ALU.mult
                                        ).then_inc(q_at.sem((u, 1)), 1)
                elif name == "level":
                    half = st[2]
                    pairs = total(u, half)
                    if half > 1:
                        dve.wait_ge(*total_at.done((u, half), h))
                    dve.wait_ge(*k_at.previous((u, halves(u)[-1] * 2), h))
                    wide = total(u, 2 * half)
                    out = wide if len(wide.shape) == 2 else wide.rearrange("p m two -> p (m two)")
                    nc.vector.tensor_tensor(out.unsqueeze(2), pairs[:, :, 0:1], pairs[:, :, 1:2], ALU.mult
                                            ).then_inc(total_at.sem((u, 2 * half)), 1)
                    dve.wait_ge(*scored.done((u, half), h))
                    dve.wait_ge(*q_at.done((u, half), h))
                    right_half = by_halves(dq, u, half)[:, :, 1, :]
                    nc.vector.tensor_tensor(right_half, right_half, pairs[:, :, 0:1].broadcast_to(list(right_half.shape)),
                                            ALU.mult).then_inc(q_at.sem((u, 2 * half)), 1)
                elif name in ("mask", "sum"):
                    last_small = min(16, halves(u)[-1])
                    levels = 1 + len([x for x in halves(u) if x <= 16])
                    w, nb = min(32, width(u)), n // width(u)
                    rows = slice(0, P if u != "m" else w)
                    within = masked[u if u == "m" else SLOT[u]][rows, 0:levels, 0:nb, 0:w]
                    if name == "mask":
                        dve.wait_ge(*scored.done((u, last_small), h))
                        nc.vector.tensor_tensor(within, (meta_small if u == "m" else small[SLOT[u]])[rows, 0:levels, 0:nb, 0:w],
                                                masks[rows, 0:levels, 0:w].unsqueeze(2).broadcast_to([rows.stop, levels, nb, w]),
                                                ALU.mult).then_inc(masked_at.sem(u), 1)
                    else:
                        dve.wait_ge(*masked_at.done(u, h))
                        if u == "m":
                            dve.wait_ge(*read.previous(u, h))
                        else:
                            dve.wait_ge(*placed.previous(u, h))
                        nc.vector.tensor_reduce(diag[u][rows, 0:nb, 0:w], within.rearrange("p l b t -> p b t l"),
                                                AX_X, ALU.add).then_inc(summed.sem(u), 1)
                elif name == "carry":
                    dve.wait_ge(*k_added.done(u, h))
                    if u == "m":
                        dve.wait_ge(*read.previous(0, h))
                        nc.vector.tensor_copy(state[0][:, 0, :], added[:, 0:P]).then_inc(states.sem((u, 0)), 1)
                    else:
                        dve.wait_ge(*total_at.done((u, P), h))
                        if u < 3:
                            dve.wait_ge(*read.previous(u + 1, h))
                        for i in range(added_blocks(u)):
                            before = (u, i - 1) if i else (("m", 0) if u == 0 else (u - 1, 3))
                            dve.wait_ge(*states.done(before, h))
                            to = state[u][:, i + 1, :] if i < 3 else state[u + 1][:, 0, :]
                            nc.vector.scalar_tensor_tensor(to, state[u][:, i, :], total(u, P)[:, i:i + 1],
                                                           added[:, i * P:(i + 1) * P], ALU.mult, ALU.add
                                                           ).then_inc(states.sem((u, i)), 1)
                elif name == "norm":
                    dve.wait_ge(*meaned.done(u, h))
                    dve.wait_ge(*rstd_made.previous("all", h))
                    nb, first = n // width(u), 0 if u == "m" else 1 + 4 * u
                    nc.vector.tensor_scalar(ms[0:width(u), first:first + nb], added[0:width(u), 0:nb], EPS, None, ALU.add
                                            ).then_inc(ms_made.sem(u), 1)
                elif name == "out":
                    dve.wait_ge(*read.done(u, h))
                    dve.wait_ge(*squared.done(u, h))
                    dve.wait_ge(*silu_made.done(u, h))
                    dve.wait_ge(left[u], h * 16 + 16)
                    nc.vector.scalar_tensor_tensor(result[u][:, :], o[:, 0:n], out_gain[:, 0:1], gate[u][:, :],
                                                   ALU.mult, ALU.mult).then_inc(mixed_at.sem(u), 1)
                elif name == "rms":
                    dve.wait_ge(*rstd_on_psum.done("all", h))
                    dve.wait_ge(rstd_left, h * 16 + 16)
                    nc.vector.tensor_copy(rstd_turned[:, :], added[0:1 + TILES, 0:P]).then_inc(rstd_copied.sem("all"), 1)

            for st in first_steps:
                step(st, 0)
            with dve.Fori(0, HEADS - 1) as h:
                for ahead, *st in steps:
                    step(st, h + 1 if ahead else h)
            for st in last_steps:
                step(st, HEADS - 1)

        @block.tensor
        def _(pe):
            for x in (scored, v_turned, k_turned, k_added, read, meaned, rstd_on_psum):
                x.credit(pe)

            def before(order, u, h):
                return order.previous(UNITS[-1], h) if u == UNITS[0] else order.done(UNITS[UNITS.index(u) - 1], h)

            def step(st, h):
                name, u = st[0:2]
                w = 0 if u in ("all", "lb") else width(u)
                if name == "turn_v":
                    pe.wait_ge(raw_in[u], h * 16 + 16)
                    pe.wait_ge(*(masked_at.done("m", h) if u == 2 else before(v_made, u, h)))
                    for i, cols in blocks(u):
                        last = nc.tensor.transpose(turned_v[0:w, i, :], raw[u][:, v_i, cols], common.ident[:, :])
                    last.then_inc(v_turned.sem(u), 1)
                elif name == "level":
                    half, ps = st[2], meta_small if u == "m" else small[SLOT[u]]
                    pe.wait_ge(*q_at.done((u, half), h))
                    if half > 1:
                        pe.wait_ge(*k_at.done((u, half), h))
                    elif u == "m":
                        pe.wait_ge(*v_made.done(1, h))
                    else:
                        pe.wait_ge(*(spread.done(u - 2, h) if u > 1 else spread.previous(u + 2, h)))
                    if half == 32:
                        pe.wait_ge(*masked_at.done(u, h))
                    if half == 64:
                        half64 = ps[0:64, 0:2, :, :].rearrange("p a b t -> p (a b t)").rearrange("p (b t) -> p b t", t=64)
                    for i, cols in blocks(u):
                        c = cols.start
                        if half == 64:
                            last = nc.tensor.matmul(half64[:, i, :], dk[u][:, c:c + 64], dq[u][:, c + 64:c + 128],
                                                    start=True, stop=True)
                        elif half == 32:
                            for p0 in (0, 64):
                                last = nc.tensor.matmul(ps[p0:p0 + 32, 6, i, :], dk[u][:, c + p0:c + p0 + 32],
                                                        dq[u][:, c + p0 + 32:c + p0 + 64], start=True, stop=True)
                        else:
                            level = half.bit_length()
                            for p0 in range(0, w, 32):
                                n = min(32, w)
                                part = slice(c + p0, c + p0 + n)
                                if half == 1:
                                    nc.tensor.matmul(ps[p0:p0 + n, 0, i, 0:n], dk[u][:, part], raw[u][:, q_i, part],
                                                     start=True, stop=True)
                                last = nc.tensor.matmul(ps[p0:p0 + n, level, i, 0:n], dk[u][:, part], dq[u][:, part],
                                                        start=True, stop=True)
                    last.then_inc(scored.sem((u, half)), 1)
                elif name == "turn_k":
                    pe.wait_ge(*k_at.done((u, w), h))
                    pe.wait_ge(*before(k_made, u, h))
                    for i, cols in blocks(u):
                        last = nc.tensor.transpose(turned_k[0:w, i, :], dk[u][:, cols], common.ident[:, :])
                    last.then_inc(k_turned.sem(u), 1)
                elif name == "carry":
                    pe.wait_ge(*v_made.done(u, h))
                    pe.wait_ge(*k_made.done(u, h))
                    for prior in added_users[("carry", u)]:
                        pe.wait_ge(*prior(h))
                    for i, cols in blocks(u)[0:added_blocks(u)]:
                        last = nc.tensor.matmul(added[:, i * P:(i + 1) * P], kT[u][0:w, i, :], v[u][0:w, i, :],
                                                start=True, stop=True)
                    last.then_inc(k_added.sem(u), 1)
                elif name == "out":
                    pe.wait_ge(*before(mixed_at, u, h))
                    if u == "m":
                        pe.wait_ge(*summed.done(u, h))
                        last = nc.tensor.matmul(o[:, 0:w], v[u][0:w, 0, :], diag[u][0:w, 0, 0:w], start=True, stop=True)
                    else:
                        pe.wait_ge(*placed.done(u, h))
                        pe.wait_ge(*spread.done(u, h))
                        pe.wait_ge(*states.done((u, 2), h))
                        for i, cols in blocks(u):
                            nc.tensor.matmul(o[:, cols], v[u][:, i, :], scores[u][:, i, :], start=True, stop=False)
                            last = nc.tensor.matmul(o[:, cols], state[u][:, i, :], dq[u][:, cols], start=False, stop=True)
                    last.then_inc(read.sem(u), 1)
                elif name == "norm":
                    pe.wait_ge(*squared.done(u, h))
                    for prior in added_users[("norm", u)]:
                        pe.wait_ge(*prior(h))
                    for i, cols in blocks(u):
                        last = nc.tensor.matmul(added[0:w, i:i + 1], squares[u][:, cols], mean_of[:, 0:1],
                                                start=True, stop=True)
                    last.then_inc(meaned.sem(u), 1)
                elif name == "rms":
                    pe.wait_ge(*rstd_made.done("all", h))
                    for prior in added_users[("rms", "all")]:
                        pe.wait_ge(*prior(h))
                    nc.tensor.transpose(added[0:1 + TILES, 0:P], rstd[:, :], common.ident[:, :]
                                        ).then_inc(rstd_on_psum.sem("all"), 1)

            for st in first_steps:
                step(st, 0)
            with pe.Fori(0, HEADS - 1) as h:
                for ahead, *st in steps:
                    step(st, h + 1 if ahead else h)
            for st in last_steps:
                step(st, HEADS - 1)

LEAD = 7


def attention_steps():
    score, values = [], []
    for g in (3, 2, 1, 0):
        for c in [*range(g, -1, -1), "m"]:
            parts = [0] if c == "m" else range(4)
            score += [("score", g, c, i) for i in parts]
            values += [(g, c, j) for j in parts]
    steps = []
    for n, at in enumerate(values):
        steps.append((int(n + 1 >= len(values)), "turn") + values[(n + 1) % len(values)])
        steps.append((int(n + LEAD >= len(score)),) + score[(n + LEAD) % len(score)])
        steps.append((0, "multiply") + at)
        if n in (1, 3):
            steps.append((0, "prepare", "m" if n == 3 else 0))
        if at[1] == "m":
            steps.append((0, "finish", at[0]))
            if at[0] > 0:
                steps.append((1, "prepare", at[0]))
    return steps


def last_user(users, slot_of):
    before = {}
    for n, user in enumerate(users):
        same = [m for m in range(len(users)) if slot_of(users[m]) == slot_of(user)]
        at = same.index(n)
        before[user] = (users[same[at - 1]], at == 0)
    return before


def attention(nc, common, stage, proj, mixed):
    steps = attention_steps()
    first_turn = ("turn", 3, 3, 0)
    first_steps = [step[1:] for step in steps if step[0]]

    def in_order(*names):
        return [step[1:] for step in sorted(steps, key=lambda step: -step[0]) if step[1] in names]

    def keys(name):
        return [step[1:] if len(step) > 2 else step[1] for step in in_order(name)]

    CHUNKS = ("m", 0, 1, 2, 3)
    with ExitStack() as ctx:
        s = Space(nc, ctx, stage)
        q_i, k_i, v_i, g_i = range(4)
        raw = s.sb("raw", [P, 4, TOK])
        k_high, k_low, q_high, q_low = (s.sb(n, [P, TOK], F32R) for n in ("k_high", "k_low", "q_high", "q_low"))
        v = s.sb("v", [P, 1 + TILES, P])
        gate_sig, gate = s.sb("gate_sig", [P, TOK]), s.sb("gate", [P, TOK])
        keep = {n: s.sb(f"keep{n}", [P, 4, META if n == "m" else 512]) for n in (0, 1, "m")}
        beta = {n: s.sb(f"beta{n}", [P, 4, META if n == "m" else 512]) for n in (0, 1, "m")}
        a = {n: s.sb(f"a{n}", [P, 4, META if n == "m" else 512]) for n in (0, 1, 2, 3, "m")}
        left_over = s.sb("left_over", [P, 4, TOK + 1])
        aT = [s.sb(f"aT{i}", [P, 512]) for i in range(2)]
        result = [s.sb(f"result{i}", [P, 512]) for i in range(2)]
        z = [s.ps(f"z{i}", [P, 512]) for i in range(4)]
        turned = [s.ps(f"turned{i}", [P, 4, P]) for i in range(2)]
        o = [s.ps(f"o{i}", [P, 512]) for i in range(2)]

        raw_in = {c: s.sem(f"raw_in_{c}") for c in CHUNKS}
        stored = [s.sem(f"stored{i}") for i in range(2)]
        high_made, v_made, gate_sig_made, low_made = (
            s.order(n, keys("prepare")) for n in ("high", "v_made", "gate_sig", "low"))
        gate_made = s.order("gate", [c for c in keys("prepare") if c != "m"])
        v_turned = s.order("v_turned", keys("prepare"))
        scored = s.order("scored", keys("score"))
        keep_made, beta_made = s.order("keep_made", keys("score")), s.order("beta_made", keys("score"))
        diagonal = [(g, c, i) for g, c, i in keys("score") if c == g]
        cut_off = s.order("cut_off", diagonal)
        scanned = s.order("scanned", keys("score"))
        a_made = s.order("a_made", keys("score"))
        a_turned = s.order("a_turned", keys("turn"))
        aT_made = s.order("aT_made", keys("turn"))
        multiplied = s.order("multiplied", keys("multiply"))
        finished = s.order("finished", keys("finish"))

        units = [(g, c) for g, c, i in keys("score") if i == 0]
        wide_units = [u for u in units if u[1] != "m"]
        sig_slot = {u: "m" if u[1] == "m" else wide_units.index(u) % 2 for u in units}
        a_slot = {u: "m" if u[1] == "m" else 3 if u == wide_units[-1] else wide_units.index(u) % 3 for u in units}

        def tiles_of(c):
            return (0,) if c == "m" else range(4)

        def last_of(c):
            return 0 if c == "m" else 3

        turns = [st for st in steps if st[1] in ("prepare", "turn")]
        turned_slot = {st[1:]: n % 2 for n, st in enumerate(turns)}
        turned_before = {}
        for n, (ahead, *st) in enumerate(turns):
            back = next(m for m in range(n - 1, n - 4, -1) if turned_slot[turns[m][1:]] == turned_slot[tuple(st)])
            turned_before[tuple(st)] = (turns[back][1:], turns[back][0] - ahead - (back < 0))
        aT_slot = {k: n % 2 for n, k in enumerate(keys("turn"))}
        aT_before = last_user(keys("turn"), lambda k: aT_slot[k])
        z_slot = {k: n % 4 for n, k in enumerate(keys("score"))}
        z_before = last_user(keys("score"), lambda k: z_slot[k])
        sig_before = last_user(units, lambda u: sig_slot[u])
        a_before = last_user(units, lambda u: a_slot[u])
        o_before = last_user(keys("finish"), lambda g: g % 2)

        def row_before(g, c, i):
            prior = g + 1 if g < 3 else (0 if c == "m" else c)
            return ((prior, "m", 0) if c in ("m", 0) else (prior, c - 1, i)), g == 3

        proj_h = proj.rearrange("(a h) p t -> h p a t", a=4)
        block = ctx.enter_context(nc.Block())

        def span(c):
            return slice(0, META) if c == "m" else slice(META + c * 512, META + (c + 1) * 512)

        def value(order, key, before, rnd):
            return order.previous(key, rnd) if before else order.done(key, rnd)

        @block.sync
        def _(sp):
            def load(c, head):
                sp.dma_start(raw[:, :, span(c)], proj_h[bass.ds(head, 1), :, :, span(c)].rearrange("h p a t -> (h p) a t")
                             ).then_inc(raw_in[c], 16)

            def reload(c, rnd, head):
                for order in (high_made, low_made, v_made) + (() if c == "m" else (gate_made,)):
                    common.wait_apart(sp, order.sem, order.done(c, rnd))
                load(c, head)

            def store(g, h):
                common.wait_apart(sp, finished.sem, finished.done(g, h))
                sp.dma_start(mixed[bass.ds(h, 1), :, span(g)].rearrange("h p t -> (h p) t"), result[g % 2][:, :]
                             ).then_inc(stored[g % 2], 16)

            def head(h, late=False):
                for ahead, name, *rest in steps:
                    if name == "prepare":
                        rnd = h + 1 if ahead else h
                        if not late:
                            reload(rest[0], rnd, h + (1 + ahead))
                        elif rnd < HEADS - 1 + ahead:
                            reload(rest[0], rnd, min(rnd + 1, HEADS - 1))
                    elif name == "finish":
                        store(rest[0], h)

            for c in CHUNKS:
                load(c, 0)
            for name, *rest in first_steps:
                if name == "prepare":
                    reload(rest[0], 0, 1)
            with sp.Fori(0, HEADS - 2) as h:
                head(h)
            head(HEADS - 2, late=True)
            head(HEADS - 1, late=True)
            for i in range(2):
                sp.wait_ge(stored[i], 16 * 2 * HEADS + 16)

        @block.scalar
        def _(act):
            for x in (high_made, v_made, gate_sig_made, keep_made, beta_made):
                x.credit(act)
            def step(st, h):
                if st[0] == "prepare":
                    c = st[1]
                    cols = span(c)
                    act.wait_ge(raw_in[c], h * 16 + 16)
                    act.wait_ge(scored.sem, scored.previous((0 if c == "m" else c, "m", 0), h))
                    if c != "m":
                        act.wait_ge(finished.sem, finished.previous(c, h))
                        nc.scalar.activation(q_high[:, cols], raw[:, q_i, cols], ACT.Copy)
                        nc.scalar.activation(gate_sig[:, cols], raw[:, g_i, cols], ACT.Sigmoid)
                    nc.scalar.activation(k_high[:, cols], raw[:, k_i, cols], ACT.Copy).then_inc(high_made.sem, 1)
                    act.wait_ge(v_turned.sem, v_turned.done(c, h))
                    act.wait_ge(multiplied.sem, multiplied.previous((0 if c == "m" else c, c, last_of(c)), h))
                    ps = turned[turned_slot[st]]
                    if c == "m":
                        nc.scalar.activation(v[0:META, 0, :], ps[0:META, 0, :], ACT.Copy).then_inc(v_made.sem, 1)
                    else:
                        nc.scalar.activation(v[:, 1 + 4 * c:5 + 4 * c, :], ps[:, :, :], ACT.Copy).then_inc(v_made.sem, 1)
                elif st[0] == "score":
                    _, g, c, i = st
                    key = (g, c, i)
                    act.wait_ge(scored.sem, scored.done(key, h))
                    (pg, pc), wrapped = sig_before[(g, c)]
                    act.wait_ge(a_made.sem, value(a_made, (pg, pc, i), wrapped, h))
                    n = sig_slot[(g, c)]
                    if c == "m":
                        zi, to_keep, to_beta = z[z_slot[key]][:, 0:4 * META], keep[n][:, :, 0:META], beta[n][:, :, 0:META]
                        zi = zi.rearrange("p (i s) -> p i s", s=META)
                    else:
                        nk = P * (i + 1) if c == g else 512
                        zi, to_keep, to_beta = z[z_slot[key]][:, 0:nk], keep[n][:, i, 0:nk], beta[n][:, i, 0:nk]
                    nc.scalar.activation(to_keep, zi, ACT.Sigmoid, scale=-SB_SCALE).then_inc(keep_made.sem, 1)
                    nc.scalar.activation(to_beta, zi, ACT.Sigmoid, scale=SB_SCALE).then_inc(beta_made.sem, 1)

            for st in first_steps:
                step(st, 0)
            with act.Fori(0, HEADS) as h:
                for st in steps:
                    step(st[1:], h + 1 if st[0] else h)

        @block.gpsimd
        def _(pool):
            for x in (gate_made, cut_off, a_made):
                x.credit(pool)
            def step(st, h):
                if st[0] == "prepare" and st[1] != "m":
                    c = st[1]
                    pool.wait_ge(high_made.sem, high_made.done(c, h))
                    pool.wait_ge(finished.sem, finished.previous(c, h))
                    nc.gpsimd.tensor_tensor(gate[:, span(c)], raw[:, g_i, span(c)], gate_sig[:, span(c)], ALU.mult
                                            ).then_inc(gate_made.sem, 1)
                elif st[0] == "score":
                    _, g, c, i = st
                    key = (g, c, i)
                    n, to = sig_slot[(g, c)], a[a_slot[(g, c)]]
                    if c == g:
                        own = slice(i * P, (i + 1) * P)
                        common.wait_apart(pool, beta_made.sem, beta_made.done(key, h))
                        for tile, fill in ((keep, 1.0), (beta, 0.0)):
                            last = nc.gpsimd.affine_select(out=tile[n][:, i, own], in_=tile[n][:, i, own],
                                                           compare_op=ALU.is_gt, fill=fill, base=0,
                                                           pattern=[[-1, P]], channel_multiplier=1)
                        last.then_inc(cut_off.sem, 1)
                        pool.wait_ge(cut_off.sem, cut_off.done(key, h))
                    else:
                        pool.wait_ge(beta_made.sem, beta_made.done(key, h))
                    pool.wait_ge(scanned.sem, scanned.done(key, h))
                    (pg, pc), wrapped = a_before[(g, c)]
                    pool.wait_ge(a_turned.sem, value(a_turned, (pg, pc, last_of(pc)), wrapped, h))
                    if c == "m":
                        nc.gpsimd.tensor_tensor(to[:, :, 0:META], beta[n][:, :, 0:META],
                                                left_over[:, :, 1:1 + META], ALU.mult).then_inc(a_made.sem, 1)
                    else:
                        nk, first = (P * (i + 1) if c == g else 512), span(c).start
                        nc.gpsimd.tensor_tensor(to[:, i, 0:nk], beta[n][:, i, 0:nk],
                                                left_over[:, i, first + 1:first + 1 + nk], ALU.mult
                                                ).then_inc(a_made.sem, 1)

            for st in first_steps:
                step(st, 0)
            with pool.Fori(0, HEADS) as h:
                for st in steps:
                    step(st[1:], h + 1 if st[0] else h)

        @block.vector
        def _(dve):
            for x in (low_made, scanned, aT_made, finished):
                x.credit(dve)
            for sem in stored:
                dve.sem_inc(sem, 16)
            def step(st, h):
                if st[0] == "prepare":
                    c = st[1]
                    cols = span(c)
                    dve.wait_ge(high_made.sem, high_made.done(c, h))
                    if c != "m":
                        nc.vector.tensor_tensor(q_low[:, cols], raw[:, q_i, cols], q_high[:, cols].bitcast(F32), ALU.subtract)
                    nc.vector.tensor_tensor(k_low[:, cols], raw[:, k_i, cols], k_high[:, cols].bitcast(F32), ALU.subtract
                                            ).then_inc(low_made.sem, 1)
                elif st[0] == "score":
                    _, g, c, i = st
                    key = (g, c, i)
                    n, first = sig_slot[(g, c)], span(c).start
                    prior, wrapped = row_before(*key)
                    dve.wait_ge(a_made.sem, value(a_made, prior, wrapped, h))
                    if c == g:
                        nk = P * (i + 1)
                        nc.vector.memset(left_over[:, i, first + nk:first + nk + 1], 1.0)
                        dve.wait_ge(cut_off.sem, cut_off.done(key, h))
                    else:
                        nk = META if c == "m" else 512
                        dve.wait_ge(keep_made.sem, keep_made.done(key, h))
                        later = (g, 0 if c == "m" else c + 1, 3 if c == "m" else i)
                        dve.wait_ge(scanned.sem, scanned.done(later, h))
                    for t in (range(4) if c == "m" else (i,)):
                        row = left_over[:, t, first:first + nk]
                        data = keep[n][:, t, 0:nk]
                        start = 1.0 if c == g else left_over[:, t, first + nk:first + nk + 1]
                        last = nc.vector.tensor_tensor_scan(row[:, ::-1], data[:, ::-1], data[:, ::-1], start,
                                                            ALU.mult, ALU.bypass)
                    last.then_inc(scanned.sem, 1)
                elif st[0] == "turn":
                    _, g, c, j = st
                    key = (g, c, j)
                    dve.wait_ge(a_turned.sem, a_turned.done(key, h))
                    prior, wrapped = aT_before[key]
                    dve.wait_ge(multiplied.sem, value(multiplied, prior, wrapped, h))
                    i0 = j if c == g else 0
                    rows = slice(0, META if c == "m" else P)
                    nc.vector.tensor_copy(aT[aT_slot[key]][rows, i0 * P:512],
                                          turned[turned_slot[st]][rows, i0:4, :].rearrange("p i t -> p (i t)")
                                          ).then_inc(aT_made.sem, 1)
                elif st[0] == "finish":
                    g = st[1]
                    dve.wait_ge(multiplied.sem, multiplied.done((g, "m", 0), h))
                    dve.wait_ge(gate_made.sem, gate_made.done(g, h))
                    dve.wait_ge(stored[g % 2], h * 32 + (16 + 16 * ((3 - g) // 2)))
                    nc.vector.tensor_tensor(result[g % 2][:, :], o[g % 2][:, :], gate[:, span(g)], ALU.mult
                                            ).then_inc(finished.sem, 1)

            for st in first_steps:
                step(st, 0)
            with dve.Fori(0, HEADS) as h:
                for st in steps:
                    step(st[1:], h + 1 if st[0] else h)

        @block.tensor
        def _(pe):
            for x in (v_turned, scored, a_turned, multiplied):
                x.credit(pe)

            def wait_turned(st, h):
                prior, rounds = turned_before[st]
                order = v_made if prior[0] == "prepare" else aT_made
                key = prior[1] if prior[0] == "prepare" else prior[1:]
                rnd = h if rounds == 0 else h + rounds
                pe.wait_ge(order.sem, order.previous(key, h) if rounds == -1 else order.done(key, rnd))
                chunks = v_made.keys
                if st == first_turn:
                    pe.wait_ge(v_made.sem, v_made.done(1, h))
                elif st == ("prepare", chunks[0]):
                    pe.wait_ge(v_made.sem, v_made.previous(chunks[-1], h))
                elif st[0] == "prepare":
                    pe.wait_ge(v_made.sem, v_made.done(chunks[chunks.index(st[1]) - 1], h))

            def step(st, h):
                if st[0] == "prepare":
                    c = st[1]
                    pe.wait_ge(raw_in[c], h * 16 + 16)
                    wait_turned(st, h)
                    ps = turned[turned_slot[st]]
                    w, cols = (META if c == "m" else P), span(c)
                    for j in tiles_of(c):
                        last = nc.tensor.transpose(ps[0:w, j, :], raw[:, v_i, cols.start + j * P:cols.start + j * P + w],
                                                   common.ident[:, :])
                    last.then_inc(v_turned.sem, 1)
                elif st[0] == "score":
                    _, g, c, i = st
                    for chunk in (g, c):
                        pe.wait_ge(low_made.sem, low_made.done(chunk, h))
                    prior, wrapped = z_before[(g, c, i)]
                    pe.wait_ge(beta_made.sem, value(beta_made, prior, wrapped, h))
                    nk = META if c == "m" else P * (i + 1) if c == g else 512
                    ks = slice(span(c).start, span(c).start + nk)
                    for t in (range(4) if c == "m" else (i,)):
                        qs = slice(span(g).start + t * P, span(g).start + (t + 1) * P)
                        bank = z[z_slot[(g, c, i)]]
                        to = bank[:, t * META:(t + 1) * META] if c == "m" else bank[:, 0:nk]
                        nc.tensor.matmul(to, q_high[:, qs], k_high[:, ks], start=True, stop=False)
                        nc.tensor.matmul(to, q_high[:, qs], k_low[:, ks], start=False, stop=False)
                        last = nc.tensor.matmul(to, q_low[:, qs], k_high[:, ks], start=False, stop=True)
                    last.then_inc(scored.sem, 1)
                elif st[0] == "turn":
                    _, g, c, j = st
                    pe.wait_ge(a_made.sem, a_made.done((g, c, last_of(c)), h))
                    wait_turned(st, h)
                    of_unit, w = a[a_slot[(g, c)]], (META if c == "m" else P)
                    for i in range(j if c == g else 0, 4):
                        last = nc.tensor.transpose(turned[turned_slot[st]][0:w, i, :], of_unit[:, i, j * P:j * P + w],
                                                   common.ident[:, :])
                    last.then_inc(a_turned.sem, 1)
                elif st[0] == "multiply":
                    _, g, c, j = st
                    key = (g, c, j)
                    pe.wait_ge(aT_made.sem, aT_made.done(key, h))
                    pe.wait_ge(v_made.sem, v_made.done(c, h))
                    if c == g and j == 0:
                        prior, wrapped = o_before[g]
                        pe.wait_ge(finished.sem, value(finished, prior, wrapped, h))
                    i0, w = (j if c == g else 0), (META if c == "m" else P)
                    tile = 0 if c == "m" else 1 + 4 * c + j
                    nc.tensor.matmul(o[g % 2][:, i0 * P:512], v[0:w, tile, :], aT[aT_slot[key]][0:w, i0 * P:512],
                                     start=(c == g and j == 0), stop=(c == "m")).then_inc(multiplied.sem, 1)

            for st in first_steps:
                step(st, 0)
            with pe.Fori(0, HEADS) as h:
                for st in steps:
                    step(st[1:], h + 1 if st[0] else h)



def program(nc, x, meta_tokens, pre_norm, post_norm, hgrn_w_in, hgrn_lb, hgrn_out_norm, hgrn_w_out, sb_w_in, sb_w_out, level_masks, out):
    proj = nc.dram_tensor("proj", (4 * HEADS, P, TOK), F32, kind="Internal").ap()
    mixed = nc.dram_tensor("mixed", (HEADS, P, TOK), F32, kind="Internal").ap()
    h1 = nc.dram_tensor("h1", (TOK, D), F32, kind="Internal").ap()
    rstd_rows = nc.dram_tensor("rstd_rows", (HEADS, 1 + TILES, P), F32, kind="Internal").ap()
    rows = x[0]
    with ExitStack() as ctx:
        s = Space(nc, ctx, "all")
        ident = s.sb("ident", [P, P])
        made = s.sem("made")
        with nc.Block() as block:
            @block.gpsimd
            def _(pool):
                nc.gpsimd.memset(ident[:, :], 1.0).then_inc(made, 1)
                pool.wait_ge(made, 1)
                nc.gpsimd.affine_select(out=ident[:, :], in_=ident[:, :], compare_op=ALU.is_equal, fill=0.0,
                                        base=0, pattern=[[-1, P]], channel_multiplier=1).then_inc(made, 1)
                pool.wait_ge(made, 2)

        common = Common(ident, s.sem("apart"))
        with ExitStack() as yctx:
            y = Space(nc, yctx, "y0")
            yT_high, yT_low = (y.sb(n, [P, KT, TOK], F32R) for n in ("high", "low"))
            with nc.cleanup_on_exit():
                normalise(nc, "n0", meta_tokens, rows, pre_norm[0], common, yT_high, yT_low)
            with nc.cleanup_on_exit():
                project(nc, "p0", hgrn_w_in[0], yT_high, yT_low, proj)
        with nc.cleanup_on_exit():
            recurrence(nc, common, "r0", proj, hgrn_lb, hgrn_out_norm[0], level_masks, mixed, rstd_rows)
        with nc.cleanup_on_exit():
            contract(nc, common, "c0", mixed, rstd_rows, hgrn_w_out[0], post_norm[0], meta_tokens, rows, h1[0:META, :], h1[META:TOK, :])
        with ExitStack() as yctx:
            y = Space(nc, yctx, "y1")
            yT_high, yT_low = (y.sb(n, [P, KT, TOK], F32R) for n in ("high", "low"))
            with nc.cleanup_on_exit():
                normalise(nc, "n1", h1[0:META, :], h1[META:TOK, :], pre_norm[1], common, yT_high, yT_low)
            with nc.cleanup_on_exit():
                project(nc, "p1", sb_w_in[0], yT_high, yT_low, proj)
        with nc.cleanup_on_exit():
            attention(nc, common, "a1", proj, mixed)
        with nc.cleanup_on_exit():
            contract(nc, common, "c1", mixed, None, sb_w_out[0], post_norm[1], None, h1[META:TOK, :], None, out[0])


OUT_SHAPE = (1, SEQ, D)
INPUTS = ("x", "meta_tokens", "pre_norm", "post_norm", "hgrn_w_in", "hgrn_lb", "hgrn_out_norm", "hgrn_w_out",
          "sb_w_in", "sb_w_out")


def small_level_masks():
    s, t = np.arange(P)[:, None, None] % 32, np.arange(32)[None, None, :]
    size = 2 ** np.arange(1, 6)[None, :, None]
    level = (s // size == t // size) & (s % size < size // 2) & (t % size >= size // 2)
    own = np.arange(P)[:, None] // 32 == np.arange(4)[None, :]
    return np.concatenate([np.concatenate([s == t, level], axis=1).reshape(P, 6 * 32), own], axis=1).astype(np.float32)


def kernel(**inputs):
    import concourse.bacc as bacc
    from concourse.bass_utils import run_bass_kernel_spmd

    nc = bacc.Bacc("TRN2", target_bir_lowering=False, num_devices=1)
    arrays, args = {}, []
    for name in INPUTS:
        a = np.ascontiguousarray(inputs[name])
        if name == "hgrn_lb":
            a = np.ascontiguousarray(a.reshape(2, HEADS, P).transpose(2, 0, 1))
        arrays[f"in_{name}"] = a
        args.append(nc.dram_tensor(f"in_{name}", a.shape, F32, kind="ExternalInput").ap())
    arrays["level_masks"] = small_level_masks()
    args.append(nc.dram_tensor("level_masks", (P, 6 * 32 + 4), F32, kind="ExternalInput").ap())
    args.append(nc.dram_tensor("out_h", OUT_SHAPE, F32, kind="ExternalOutput").ap())
    program(nc, *args)
    return run_bass_kernel_spmd(nc, [arrays], core_ids=[0]).results[0]["out_h"]
```

```python
from contextlib import ExitStack

import numpy as np

import concourse.bass as bass
from concourse import mybir

F32 = mybir.dt.float32
F32R = mybir.dt.float32r
ALU = mybir.AluOpType
ACT = mybir.ActivationFunctionType
AX_X = mybir.AxisListType.X

P = 128
D = 1024
KT = D // P
HEADS = D // P
SEQ = 2048
META = 16
TOK = META + SEQ
TILES = SEQ // P
EPS = 1e-6
SB_SCALE = float(P) ** -0.5


class Order:

    def __init__(self, sem, keys):
        self.sem, self.keys = sem, list(keys)

    def credit(self, engine):
        engine.sem_inc(self.sem, len(self.keys))

    def previous(self, key, rnd):
        return rnd * len(self.keys) + (self.keys.index(key) + 1)

    def done(self, key, rnd):
        return self.previous(key, rnd) + len(self.keys)


class AheadOrder:

    def __init__(self, orders):
        self.orders = orders

    def of(self, key):
        return next(order for order in self.orders if key in order.keys)

    def credit(self, engine):
        for order in self.orders:
            order.credit(engine)

    def sem(self, key):
        return self.of(key).sem

    def previous(self, key, rnd):
        return self.of(key).sem, self.of(key).previous(key, rnd)

    def done(self, key, rnd):
        return self.of(key).sem, self.of(key).done(key, rnd)


class Space:

    def __init__(self, nc, ctx, stage):
        self.nc, self.ctx, self.stage = nc, ctx, stage

    def sb(self, name, shape, dt=F32):
        return self.ctx.enter_context(self.nc.sbuf_tensor(f"{self.stage}_{name}", shape, dt))

    def ps(self, name, shape):
        return self.ctx.enter_context(self.nc.psum_tensor(f"{self.stage}_{name}", shape, F32))

    def sem(self, name):
        return self.nc.alloc_semaphore(f"{self.stage}_{name}")

    def order(self, name, keys):
        return Order(self.sem(name), keys)

    def ahead_order(self, name, keys):
        return AheadOrder([self.order(f"{name}{of}", [key for ahead, key in keys if ahead == flag])
                           for flag, of in ((1, "_ahead"), (0, "")) if any(ahead == flag for ahead, key in keys)])


class Common:

    def __init__(self, ident, apart):
        self.ident, self.apart = ident, apart

    def wait_apart(self, engine, sem, value):
        engine.wait_ge(sem, value)
        engine.sem_inc(self.apart, 1)


def row_to_all(row):
    return row.unsqueeze(0).broadcast_to([P, row.shape[0]])


META_BUF = 2


def credit(engine, *sems, by=1):
    for sem in sems:
        engine.sem_inc(sem, by)


FIRST = 2


def normalise(nc, stage, rows_meta, rows_seq, gain, common, yT_high, yT_low, w_in, proj):
    QUADS = TILES // 4
    WIDE = 4 * P
    with ExitStack() as ctx:
        s = Space(nc, ctx, stage)
        gain_all = s.sb("gain", [P, D])
        x = [s.sb(f"x{b}", [P, D]) for b in range(4)]
        y = [s.sb(f"y{b}", [P, D]) for b in range(2)]
        squares = s.sb("squares", [P, D])
        sumsq, rms, rstd = (s.sb(n, [P, 4]) for n in ("sumsq", "rms", "rstd"))
        minus_half = s.sb("minus_half", [P, 1])
        w = [s.sb(f"w{c}", [P, KT, P]) for c in range(FIRST)]
        w_high, w_low = ([s.sb(f"{n}{c}", [P, KT, P], F32R) for c in range(FIRST)] for n in ("wh", "wl"))
        out_cols = [s.sb(f"out{c}", [P, WIDE]) for c in range(FIRST)]
        yT = [s.ps(f"yT{b}", [P, KT, P]) for b in range(3)]
        acc = [s.ps(f"acc{c}", [P, WIDE]) for c in range(FIRST)]
        gain_in = s.sem("gain_in")
        x_in = [s.sem(f"x_in{b}") for b in range(4)]
        w_loaded = [s.sem(f"w_loaded{c}") for c in range(FIRST)]
        sumsq_ready, rms_ready, rstd_ready, half_ready = (s.sem(n) for n in ("sumsq", "rms", "rstd", "half"))
        y_ready, yT_ready, high_done, low_done = (s.sem(n) for n in ("y", "yT", "high", "low"))
        w_high_ready, w_low_ready, products, copied = (s.sem(n) for n in ("w_high", "w_low", "products", "copied"))
        stored = [s.sem(f"stored{c}") for c in range(FIRST)]
        w_cols = w_in.rearrange("(k p) n -> p k n", p=P)
        block = ctx.enter_context(nc.Block())


        def rows_of(j):
            return META if j < 0 else P

        def columns(n, j):
            return slice(0, META) if j < 0 else bass.ds(n * P + (META - P), P)

        def run(engine, start, finish, project_group=None):
            start(0, -1)
            start(1, 0)
            for n in range(5):
                finish(n, (n - 1) % 4 if n else -1)
                start(n + 2, (n + 1) % 4)

            def group(i, ahead):
                for j in range(4):
                    finish(i * 4 + (5 + j), j)
                    if ahead or j < 2:
                        start(i * 4 + (7 + j), (j + 2) % 4)
                    if project_group:
                        project_group(i, j)

            with engine.Fori(0, QUADS - 2) as i:
                group(i, True)
            group(QUADS - 2, False)
            if project_group:
                for i in (QUADS - 1, QUADS):
                    for j in range(4):
                        project_group(i, j)

        def nothing(n, j):
            pass

        def group_columns(i):
            return slice(0, META) if isinstance(i, int) and i == QUADS else bass.ds(i * WIDE + META, WIDE)

        def group_width(i):
            return META if isinstance(i, int) and i == QUADS else WIDE

        @block.sync
        def _(sp):
            sp.dma_start(x[3][0:META, :], rows_meta).then_inc(x_in[3], 16)
            sp.dma_start(gain_all[:, :], row_to_all(gain)).then_inc(gain_in, 16)
            for j in range(4):
                if j == 3:
                    sp.wait_ge(y_ready, 2)
                sp.dma_start(x[j][:, :], rows_seq[j * P:(j + 1) * P, :]).then_inc(x_in[j], 16)
                if j % 2 and j // 2 < FIRST:
                    c = j // 2
                    sp.dma_start(w[c][:, :, :], w_cols[:, :, c * P:(c + 1) * P]).then_inc(w_loaded[c], 16)
            with sp.Fori(0, QUADS - 1) as i:
                for j in range(4):
                    sp.wait_ge(y_ready, i * 4 + (j + 3))
                    sp.dma_start(x[j][:, :], rows_seq[bass.ds(i * WIDE + (4 + j) * P, P), :]).then_inc(x_in[j], 16)
            for c in range(FIRST):
                sp.wait_ge(stored[c], 16 * (QUADS + 1) + 16)

        @block.scalar
        def _(act):
            credit(act, sumsq_ready, high_done)
            credit(act, copied, by=FIRST)
            credit(act, *stored, by=16)

            def start(n, j):
                common.wait_apart(act, sumsq_ready, n + 1)
                if j < 0:
                    act.wait_ge(x_in[3], 16)
                else:
                    common.wait_apart(act, x_in[j], (n - j) * 4 + (12 + 16 * (j == 3)))
                nc.scalar.activation(squares[0:rows_of(j), :], x[j][0:rows_of(j), :], ACT.Square,
                                     accum_out=sumsq[0:rows_of(j), j % 4:j % 4 + 1]).then_inc(sumsq_ready, 1)

            def finish(n, j):
                common.wait_apart(act, yT_ready, n + 2)
                for half in range(2):
                    ks = slice(half * KT // 2, (half + 1) * KT // 2)
                    nc.scalar.activation(yT_high[:, ks, columns(n, j)], yT[2 if j < 0 else j % 2][:, ks, 0:rows_of(j)],
                                         ACT.Copy).then_inc(high_done, 1)
                if isinstance(n, int) and n < FIRST:
                    act.wait_ge(w_loaded[n], 16)
                    nc.scalar.activation(w_high[n][:, :, :], w[n][:, :, :], ACT.Copy).then_inc(w_high_ready, 1)

            def read_out(i, j):
                if j % 2:
                    c, width = j // 2, group_width(i)
                    common.wait_apart(act, stored[c], i * 16 + 16)
                    common.wait_apart(act, products, i * FIRST + (c + 1))
                    nc.scalar.activation(out_cols[c][:, 0:width], acc[c][:, 0:width], ACT.Copy).then_inc(copied, 1)
                    common.wait_apart(act, copied, i * FIRST + (FIRST + c + 1))
                    act.dma_start(proj[c, :, group_columns(i)], out_cols[c][:, 0:width]).then_inc(stored[c], 16)

            run(act, start, finish, read_out)

        @block.gpsimd
        def _(pool):
            nc.gpsimd.memset(minus_half[:, :], -0.5).then_inc(half_ready, 1)
            pool.wait_ge(half_ready, 1)
            credit(pool, rms_ready, rstd_ready)

            def tile(n, j):
                rows, col = rows_of(j), slice(j % 4, j % 4 + 1)
                common.wait_apart(pool, sumsq_ready, n + 2)
                nc.gpsimd.tensor_scalar(rms[0:rows, col], sumsq[0:rows, col], 1.0 / D, EPS,
                                        ALU.mult, ALU.add).then_inc(rms_ready, 1)
                pool.wait_ge(rms_ready, n + 2)
                nc.gpsimd.tensor_tensor(rstd[0:rows, col], rms[0:rows, col], minus_half[0:rows, :],
                                        ALU.pow).then_inc(rstd_ready, 1)

            tile(0, -1)
            with pool.Fori(0, QUADS) as i:
                for j in range(4):
                    tile(i * 4 + (1 + j), j)

        @block.vector
        def _(dve):
            dve.wait_ge(gain_in, 16)
            credit(dve, y_ready, low_done)

            def start(n, j):
                dve.wait_ge(rstd_ready, n + 2)
                nc.vector.scalar_tensor_tensor(y[j % 2][0:rows_of(j), :], x[j][0:rows_of(j), :],
                                               rstd[0:rows_of(j), j % 4:j % 4 + 1],
                                               gain_all[0:rows_of(j), :], ALU.mult, ALU.mult).then_inc(y_ready, 1)

            def finish(n, j):
                for half in range(2):
                    dve.wait_ge(high_done, n * 2 + (half + 2))
                    ks = slice(half * KT // 2, (half + 1) * KT // 2)
                    nc.vector.tensor_tensor(yT_low[:, ks, columns(n, j)], yT[2 if j < 0 else j % 2][:, ks, 0:rows_of(j)],
                                            yT_high[:, ks, columns(n, j)].bitcast(F32), ALU.subtract).then_inc(low_done, 1)
                if isinstance(n, int) and n < FIRST:
                    dve.wait_ge(w_high_ready, n + 1)
                    nc.vector.tensor_tensor(w_low[n][:, :, :], w[n][:, :, :], w_high[n][:, :, :].bitcast(F32),
                                            ALU.subtract).then_inc(w_low_ready, 1)

            run(dve, start, finish)

        @block.tensor
        def _(pe):
            credit(pe, yT_ready)

            def turn(n, j):
                pe.wait_ge(y_ready, n + 2)
                if not isinstance(n, int) or n > 2:
                    pe.wait_ge(low_done, n * 2 - 1)
                to, of, rows = yT[2 if j < 0 else j % 2], y[j % 2], rows_of(j)
                for k in range(KT):
                    last = nc.tensor.transpose(to[:, k, 0:rows], of[0:rows, k * P:(k + 1) * P], common.ident[0:rows, 0:rows])
                last.then_inc(yT_ready, 1)

            def multiply(i, j):
                c, width, t = j // 2, group_width(i), group_columns(i)
                if j == 0:
                    pe.wait_ge(low_done, i * 8 + 11 if width == WIDE else 3)
                if j % 2 == 0:
                    pe.wait_ge(w_low_ready, c + 1)
                    pe.wait_ge(copied, i * FIRST + (c + 1))
                for k in range((j % 2) * KT // 2, (j % 2 + 1) * KT // 2):
                    for n, (wp, yp) in enumerate(((w_high, yT_high), (w_high, yT_low), (w_low, yT_high))):
                        last = nc.tensor.matmul(acc[c][:, 0:width], wp[c][:, k, :], yp[:, k, t],
                                                start=(k == 0 and n == 0), stop=(k == KT - 1 and n == 2))
                if j % 2:
                    last.then_inc(products, 1)

            run(pe, nothing, turn, multiply)


def project(nc, stage, w_in, yT_high, yT_low, proj):
    widths = [416, 416, 416, 416, 400]
    starts = [sum(widths[:g]) for g in range(len(widths))]
    assert sum(widths) == TOK
    G = len(widths)
    PAIRS = (4 * HEADS - FIRST) // 2
    with ExitStack() as ctx:
        s = Space(nc, ctx, stage)
        w = [s.sb(f"w{b}", [P, KT, P]) for b in range(2)]
        w_high = [s.sb(f"wh{b}", [P, KT, P], F32R) for b in range(2)]
        w_low = [s.sb(f"wl{b}", [P, KT, P], F32R) for b in range(2)]
        out_rows = [s.sb(f"out{b}", [P, TOK]) for b in range(2)]
        acc = [s.ps(f"acc{g}", [P, 512]) for g in range(G)]
        w_loaded = [s.sem(f"w_loaded{b}") for b in range(2)]
        stored = [s.sem(f"stored{b}") for b in range(2)]
        high_ready, low_ready = s.sem("high"), s.sem("low")
        products = s.order("products", [(b, g) for b in range(2) for g in range(G)])
        copied = s.order("copied", [(b, g) for b in range(2) for g in range(G)])
        w_cols = w_in.rearrange("(k p) n -> p k n", p=P)
        block = ctx.enter_context(nc.Block())

        @block.sync
        def _(sp):
            credit(sp, *stored, by=16)

            def load(b, pair):
                sp.dma_start(w[b][:, :, :], w_cols[:, :, bass.ds(pair * (2 * P) + (FIRST + b) * P, P)]).then_inc(w_loaded[b], 16)

            def store(b, pair):
                sp.wait_ge(copied.sem, copied.done((b, G - 1), pair))
                sp.dma_start(proj[bass.ds(pair * 2 + (FIRST + b), 1), :, :].rearrange("c p t -> (c p) t"),
                             out_rows[b][:, :]).then_inc(stored[b], 16)

            for b in range(2):
                load(b, 0)
            with sp.Fori(0, PAIRS - 1) as pair:
                for b in range(2):
                    sp.wait_ge(low_ready, pair * 2 + (b + 2))
                    load(b, pair + 1)
                    store(b, pair)
            for b in range(2):
                store(b, PAIRS - 1)
            for b in range(2):
                sp.wait_ge(stored[b], 16 * (PAIRS) + 16)

        @block.scalar
        def _(act):
            copied.credit(act)

            def split(b, pair):
                act.wait_ge(w_loaded[b], pair * 16 + 16)
                nc.scalar.activation(w_high[b][:, :, :], w[b][:, :, :], ACT.Copy).then_inc(high_ready, 1)

            def read_out(b, pair):
                act.wait_ge(stored[b], pair * 16 + 16)
                for g in range(G):
                    act.wait_ge(products.sem, products.done((b, g), pair))
                    nc.scalar.activation(out_rows[b][:, starts[g]:starts[g] + widths[g]], acc[g][:, 0:widths[g]],
                                         ACT.Copy).then_inc(copied.sem, 1)

            for b in range(2):
                split(b, 0)
            with act.Fori(0, PAIRS - 1) as pair:
                for b in range(2):
                    read_out(b, pair)
                    split(b, pair + 1)
            for b in range(2):
                read_out(b, PAIRS - 1)

        @block.vector
        def _(dve):
            credit(dve, low_ready)
            with dve.Fori(0, PAIRS) as pair:
                for b in range(2):
                    dve.wait_ge(high_ready, pair * 2 + (b + 1))
                    dve.wait_ge(products.sem, products.previous((b, G - 1), pair))
                    nc.vector.tensor_tensor(w_low[b][:, :, :], w[b][:, :, :], w_high[b][:, :, :].bitcast(F32),
                                            ALU.subtract).then_inc(low_ready, 1)

        @block.tensor
        def _(pe):
            products.credit(pe)
            with pe.Fori(0, PAIRS) as pair:
                for b in range(2):
                    pe.wait_ge(low_ready, pair * 2 + (b + 2))
                    for g in range(G):
                        if b == 0:
                            pe.wait_ge(copied.sem, copied.previous((1, g), pair))
                        else:
                            pe.wait_ge(copied.sem, copied.done((0, g), pair))
                        t = slice(starts[g], starts[g] + widths[g])
                        for k in range(KT):
                            for n, (wp, yp) in enumerate(((w_high, yT_high), (w_high, yT_low), (w_low, yT_high))):
                                last = nc.tensor.matmul(acc[g][:, 0:widths[g]], wp[b][:, k, :], yp[:, k, t],
                                                        start=(k == 0 and n == 0), stop=(k == KT - 1 and n == 2))
                        last.then_inc(products.sem, 1)


def contract(nc, common, stage, mixed, rstd_rows, w_out, gain, res_meta, res_seq, out_meta, out_seq):
    with ExitStack() as ctx:
        s = Space(nc, ctx, stage)
        HALF = D // 2
        wo_high, wo_low = (s.sb(n, [P, KT, D], F32R) for n in ("wo_high", "wo_low"))
        WO_BUFS = 4
        wo = [s.sb(f"wo{b}", [P, D]) for b in range(WO_BUFS)]
        gain_all = s.sb("gain", [P, D])
        minus_half = s.sb("minus_half", [P, 1])
        m = [s.sb(f"m{b}", [P, KT, P]) for b in range(3)]
        r = [s.sb(f"r{b}", [P, KT, P]) for b in range(3)] if rstd_rows is not None else None
        m_high = [s.sb(f"mh{b}", [P, KT, P], F32R) for b in range(3)]
        m_low = [s.sb(f"ml{b}", [P, KT, P], F32R) for b in range(3)]
        res = [s.sb(f"res{b}", [P, D]) for b in range(3)]
        normed = [s.sb(f"normed{b}", [P, D]) for b in range(3)]
        squares = [s.sb(f"squares{b}", [P, D]) for b in range(3)]
        sumsq, rms, rstd = (s.sb(n, [P, 4]) for n in ("sumsq", "rms", "rstd"))
        acc = [s.ps(f"acc{b}", [P, 2, HALF]) for b in range(3)]
        wo_in = [s.sem(f"wo_in{b}") for b in range(WO_BUFS)]
        m_in = [s.sem(f"m_in{b}") for b in range(3)]
        res_in = [s.sem(f"res_in{b}") for b in range(3)]
        stored = [s.sem(f"stored{b}") for b in range(3)]
        names = ("scaled", "wo_high", "wo_low", "gain_in", "m_high", "m_low", "product", "sumsq", "rms", "rstd", "half",
                 "normed", "summed")
        (scaled_ready, wo_high_ready, wo_low_ready, gain_in, high_ready, low_ready, product, sumsq_ready, rms_ready, rstd_ready,
         half_ready, normed_ready, summed) = (s.sem(n) for n in names)
        block = ctx.enter_context(nc.Block())
        with_meta = out_meta is not None

        def steps(engine, raised, start, finish, split_weights=None):
            last = TILES // 2 - 1
            credit(engine, *raised, by=1 if with_meta else 2)
            if with_meta:
                start(META_BUF, META, 0, 0)
            start(0, P, 1, 0)
            if split_weights:
                split_weights()
            start(1, P, 2, 0)
            if with_meta:
                finish(META_BUF, META, 0, 0)
            with engine.Fori(0, last) as pair:
                for b in range(2):
                    finish(b, P, pair * 2 + (1 + b), pair)
                    start(b, P, pair * 2 + (3 + b), pair + 1)
            for b in range(2):
                finish(b, P, last * 2 + 1 + b, last)

        def nothing(b, rows, n, pair):
            pass

        @block.sync
        def _(sp):
            def load(b, n, rows, cols):
                sp.dma_start(m[b][:, :, 0:rows], mixed[:, :, cols].rearrange("k p t -> p k t")).then_inc(m_in[b], 16)
                if r is not None:
                    tile = rstd_rows[:, n:n + 1, 0:rows] if b == META_BUF else rstd_rows[:, bass.ds(n, 1), 0:rows]
                    sp.dma_start(r[b][:, :, 0:rows], tile.rearrange("k n t -> n k t").broadcast_to([P, KT, rows])
                                 ).then_inc(m_in[b], 16)

            def load_residual(b, rows, pair):
                rows_in = res_meta if b == META_BUF else res_seq[bass.ds(pair * (2 * P) + b * P, P), :]
                sp.dma_start(res[b][0:rows, :], rows_in).then_inc(res_in[b], 16)

            def load_tile(b, pair):
                load(b, pair * 2 + (1 + b), P, bass.ds(pair * (2 * P) + (META + b * P), P))

            def store(b, rows, n, pair):
                sp.wait_ge(summed, n + 2)
                to = out_meta if b == META_BUF else out_seq[bass.ds(pair * (2 * P) + b * P, P), :]
                sp.dma_start(to, res[b][0:rows, :]).then_inc(stored[b], 16)

            credit(sp, *stored, by=16)
            last = TILES // 2 - 1
            if with_meta:
                load(META_BUF, 0, META, slice(0, META))
            load_tile(0, 0)
            for k in range(KT):
                if k == WO_BUFS:
                    load_tile(1, 0)
                if k >= WO_BUFS:
                    sp.wait_ge(wo_low_ready, k - WO_BUFS + 1)
                sp.dma_start(wo[k % WO_BUFS][:, :], w_out[k * P:(k + 1) * P, :]).then_inc(wo_in[k % WO_BUFS], 16)
            sp.dma_start(gain_all[:, :], row_to_all(gain)).then_inc(gain_in, 16)
            if with_meta:
                load_residual(META_BUF, META, 0)
            for b in range(2):
                load_residual(b, P, 0)
            if with_meta:
                store(META_BUF, META, 0, 0)
            with sp.Fori(0, last) as pair:
                for b in range(2):
                    n = pair * 2 + (1 + b)
                    sp.wait_ge(low_ready, n + 2)
                    load_tile(b, pair + 1)
                    store(b, P, n, pair)
                    sp.wait_ge(stored[b], pair * 16 + 32)
                    load_residual(b, P, pair + 1)
            for b in range(2):
                store(b, P, last * 2 + 1 + b, last)
            for b in range(2 + with_meta):
                sp.wait_ge(stored[b], 32 if b == META_BUF else 16 * (TILES // 2) + 16)

        @block.scalar
        def _(act):
            def split_weights():
                for k in range(KT):
                    act.wait_ge(wo_in[k % WO_BUFS], 16 * (k // WO_BUFS + 1))
                    nc.scalar.activation(wo_high[:, k, :], wo[k % WO_BUFS][:, :], ACT.Copy).then_inc(wo_high_ready, 1)

            def start(b, rows, n, pair):
                if r is None:
                    act.wait_ge(m_in[b], pair * 16 + 16)
                else:
                    act.wait_ge(scaled_ready, n + 2)
                nc.scalar.activation(m_high[b][:, :, 0:rows], m[b][:, :, 0:rows], ACT.Copy).then_inc(high_ready, 1)

            def finish(b, rows, n, pair):
                act.wait_ge(product, n + 2)
                nc.scalar.activation(squares[b][0:rows, :], acc[b][0:rows, :, :].rearrange("p h n -> p (h n)"), ACT.Square,
                                     accum_out=sumsq[0:rows, b:b + 1]).then_inc(sumsq_ready, 1)

            steps(act, (high_ready, sumsq_ready), start, finish, split_weights)

        @block.gpsimd
        def _(pool):
            nc.gpsimd.memset(minus_half[:, :], -0.5).then_inc(half_ready, 1)
            pool.wait_ge(half_ready, 1)

            def tile(b, rows, n, pair):
                common.wait_apart(pool, sumsq_ready, n + 2)
                nc.gpsimd.tensor_scalar(rms[0:rows, b:b + 1], sumsq[0:rows, b:b + 1], 1.0 / D, EPS,
                                        ALU.mult, ALU.add).then_inc(rms_ready, 1)
                pool.wait_ge(rms_ready, n + 2)
                nc.gpsimd.tensor_tensor(rstd[0:rows, b:b + 1], rms[0:rows, b:b + 1], minus_half[0:rows, :],
                                        ALU.pow).then_inc(rstd_ready, 1)
                pool.wait_ge(res_in[b], pair * 16 + 16)
                pool.wait_ge(normed_ready, n + 2)
                nc.gpsimd.tensor_tensor(res[b][0:rows, :], normed[b][0:rows, :], res[b][0:rows, :],
                                        ALU.add).then_inc(summed, 1)

            steps(pool, (rms_ready, rstd_ready, summed), nothing, tile)

        @block.vector
        def _(dve):
            def split_weights():
                for k in range(KT):
                    dve.wait_ge(wo_high_ready, k + 1)
                    nc.vector.tensor_tensor(wo_low[:, k, :], wo[k % WO_BUFS][:, :], wo_high[:, k, :].bitcast(F32),
                                            ALU.subtract).then_inc(wo_low_ready, 1)
                dve.wait_ge(gain_in, 16)

            def start(b, rows, n, pair):
                if r is not None:
                    dve.wait_ge(m_in[b], pair * 32 + 32)
                    nc.vector.tensor_tensor(m[b][:, :, 0:rows], m[b][:, :, 0:rows], r[b][:, :, 0:rows], ALU.mult
                                            ).then_inc(scaled_ready, 1)
                dve.wait_ge(high_ready, n + 2)
                if not isinstance(n, int):
                    dve.wait_ge(product, n)
                nc.vector.tensor_tensor(m_low[b][:, :, 0:rows], m[b][:, :, 0:rows], m_high[b][:, :, 0:rows].bitcast(F32),
                                        ALU.subtract).then_inc(low_ready, 1)

            def finish(b, rows, n, pair):
                dve.wait_ge(rstd_ready, n + 2)
                if b != META_BUF:
                    dve.wait_ge(summed, pair * 2 + (b + 1))
                nc.vector.scalar_tensor_tensor(normed[b][0:rows, :], acc[b][0:rows, :, :].rearrange("p h n -> p (h n)"),
                                               rstd[0:rows, b:b + 1], gain_all[0:rows, :],
                                               ALU.mult, ALU.mult).then_inc(normed_ready, 1)

            steps(dve, (low_ready, normed_ready, scaled_ready), start, finish, split_weights)

        @block.tensor
        def _(pe):
            def multiply(b, rows, k):
                for mp, wps in ((m_high, (wo_high, wo_low)), (m_low, (wo_high,))):
                    for half in range(2):
                        cols = slice(half * HALF, (half + 1) * HALF)
                        for wp in wps:
                            last = nc.tensor.matmul(acc[b][0:rows, half, :], mp[b][:, k, 0:rows], wp[:, k, cols],
                                                    start=(k == 0 and mp is m_high and wp is wo_high),
                                                    stop=(k == KT - 1 and mp is m_low))
                return last

            credit(pe, product, by=1 if with_meta else 2)
            for k in range(KT):
                pe.wait_ge(wo_low_ready, k + 1)
                for b, rows, n in ([(META_BUF, META, 0)] if with_meta else []) + [(0, P, 1)]:
                    if k == 0:
                        pe.wait_ge(low_ready, n + 2)
                    last = multiply(b, rows, k)
                    if k == KT - 1:
                        last.then_inc(product, 1)
            pe.wait_ge(low_ready, 4)
            for k in range(KT):
                last = multiply(1, P, k)
            last.then_inc(product, 1)
            with pe.Fori(0, TILES // 2 - 1) as pair:
                for b in range(2):
                    pe.wait_ge(low_ready, pair * 2 + (b + 5))
                    pe.wait_ge(normed_ready, pair * 2 + (b + 3))
                    for k in range(KT):
                        last = multiply(b, P, k)
                    last.then_inc(product, 1)


UNITS = ("m", 0, 1, 2, 3)
GROUP = 4 * P
SMALL = (1, 2, 4, 8, 16)
SLOT = {0: 0, 1: 1, 2: 0, 3: 1}


def width(u):
    return META if u == "m" else P


def tokens(u):
    return META if u == "m" else GROUP


def added_blocks(u):
    return 1 if u == "m" else 3 if u == 3 else 4


def halves(u):
    return [h for h in (1, 2, 4, 8, 16, 32, 64) if h < width(u)]


def recurrence_steps():
    def own(*steps):
        return [(0,) + step for step in steps]

    def ahead(*steps):
        return [(1,) + step for step in steps]

    def level(us, h):
        return [("level", u, h) for u in us]

    late, early = (2, 3), (0, 1)
    return (ahead(("load", "m"), ("load", 0), ("load", 1)) + own(*level(late, 1), ("turn_k", 0))
            + own(*level(late, 2), ("turn_k", 1), ("carry", 0)) + ahead(("bound", "lb"), ("gates", "m"))
            + own(*level(late, 4), ("carry", 1), ("out", 0)) + ahead(("gates", 0))
            + own(*level(late, 8), ("norm", 0), ("out", 1)) + ahead(("product", "m"), ("turn_v", "m"))
            + own(*level(late, 16), ("norm", 1)) + ahead(("gates", 1)) + own(("mask", 2), ("mask", 3))
            + ahead(("product", 0)) + own(("sum", 2), ("sum", 3)) + ahead(("turn_v", 0))
            + own(*level(late, 32), ("place", 2), ("place", 3)) + ahead(("product", 1), ("turn_v", 1))
            + own(*level(late, 64), ("spread", 2), ("spread", 3)) + ahead(("load", 2), ("load", 3))
            + ahead(*level(early, 1)) + own(("turn_k", 2)) + ahead(("level", "m", 1))
            + ahead(*level(early, 2)) + own(("turn_k", 3), ("carry", 2)) + ahead(("level", "m", 2))
            + ahead(*level(early, 4)) + own(("carry", 3), ("out", 2)) + ahead(("gates", 2), ("level", "m", 4))
            + ahead(*level(early, 8)) + own(("norm", 2), ("out", 3)) + ahead(("level", "m", 8), ("gates", 3))
            + ahead(*level(early, 16)) + own(("norm", 3)) + ahead(("mask", 0), ("mask", 1), ("product", 2), ("mask", "m"))
            + ahead(("sum", 0), ("sum", 1), ("sum", "m"), ("turn_k", "m"))
            + ahead(*level(early, 32), ("place", 0), ("place", 1)) + own(("rms", "all"), ("rms_out", "all")) + ahead(("product", 3), ("turn_v", 2))
            + ahead(*level(early, 64)) + ahead(("carry", "m"), ("spread", 0), ("spread", 1), ("out", "m"), ("turn_v", 3), ("norm", "m")))


def recurrence(nc, common, stage, proj, lb_logits, out_norm, level_masks, mixed, rstd_rows):
    steps = recurrence_steps()

    first_steps = [step[1:] for step in steps if step[0]]
    last_steps = [step[1:] for step in steps if not step[0]]

    def keys(name):
        return [(step[0], step[2:] if len(step) > 3 else step[2]) for step in steps if step[1] == name]

    with ExitStack() as ctx:
        s = Space(nc, ctx, stage)
        q_i, f_i, v_i, g_i = range(4)

        def each(name, shape, dt=F32):
            return {u: s.sb(f"{name}_{u}", shape(u), dt) for u in UNITS}

        raw = each("raw", lambda u: [P, 4, tokens(u)])
        sig = each("sig", lambda u: [P, 2, tokens(u)])
        decay = each("decay", lambda u: [P, tokens(u)])
        gate_sig = each("gate_sig", lambda u: [P, tokens(u)])
        gate = each("gate", lambda u: [P, tokens(u)])
        dq = each("dq", lambda u: [P, tokens(u)])
        dk = each("dk", lambda u: [P, tokens(u)])
        totals = each("totals", lambda u: [P, GROUP])
        v = each("v", lambda u: [P, tokens(u) // width(u), P])
        kT = each("kT", lambda u: [P, tokens(u) // width(u), P])
        state = {u: s.sb(f"state_{u}", [P, 4, P]) for u in (0, 1, 2, 3)}
        scores = each("scores", lambda u: [P, 4, P])
        masked = {i: s.sb(f"masked{i}", [P, 6, 4, 32]) for i in (0, 1)}
        masked["m"] = s.sb("masked_m", [META, 5, 1, META])
        diag = each("diag", lambda u: [P, 4, 32])
        squares = each("squares", lambda u: [P, tokens(u)])
        ms = s.sb("ms", [P, 1 + TILES])
        rstd = s.sb("rstd", [P, 1 + TILES])
        rstd_turned = s.sb("rstd_turned", [1 + TILES, P])
        result = each("result", lambda u: [P, tokens(u)])
        mask_rows = s.sb("masks", [P, 6 * 32 + 4])
        masks = mask_rows[:, 0:6 * 32].rearrange("p (l t) -> p l t", t=32)
        own_32 = mask_rows[:, 6 * 32:6 * 32 + 4]
        mean_of = s.sb("mean_of", [P, 1])
        minus_half = s.sb("minus_half", [P, 1 + TILES])
        out_gain = s.sb("out_gain", [P, 1])
        logits = s.sb("logits", [P, 2, HEADS])
        lb_work = s.sb("lb_work", [P, 6, HEADS])
        lb, one_less_lb = s.sb("lb", [P, HEADS]), s.sb("one_less_lb", [P, HEADS])
        lb_now = s.sb("lb_now", [P, 2])

        small = [s.ps(f"small{i}", [P, 8, 4, 32]) for i in range(2)]
        turned_v, turned_k = s.ps("turned_v", [P, 4, P]), s.ps("turned_k", [P, 4, P])
        meta_small = turned_v[:, 0, 0:5 * META].rearrange("p (l b t) -> p l b t", b=1, t=META)
        added = s.ps("added", [P, GROUP])
        o = s.ps("o", [P, GROUP])

        raw_in = {u: s.sem(f"raw_in_{u}") for u in UNITS}
        left = {u: s.sem(f"left_{u}") for u in UNITS}
        consts_in, set_up, exps_made, lb_steps = (s.sem(n) for n in ("consts_in", "set_up", "exps_made", "lb_steps"))
        sig_made = s.ahead_order("sig_made", keys("gates"))
        gates_made = s.ahead_order("gates_made", keys("gates"))
        silu_made = s.ahead_order("silu_made", keys("product"))
        q_at = s.ahead_order("q_at", [(st[0], (st[2], 1) if st[1] == "product" else (st[2], 2 * st[3]))
                                      for st in steps if st[1] in ("product", "level")])
        total_at = s.ahead_order("total_at", [(ahead, (u, 2 * h)) for ahead, (u, h) in keys("level")])
        k_at = s.ahead_order("k_at", [(ahead, (u, 2 * h)) for ahead, (u, h) in keys("level")])
        scored = s.ahead_order("scored", keys("level"))
        masked_at = s.ahead_order("masked_at", keys("mask"))
        summed = s.ahead_order("summed", keys("sum"))
        placed = s.ahead_order("placed", keys("place"))
        spread = s.ahead_order("spread", keys("spread"))
        v_turned, k_turned = s.ahead_order("v_turned", keys("turn_v")), s.ahead_order("k_turned", keys("turn_k"))
        v_made, k_made = s.ahead_order("v_made", keys("turn_v")), s.ahead_order("k_made", keys("turn_k"))
        k_added = s.ahead_order("k_added", keys("carry"))
        states = s.ahead_order("states", [(ahead, (u, n)) for ahead, u in keys("carry") for n in range(added_blocks(u))])
        read, meaned = s.ahead_order("read", keys("out")), s.ahead_order("meaned", keys("norm"))
        squared = s.ahead_order("squared", keys("out"))
        ms_made = s.ahead_order("ms_made", keys("norm"))
        mixed_at = s.ahead_order("mixed_at", keys("out"))
        rstd_made = s.ahead_order("rstd_made", keys("rms"))
        rstd_on_psum = s.ahead_order("rstd_on_psum", keys("rms_out"))
        rstd_copied = s.ahead_order("rstd_copied", keys("rms_out"))
        rstd_left = s.sem("rstd_left")
        head_lb = s.ahead_order("head_lb", keys("bound"))

        users = [st for st in first_steps + last_steps if st[0] in ("carry", "norm", "rms_out")]
        added_users = {}
        for at, st in enumerate(users):
            name, u = users[at - 1]
            order, key = {"carry": (states, (u, added_blocks(u) - 1)), "norm": (ms_made, u),
                          "rms_out": (rstd_copied, "all")}[name]
            added_users[st] = [lambda h, order=order, key=key, at=at:
                               (order.done if at else order.previous)(key, h)]

        proj_h = proj.rearrange("(a h) p t -> h p a t", a=4)

        def span(u):
            return slice(0, META) if u == "m" else slice(META + u * GROUP, META + (u + 1) * GROUP)

        def blocks(u):
            w = width(u)
            return [(i, slice(i * w, (i + 1) * w)) for i in range(tokens(u) // w)]

        def by_halves(tile, u, h):
            return tile[u][:, 0:tokens(u)].rearrange("p (m two h) -> p m two h", two=2, h=h)

        def total(u, h):
            n = tokens(u) // h
            t = decay[u][:, 0:n] if h == 1 else totals[u][:, GROUP - 2 * GROUP // h:GROUP - 2 * GROUP // h + n]
            return t.rearrange("p (m two) -> p m two", two=2) if n > 1 and h < width(u) else t

        def load(u, h):
            nc.sync.dma_start(raw[u][:, :, :], proj_h[bass.ds(h, 1), :, :, span(u)].rearrange("h p a t -> (h p) a t")
                              ).then_inc(raw_in[u], 16)

        with nc.Block() as prologue:
            @prologue.sync
            def _(sp):
                sp.dma_start(logits[:, :, :], lb_logits).then_inc(consts_in, 16)
                sp.dma_start(mask_rows[:, :], level_masks).then_inc(consts_in, 16)
                sp.dma_start(out_gain[:, :], out_norm.unsqueeze(1)).then_inc(consts_in, 16)
                for u in UNITS:
                    load(u, 0)
                sp.wait_ge(consts_in, 48)

            @prologue.gpsimd
            def _(pool):
                nc.gpsimd.memset(minus_half[:, :], -0.5).then_inc(set_up, 1)
                nc.gpsimd.memset(mean_of[:, :], 1.0 / P).then_inc(set_up, 1)
                nc.gpsimd.memset(ms[:, :], 1.0).then_inc(set_up, 1)
                pool.wait_ge(set_up, 3)

            @prologue.vector
            def _(dve):
                made = 0

                def chained(op):
                    nonlocal made
                    made += 1
                    op.then_inc(lb_steps, 1)
                    dve.wait_ge(lb_steps, made)

                w = lb_work
                dve.wait_ge(consts_in, 48)
                chained(nc.vector.tensor_tensor(w[:, 0, :], logits[:, 0, :], logits[:, 1, :], ALU.max))
                chained(nc.vector.tensor_tensor(w[:, 1, :], logits[:, 0, :], w[:, 0, :], ALU.subtract))
                chained(nc.vector.tensor_tensor(w[:, 2, :], logits[:, 1, :], w[:, 0, :], ALU.subtract))
                dve.wait_ge(exps_made, 1)
                chained(nc.vector.tensor_tensor(w[:, 5, :], w[:, 3, :], w[:, 4, :], ALU.add))
                chained(nc.vector.reciprocal(w[:, 0, :], w[:, 5, :]))
                chained(nc.vector.tensor_tensor(lb[:, :], w[:, 3, :], w[:, 0, :], ALU.mult))
                chained(nc.vector.tensor_scalar(one_less_lb[:, :], lb[:, :], -1.0, 1.0, ALU.mult, ALU.add))

            @prologue.scalar
            def _(act):
                act.wait_ge(lb_steps, 3)
                nc.scalar.activation(lb_work[:, 3:5, :], lb_work[:, 1:3, :], ACT.Exp).then_inc(exps_made, 1)

        block = ctx.enter_context(nc.Block())

        @block.sync
        def _(sp):
            def store_rstd(h):
                common.wait_apart(sp, *rstd_copied.done("all", h))
                sp.dma_start(rstd_rows[bass.ds(h, 1), :, :].rearrange("h n t -> (h n) t"), rstd_turned[:, :]
                             ).then_inc(rstd_left, 16)

            def store(u, h):
                common.wait_apart(sp, *mixed_at.done(u, h))
                sp.dma_start(mixed[bass.ds(h, 1), :, span(u)].rearrange("h p t -> (h p) t"), result[u][:, :]).then_inc(left[u], 16)

            def step(st, h):
                name, u = st[0:2]
                if name == "load":
                    common.wait_apart(sp, *scored.previous((u, 1), h))
                    common.wait_apart(sp, *v_turned.previous(u, h))
                    common.wait_apart(sp, *silu_made.previous(u, h))
                    load(u, h)
                elif name == "out":
                    store(u, h)
                elif name == "rms_out":
                    store_rstd(h)

            for st in first_steps:
                if st[0] != "load":
                    step(st, 0)
            with sp.Fori(0, HEADS - 1) as h:
                for ahead, *st in steps:
                    step(st, h + 1 if ahead else h)
            for st in last_steps:
                step(st, HEADS - 1)
            sp.wait_ge(rstd_left, 16 * HEADS + 16)
            for u in UNITS:
                sp.wait_ge(left[u], 16 * HEADS + 16)

        @block.scalar
        def _(act):
            for x in (sig_made, gates_made, spread, v_made, k_made, squared):
                x.credit(act)
            def step(st, h):
                name, u = st[0:2]
                if name == "gates":
                    act.wait_ge(*head_lb.done("lb", h))
                    act.wait_ge(raw_in[u], h * 16 + 16)
                    act.wait_ge(*silu_made.previous(u, h))
                    act.wait_ge(*total_at.previous((u, 2 * halves(u)[-1]), h))
                    act.wait_ge(*k_at.previous((u, 2 * halves(u)[-1]), h))
                    act.wait_ge(*k_turned.previous(u, h))
                    nc.scalar.activation(sig[u][:, 0, :], raw[u][:, f_i, :], ACT.Sigmoid)
                    nc.scalar.activation(sig[u][:, 1, :], raw[u][:, f_i, :], ACT.Sigmoid, scale=-1.0).then_inc(sig_made.sem(u), 1)
                    nc.scalar.activation(gate_sig[u][:, :], raw[u][:, g_i, :], ACT.Sigmoid)
                    act.wait_ge(*sig_made.done(u, h))
                    nc.scalar.activation(decay[u][:, :], sig[u][:, 0, :], ACT.Identity, bias=lb_now[:, 0:1],
                                         scale=lb_now[:, 1:2])
                    nc.scalar.activation(dk[u][:, :], sig[u][:, 1, :], ACT.Copy, scale=lb_now[:, 1:2]
                                         ).then_inc(gates_made.sem(u), 1)
                elif name == "turn_v":
                    act.wait_ge(*v_turned.done(u, h))
                    act.wait_ge(*read.previous(u, h))
                    act.wait_ge(*k_added.previous(u, h))
                    w, n = width(u), tokens(u) // width(u)
                    nc.scalar.activation(v[u][0:w, :, :], turned_v[0:w, 0:n, :], ACT.Copy).then_inc(v_made.sem(u), 1)
                elif name == "turn_k":
                    act.wait_ge(*k_turned.done(u, h))
                    act.wait_ge(*k_added.previous(u, h))
                    w, n = width(u), tokens(u) // width(u)
                    nc.scalar.activation(kT[u][0:w, :, :], turned_k[0:w, 0:n, :], ACT.Copy).then_inc(k_made.sem(u), 1)
                elif name == "spread":
                    act.wait_ge(*scored.done((u, 64), h))
                    act.wait_ge(*placed.done(u, h))
                    ps = small[SLOT[u]]
                    for p0 in (0, 64):
                        nc.scalar.activation(scores[u][p0:p0 + 32, :, p0 + 32:p0 + 64], ps[p0:p0 + 32, 6, :, :], ACT.Copy)
                    nc.scalar.activation(scores[u][0:64, :, 64:128],
                                         ps[0:64, 0:2, :, :].rearrange("p a b t -> p (a b t)").rearrange("p (b t) -> p b t", t=64),
                                         ACT.Copy).then_inc(spread.sem(u), 1)
                elif name == "out":
                    act.wait_ge(*read.done(u, h))
                    nc.scalar.activation(squares[u][:, :], o[:, 0:tokens(u)], ACT.Square).then_inc(squared.sem(u), 1)

            for st in first_steps:
                step(st, 0)
            with act.Fori(0, HEADS - 1) as h:
                for ahead, *st in steps:
                    step(st, h + 1 if ahead else h)
            for st in last_steps:
                step(st, HEADS - 1)

        @block.gpsimd
        def _(pool):
            for x in (silu_made, k_at, placed, rstd_made):
                x.credit(pool)
            def step(st, h):
                name, u = st[0:2]
                if name == "product":
                    pool.wait_ge(*gates_made.done(u, h))
                    pool.wait_ge(*mixed_at.previous(u, h))
                    nc.gpsimd.tensor_tensor(gate[u][:, :], raw[u][:, g_i, :], gate_sig[u][:, :], ALU.mult
                                            ).then_inc(silu_made.sem(u), 1)
                elif name == "level":
                    half = st[2]
                    pool.wait_ge(*scored.done((u, half), h))
                    if half > 1:
                        pool.wait_ge(*total_at.done((u, half), h))
                        pool.wait_ge(*k_at.done((u, half), h))
                    left_half = by_halves(dk, u, half)[:, :, 0, :]
                    right_total = total(u, half)[:, :, 1:2].broadcast_to(list(left_half.shape))
                    nc.gpsimd.tensor_tensor(left_half, left_half, right_total, ALU.mult).then_inc(k_at.sem((u, 2 * half)), 1)
                elif name == "place":
                    pool.wait_ge(*summed.done(u, h))
                    pool.wait_ge(*read.previous(u, h))
                    nc.gpsimd.tensor_tensor(scores[u][:, :, :].rearrange("p b (i t) -> p b i t", t=32),
                                            diag[u][:, :, :].unsqueeze(2).broadcast_to([P, 4, 4, 32]),
                                            own_32[:, :].unsqueeze(1).unsqueeze(3).broadcast_to([P, 4, 4, 32]),
                                            ALU.mult).then_inc(placed.sem(u), 1)
                elif name == "rms":
                    pool.wait_ge(*ms_made.done(3, h))
                    pool.wait_ge(*rstd_on_psum.previous("all", h))
                    nc.gpsimd.tensor_tensor(rstd[:, :], ms[:, :], minus_half[:, :], ALU.pow).then_inc(rstd_made.sem("all"), 1)

            for st in first_steps:
                step(st, 0)
            with pool.Fori(0, HEADS - 1) as h:
                for ahead, *st in steps:
                    step(st, h + 1 if ahead else h)
            for st in last_steps:
                step(st, HEADS - 1)

        @block.vector
        def _(dve):
            for x in (q_at, total_at, masked_at, summed, states, ms_made, mixed_at, rstd_copied, head_lb):
                x.credit(dve)
            for sem in (*left.values(), rstd_left):
                dve.sem_inc(sem, 16)

            def step(st, h):
                name, u = st[0:2]
                n = 0 if u in ("all", "lb") else tokens(u)
                if name == "bound":
                    dve.wait_ge(*gates_made.previous(3, h))
                    nc.vector.tensor_copy(lb_now[:, 0:1], lb[:, bass.ds(h, 1)])
                    nc.vector.tensor_copy(lb_now[:, 1:2], one_less_lb[:, bass.ds(h, 1)]).then_inc(head_lb.sem("lb"), 1)
                elif name == "product":
                    dve.wait_ge(*gates_made.done(u, h))
                    dve.wait_ge(*read.previous(u, h))
                    nc.vector.tensor_tensor(dq[u][:, :], raw[u][:, q_i, :], decay[u][:, :], ALU.mult
                                        ).then_inc(q_at.sem((u, 1)), 1)
                elif name == "level":
                    half = st[2]
                    pairs = total(u, half)
                    if half > 1:
                        dve.wait_ge(*total_at.done((u, half), h))
                    dve.wait_ge(*k_at.previous((u, halves(u)[-1] * 2), h))
                    wide = total(u, 2 * half)
                    out = wide if len(wide.shape) == 2 else wide.rearrange("p m two -> p (m two)")
                    nc.vector.tensor_tensor(out.unsqueeze(2), pairs[:, :, 0:1], pairs[:, :, 1:2], ALU.mult
                                            ).then_inc(total_at.sem((u, 2 * half)), 1)
                    dve.wait_ge(*scored.done((u, half), h))
                    dve.wait_ge(*q_at.done((u, half), h))
                    right_half = by_halves(dq, u, half)[:, :, 1, :]
                    nc.vector.tensor_tensor(right_half, right_half, pairs[:, :, 0:1].broadcast_to(list(right_half.shape)),
                                            ALU.mult).then_inc(q_at.sem((u, 2 * half)), 1)
                elif name in ("mask", "sum"):
                    last_small = min(16, halves(u)[-1])
                    levels = 1 + len([x for x in halves(u) if x <= 16])
                    w, nb = min(32, width(u)), n // width(u)
                    rows = slice(0, P if u != "m" else w)
                    within = masked[u if u == "m" else SLOT[u]][rows, 0:levels, 0:nb, 0:w]
                    if name == "mask":
                        dve.wait_ge(*scored.done((u, last_small), h))
                        nc.vector.tensor_tensor(within, (meta_small if u == "m" else small[SLOT[u]])[rows, 0:levels, 0:nb, 0:w],
                                                masks[rows, 0:levels, 0:w].unsqueeze(2).broadcast_to([rows.stop, levels, nb, w]),
                                                ALU.mult).then_inc(masked_at.sem(u), 1)
                    else:
                        dve.wait_ge(*masked_at.done(u, h))
                        if u == "m":
                            dve.wait_ge(*read.previous(u, h))
                        else:
                            dve.wait_ge(*placed.previous(u, h))
                        nc.vector.tensor_reduce(diag[u][rows, 0:nb, 0:w], within.rearrange("p l b t -> p b t l"),
                                                AX_X, ALU.add).then_inc(summed.sem(u), 1)
                elif name == "carry":
                    dve.wait_ge(*k_added.done(u, h))
                    if u == "m":
                        dve.wait_ge(*read.previous(0, h))
                        nc.vector.tensor_copy(state[0][:, 0, :], added[:, 0:P]).then_inc(states.sem((u, 0)), 1)
                    else:
                        dve.wait_ge(*total_at.done((u, P), h))
                        if u < 3:
                            dve.wait_ge(*read.previous(u + 1, h))
                        for i in range(added_blocks(u)):
                            before = (u, i - 1) if i else (("m", 0) if u == 0 else (u - 1, 3))
                            dve.wait_ge(*states.done(before, h))
                            to = state[u][:, i + 1, :] if i < 3 else state[u + 1][:, 0, :]
                            nc.vector.scalar_tensor_tensor(to, state[u][:, i, :], total(u, P)[:, i:i + 1],
                                                           added[:, i * P:(i + 1) * P], ALU.mult, ALU.add
                                                           ).then_inc(states.sem((u, i)), 1)
                elif name == "norm":
                    dve.wait_ge(*meaned.done(u, h))
                    dve.wait_ge(*rstd_made.previous("all", h))
                    nb, first = n // width(u), 0 if u == "m" else 1 + 4 * u
                    nc.vector.tensor_scalar(ms[0:width(u), first:first + nb], added[0:width(u), 0:nb], EPS, None, ALU.add
                                            ).then_inc(ms_made.sem(u), 1)
                elif name == "out":
                    dve.wait_ge(*read.done(u, h))
                    dve.wait_ge(*squared.done(u, h))
                    dve.wait_ge(*silu_made.done(u, h))
                    dve.wait_ge(left[u], h * 16 + 16)
                    nc.vector.scalar_tensor_tensor(result[u][:, :], o[:, 0:n], out_gain[:, 0:1], gate[u][:, :],
                                                   ALU.mult, ALU.mult).then_inc(mixed_at.sem(u), 1)
                elif name == "rms_out":
                    dve.wait_ge(*rstd_on_psum.done("all", h))
                    dve.wait_ge(rstd_left, h * 16 + 16)
                    nc.vector.tensor_copy(rstd_turned[:, :], added[0:1 + TILES, 0:P]).then_inc(rstd_copied.sem("all"), 1)

            for st in first_steps:
                step(st, 0)
            with dve.Fori(0, HEADS - 1) as h:
                for ahead, *st in steps:
                    step(st, h + 1 if ahead else h)
            for st in last_steps:
                step(st, HEADS - 1)

        @block.tensor
        def _(pe):
            for x in (scored, v_turned, k_turned, k_added, read, meaned, rstd_on_psum):
                x.credit(pe)

            def before(order, u, h):
                return order.previous(UNITS[-1], h) if u == UNITS[0] else order.done(UNITS[UNITS.index(u) - 1], h)

            def step(st, h):
                name, u = st[0:2]
                w = 0 if u in ("all", "lb") else width(u)
                if name == "turn_v":
                    pe.wait_ge(raw_in[u], h * 16 + 16)
                    pe.wait_ge(*(masked_at.done("m", h) if u == 2 else before(v_made, u, h)))
                    for i, cols in blocks(u):
                        last = nc.tensor.transpose(turned_v[0:w, i, :], raw[u][:, v_i, cols], common.ident[:, :])
                    last.then_inc(v_turned.sem(u), 1)
                elif name == "level":
                    half, ps = st[2], meta_small if u == "m" else small[SLOT[u]]
                    pe.wait_ge(*q_at.done((u, half), h))
                    if half > 1:
                        pe.wait_ge(*k_at.done((u, half), h))
                    elif u == "m":
                        pe.wait_ge(*v_made.done(1, h))
                    else:
                        pe.wait_ge(*(spread.done(u - 2, h) if u > 1 else spread.previous(u + 2, h)))
                    if half == 32:
                        pe.wait_ge(*masked_at.done(u, h))
                    if half == 64:
                        half64 = ps[0:64, 0:2, :, :].rearrange("p a b t -> p (a b t)").rearrange("p (b t) -> p b t", t=64)
                    for i, cols in blocks(u):
                        c = cols.start
                        if half == 64:
                            last = nc.tensor.matmul(half64[:, i, :], dk[u][:, c:c + 64], dq[u][:, c + 64:c + 128],
                                                    start=True, stop=True)
                        elif half == 32:
                            for p0 in (0, 64):
                                last = nc.tensor.matmul(ps[p0:p0 + 32, 6, i, :], dk[u][:, c + p0:c + p0 + 32],
                                                        dq[u][:, c + p0 + 32:c + p0 + 64], start=True, stop=True)
                        else:
                            level = half.bit_length()
                            for p0 in range(0, w, 32):
                                n = min(32, w)
                                part = slice(c + p0, c + p0 + n)
                                if half == 1:
                                    nc.tensor.matmul(ps[p0:p0 + n, 0, i, 0:n], dk[u][:, part], raw[u][:, q_i, part],
                                                     start=True, stop=True)
                                last = nc.tensor.matmul(ps[p0:p0 + n, level, i, 0:n], dk[u][:, part], dq[u][:, part],
                                                        start=True, stop=True)
                    last.then_inc(scored.sem((u, half)), 1)
                elif name == "turn_k":
                    pe.wait_ge(*k_at.done((u, w), h))
                    pe.wait_ge(*before(k_made, u, h))
                    for i, cols in blocks(u):
                        last = nc.tensor.transpose(turned_k[0:w, i, :], dk[u][:, cols], common.ident[:, :])
                    last.then_inc(k_turned.sem(u), 1)
                elif name == "carry":
                    pe.wait_ge(*v_made.done(u, h))
                    pe.wait_ge(*k_made.done(u, h))
                    for prior in added_users[("carry", u)]:
                        pe.wait_ge(*prior(h))
                    for i, cols in blocks(u)[0:added_blocks(u)]:
                        last = nc.tensor.matmul(added[:, i * P:(i + 1) * P], kT[u][0:w, i, :], v[u][0:w, i, :],
                                                start=True, stop=True)
                    last.then_inc(k_added.sem(u), 1)
                elif name == "out":
                    pe.wait_ge(*before(mixed_at, u, h))
                    if u == "m":
                        pe.wait_ge(*summed.done(u, h))
                        last = nc.tensor.matmul(o[:, 0:w], v[u][0:w, 0, :], diag[u][0:w, 0, 0:w], start=True, stop=True)
                    else:
                        pe.wait_ge(*placed.done(u, h))
                        pe.wait_ge(*spread.done(u, h))
                        pe.wait_ge(*states.done((u, 2), h))
                        for i, cols in blocks(u):
                            nc.tensor.matmul(o[:, cols], v[u][:, i, :], scores[u][:, i, :], start=True, stop=False)
                            last = nc.tensor.matmul(o[:, cols], state[u][:, i, :], dq[u][:, cols], start=False, stop=True)
                    last.then_inc(read.sem(u), 1)
                elif name == "norm":
                    pe.wait_ge(*squared.done(u, h))
                    for prior in added_users[("norm", u)]:
                        pe.wait_ge(*prior(h))
                    for i, cols in blocks(u):
                        last = nc.tensor.matmul(added[0:w, i:i + 1], squares[u][:, cols], mean_of[:, 0:1],
                                                start=True, stop=True)
                    last.then_inc(meaned.sem(u), 1)
                elif name == "rms_out":
                    pe.wait_ge(*rstd_made.done("all", h))
                    for prior in added_users[("rms_out", "all")]:
                        pe.wait_ge(*prior(h))
                    nc.tensor.transpose(added[0:1 + TILES, 0:P], rstd[:, :], common.ident[:, :]
                                        ).then_inc(rstd_on_psum.sem("all"), 1)

            for st in first_steps:
                step(st, 0)
            with pe.Fori(0, HEADS - 1) as h:
                for ahead, *st in steps:
                    step(st, h + 1 if ahead else h)
            for st in last_steps:
                step(st, HEADS - 1)

LEAD = 8

PREPARE = {
    1: [(0, "turn_v", 0)], 3: [(0, "gate", 0)], 4: [(0, "silu", 0), (0, "load", 0)],
    5: [(0, "turn_v", "m")], 6: [(0, "load", "m")],
    17: [(1, "queries", 3)], 18: [(1, "queries_low", 3), (1, "gate", 3)], 19: [(1, "keys", 3), (1, "silu", 3)],
    20: [(1, "keys_low", 3), (1, "turn_v", 3)], 21: [(1, "load", 3)],
    23: [(1, "keys", 2)], 24: [(1, "keys_low", 2)], 25: [(1, "queries", 2)], 26: [(1, "queries_low", 2)],
    27: [(1, "turn_v", 2)], 30: [(1, "gate", 2)], 31: [(1, "silu", 2), (1, "load", 2)],
    32: [(1, "keys", 1)], 33: [(1, "keys_low", 1)], 34: [(1, "queries", 1)], 35: [(1, "queries_low", 1)],
    36: [(1, "turn_v", 1)], 39: [(1, "gate", 1)], 40: [(1, "silu", 1), (1, "load", 1), (1, "keys", 0)],
    41: [(1, "keys_low", 0), (1, "queries", 0)], 42: [(1, "queries_low", 0), (1, "keys", "m")], 43: [(1, "keys_low", "m")],
}


def attention_steps():
    score, values = [], []
    for g in (3, 2, 1, 0):
        for c in [*range(g, -1, -1), "m"]:
            parts = [0] if c == "m" else range(4)
            score += [("score", g, c, i) for i in parts]
            values += [(g, c, j) for j in parts]
    steps = []
    for n, at in enumerate(values):
        steps.append((int(n + 1 >= len(values)), "turn") + values[(n + 1) % len(values)])
        steps.append((int(n + LEAD >= len(score)),) + score[(n + LEAD) % len(score)])
        steps.append((0, "multiply") + at)
        if at[1] == "m":
            steps.append((0, "finish", at[0]))
        steps += PREPARE.get(n, [])
    return steps


def last_user(users, slot_of):
    before = {}
    for n, user in enumerate(users):
        same = [m for m in range(len(users)) if slot_of(users[m]) == slot_of(user)]
        at = same.index(n)
        before[user] = (users[same[at - 1]], at == 0)
    return before


def attention(nc, common, stage, proj, mixed):
    steps = attention_steps()
    first_turn = ("turn", 3, 3, 0)
    first_steps = [step[1:] for step in steps if step[0]]

    def in_order(*names):
        return [step[1:] for step in sorted(steps, key=lambda step: -step[0]) if step[1] in names]

    def keys(name):
        return [step[1:] if len(step) > 2 else step[1] for step in in_order(name)]

    CHUNKS = ("m", 0, 1, 2, 3)
    with ExitStack() as ctx:
        s = Space(nc, ctx, stage)
        q_i, k_i, v_i, g_i = range(4)
        raw = s.sb("raw", [P, 4, TOK])
        k_high, k_low, q_high, q_low = (s.sb(n, [P, TOK], F32R) for n in ("k_high", "k_low", "q_high", "q_low"))
        v = s.sb("v", [P, 1 + TILES, P])
        gate = s.sb("gate", [P, TOK])
        keep = {n: s.sb(f"keep{n}", [P, 4, META if n == "m" else 512]) for n in (0, 1, "m")}
        beta = {n: s.sb(f"beta{n}", [P, 4, META if n == "m" else 512]) for n in (0, 1, "m")}
        a = {n: s.sb(f"a{n}", [P, 4, META if n == "m" else 512]) for n in (0, 1, 2, 3, "m")}
        left_over = s.sb("left_over", [P, 4, TOK + 1])
        aT = [s.sb(f"aT{i}", [P, 512]) for i in range(2)]
        result = [s.sb(f"result{i}", [P, 512]) for i in range(2)]
        z = [s.ps(f"z{i}", [P, 512]) for i in range(4)]
        turned = [s.ps(f"turned{i}", [P, 4, P]) for i in range(2)]
        o = [s.ps(f"o{i}", [P, 512]) for i in range(2)]

        raw_in = {c: s.sem(f"raw_in_{c}") for c in CHUNKS}
        stored = [s.sem(f"stored{i}") for i in range(2)]
        q_high_made, k_high_made = s.order("q_high_made", keys("queries")), s.order("k_high_made", keys("keys"))
        q_low_made, k_low_made = s.order("q_low_made", keys("queries_low")), s.order("k_low_made", keys("keys_low"))
        gate_sig_made = s.order("gate_sig_made", keys("gate"))
        gate_made = s.order("gate_made", keys("silu"))
        v_turned = s.order("v_turned", keys("turn_v"))
        v_made = s.order("v_made", keys("turn_v"))
        scored = s.order("scored", keys("score"))
        keep_made, beta_made = s.order("keep_made", keys("score")), s.order("beta_made", keys("score"))
        diagonal = [(g, c, i) for g, c, i in keys("score") if c == g]
        cut_off = s.order("cut_off", diagonal)
        scanned = s.order("scanned", keys("score"))
        a_made = s.order("a_made", keys("score"))
        a_turned = s.order("a_turned", keys("turn"))
        aT_made = s.order("aT_made", keys("turn"))
        multiplied = s.order("multiplied", keys("multiply"))
        finished = s.order("finished", keys("finish"))

        units = [(g, c) for g, c, i in keys("score") if i == 0]
        wide_units = [u for u in units if u[1] != "m"]
        sig_slot = {u: "m" if u[1] == "m" else wide_units.index(u) % 2 for u in units}
        a_slot = {u: "m" if u[1] == "m" else 3 if u == wide_units[-1] else wide_units.index(u) % 3 for u in units}

        def tiles_of(c):
            return (0,) if c == "m" else range(4)

        def last_of(c):
            return 0 if c == "m" else 3

        turns = [st for st in steps if st[1] in ("turn_v", "turn")]
        turned_slot = {st[1:]: n % 2 for n, st in enumerate(turns)}
        turned_before = {}
        for n, (ahead, *st) in enumerate(turns):
            back = next(m for m in range(n - 1, n - 4, -1) if turned_slot[turns[m][1:]] == turned_slot[tuple(st)])
            turned_before[tuple(st)] = (turns[back][1:], turns[back][0] - ahead - (back < 0))
        aT_slot = {k: n % 2 for n, k in enumerate(keys("turn"))}
        aT_before = last_user(keys("turn"), lambda k: aT_slot[k])
        z_slot = {k: n % 4 for n, k in enumerate(keys("score"))}
        z_before = last_user(keys("score"), lambda k: z_slot[k])
        sig_before = last_user(units, lambda u: sig_slot[u])
        a_before = last_user(units, lambda u: a_slot[u])
        o_before = last_user(keys("finish"), lambda g: g % 2)

        def row_before(g, c, i):
            prior = g + 1 if g < 3 else (0 if c == "m" else c)
            return ((prior, "m", 0) if c in ("m", 0) else (prior, c - 1, i)), g == 3

        proj_h = proj.rearrange("(a h) p t -> h p a t", a=4)
        block = ctx.enter_context(nc.Block())

        def span(c):
            return slice(0, META) if c == "m" else slice(META + c * 512, META + (c + 1) * 512)

        def value(order, key, before, rnd):
            return order.previous(key, rnd) if before else order.done(key, rnd)

        def turned_part(part, st):
            _, g, c, j = st
            i0, rows = (j if c == g else 0), slice(0, META if c == "m" else P)
            return (part[aT_slot[(g, c, j)]][rows, i0 * P:512],
                    turned[turned_slot[st]][rows, i0:4, :].rearrange("p i t -> p (i t)"))

        @block.sync
        def _(sp):
            def load(c, head):
                sp.dma_start(raw[:, :, span(c)], proj_h[bass.ds(head, 1), :, :, span(c)].rearrange("h p a t -> (h p) a t")
                             ).then_inc(raw_in[c], 16)

            def reload(c, rnd, head):
                for order in (k_low_made, v_turned) + (() if c == "m" else (q_low_made, gate_made)):
                    common.wait_apart(sp, order.sem, order.done(c, rnd))
                load(c, head)

            def store(g, h):
                common.wait_apart(sp, finished.sem, finished.done(g, h))
                sp.dma_start(mixed[bass.ds(h, 1), :, span(g)].rearrange("h p t -> (h p) t"), result[g % 2][:, :]
                             ).then_inc(stored[g % 2], 16)

            def head(h, late=False):
                for ahead, name, *rest in steps:
                    if name == "load":
                        rnd = h + 1 if ahead else h
                        if not late:
                            reload(rest[0], rnd, h + (1 + ahead))
                        elif rnd < HEADS:
                            reload(rest[0], rnd, min(rnd + 1, HEADS - 1))
                    elif name == "finish":
                        store(rest[0], h)

            for c in (3, 2, 1, 0, "m"):
                load(c, 0)
            for name, *rest in first_steps:
                if name == "load":
                    reload(rest[0], 0, 1)
            with sp.Fori(0, HEADS - 2) as h:
                head(h)
            head(HEADS - 2, late=True)
            head(HEADS - 1, late=True)
            for i in range(2):
                sp.wait_ge(stored[i], 16 * 2 * HEADS + 16)

        @block.scalar
        def _(act):
            for x in (q_high_made, k_high_made, gate_sig_made, v_made, keep_made, beta_made):
                x.credit(act)
            def step(st, h):
                if st[0] in ("queries", "keys"):
                    c = st[1]
                    act.wait_ge(raw_in[c], h * 16 + 16)
                    act.wait_ge(scored.sem, scored.previous((0 if c == "m" else c, "m", 0), h))
                    if st[0] == "queries":
                        nc.scalar.activation(q_high[:, span(c)], raw[:, q_i, span(c)], ACT.Copy).then_inc(q_high_made.sem, 1)
                    else:
                        nc.scalar.activation(k_high[:, span(c)], raw[:, k_i, span(c)], ACT.Copy).then_inc(k_high_made.sem, 1)
                elif st[0] == "gate":
                    c = st[1]
                    act.wait_ge(raw_in[c], h * 16 + 16)
                    act.wait_ge(finished.sem, finished.previous(c, h))
                    nc.scalar.activation(gate[:, span(c)], raw[:, g_i, span(c)], ACT.Sigmoid).then_inc(gate_sig_made.sem, 1)
                elif st[0] == "turn_v":
                    c = st[1]
                    act.wait_ge(v_turned.sem, v_turned.done(c, h))
                    act.wait_ge(multiplied.sem, multiplied.previous((0 if c == "m" else c, c, last_of(c)), h))
                    ps = turned[turned_slot[st]]
                    if c == "m":
                        nc.scalar.activation(v[0:META, 0, :], ps[0:META, 0, :], ACT.Copy).then_inc(v_made.sem, 1)
                    else:
                        nc.scalar.activation(v[:, 1 + 4 * c:5 + 4 * c, :], ps[:, :, :], ACT.Copy
                                             ).then_inc(v_made.sem, 1)
                elif st[0] == "score":
                    _, g, c, i = st
                    key = (g, c, i)
                    act.wait_ge(scored.sem, scored.done(key, h))
                    (pg, pc), wrapped = sig_before[(g, c)]
                    act.wait_ge(a_made.sem, value(a_made, (pg, pc, i), wrapped, h))
                    n = sig_slot[(g, c)]
                    if c == "m":
                        zi, to_keep, to_beta = z[z_slot[key]][:, 0:4 * META], keep[n][:, :, 0:META], beta[n][:, :, 0:META]
                        zi = zi.rearrange("p (i s) -> p i s", s=META)
                    else:
                        nk = P * (i + 1) if c == g else 512
                        zi, to_keep, to_beta = z[z_slot[key]][:, 0:nk], keep[n][:, i, 0:nk], beta[n][:, i, 0:nk]
                    nc.scalar.activation(to_keep, zi, ACT.Sigmoid, scale=-SB_SCALE).then_inc(keep_made.sem, 1)
                    nc.scalar.activation(to_beta, zi, ACT.Sigmoid, scale=SB_SCALE).then_inc(beta_made.sem, 1)

            for st in first_steps:
                step(st, 0)
            with act.Fori(0, HEADS) as h:
                for st in steps:
                    step(st[1:], h + 1 if st[0] else h)

        @block.gpsimd
        def _(pool):
            for x in (gate_made, cut_off, a_made):
                x.credit(pool)
            def step(st, h):
                if st[0] == "silu":
                    c = st[1]
                    pool.wait_ge(gate_sig_made.sem, gate_sig_made.done(c, h))
                    nc.gpsimd.tensor_tensor(gate[:, span(c)], raw[:, g_i, span(c)], gate[:, span(c)], ALU.mult
                                            ).then_inc(gate_made.sem, 1)
                elif st[0] == "score":
                    _, g, c, i = st
                    key = (g, c, i)
                    n, to = sig_slot[(g, c)], a[a_slot[(g, c)]]
                    if c == g:
                        own = slice(i * P, (i + 1) * P)
                        common.wait_apart(pool, beta_made.sem, beta_made.done(key, h))
                        for tile, fill in ((keep, 1.0), (beta, 0.0)):
                            last = nc.gpsimd.affine_select(out=tile[n][:, i, own], in_=tile[n][:, i, own],
                                                           compare_op=ALU.is_gt, fill=fill, base=0,
                                                           pattern=[[-1, P]], channel_multiplier=1)
                        last.then_inc(cut_off.sem, 1)
                        pool.wait_ge(cut_off.sem, cut_off.done(key, h))
                    else:
                        pool.wait_ge(beta_made.sem, beta_made.done(key, h))
                    pool.wait_ge(scanned.sem, scanned.done(key, h))
                    (pg, pc), wrapped = a_before[(g, c)]
                    pool.wait_ge(a_turned.sem, value(a_turned, (pg, pc, last_of(pc)), wrapped, h))
                    if c == "m":
                        nc.gpsimd.tensor_tensor(to[:, :, 0:META], beta[n][:, :, 0:META],
                                                left_over[:, :, 1:1 + META], ALU.mult).then_inc(a_made.sem, 1)
                    else:
                        nk, first = (P * (i + 1) if c == g else 512), span(c).start
                        nc.gpsimd.tensor_tensor(to[:, i, 0:nk], beta[n][:, i, 0:nk],
                                                left_over[:, i, first + 1:first + 1 + nk], ALU.mult
                                                ).then_inc(a_made.sem, 1)

            for st in first_steps:
                step(st, 0)
            with pool.Fori(0, HEADS) as h:
                for st in steps:
                    step(st[1:], h + 1 if st[0] else h)

        @block.vector
        def _(dve):
            for x in (q_low_made, k_low_made, scanned, aT_made, finished):
                x.credit(dve)
            for sem in stored:
                dve.sem_inc(sem, 16)
            def step(st, h):
                if st[0] == "queries_low":
                    cols = span(st[1])
                    dve.wait_ge(q_high_made.sem, q_high_made.done(st[1], h))
                    nc.vector.tensor_tensor(q_low[:, cols], raw[:, q_i, cols], q_high[:, cols].bitcast(F32), ALU.subtract
                                            ).then_inc(q_low_made.sem, 1)
                elif st[0] == "keys_low":
                    cols = span(st[1])
                    dve.wait_ge(k_high_made.sem, k_high_made.done(st[1], h))
                    nc.vector.tensor_tensor(k_low[:, cols], raw[:, k_i, cols], k_high[:, cols].bitcast(F32), ALU.subtract
                                            ).then_inc(k_low_made.sem, 1)
                elif st[0] == "score":
                    _, g, c, i = st
                    key = (g, c, i)
                    n, first = sig_slot[(g, c)], span(c).start
                    prior, wrapped = row_before(*key)
                    dve.wait_ge(a_made.sem, value(a_made, prior, wrapped, h))
                    if c == g:
                        nk = P * (i + 1)
                        nc.vector.memset(left_over[:, i, first + nk:first + nk + 1], 1.0)
                        dve.wait_ge(cut_off.sem, cut_off.done(key, h))
                    else:
                        nk = META if c == "m" else 512
                        dve.wait_ge(keep_made.sem, keep_made.done(key, h))
                        later = (g, 0 if c == "m" else c + 1, 3 if c == "m" else i)
                        dve.wait_ge(scanned.sem, scanned.done(later, h))
                    for t in (range(4) if c == "m" else (i,)):
                        row = left_over[:, t, first:first + nk]
                        data = keep[n][:, t, 0:nk]
                        start = 1.0 if c == g else left_over[:, t, first + nk:first + nk + 1]
                        last = nc.vector.tensor_tensor_scan(row[:, ::-1], data[:, ::-1], data[:, ::-1], start,
                                                            ALU.mult, ALU.bypass)
                    last.then_inc(scanned.sem, 1)
                elif st[0] == "turn":
                    _, g, c, j = st
                    key = (g, c, j)
                    dve.wait_ge(a_turned.sem, a_turned.done(key, h))
                    prior, wrapped = aT_before[key]
                    dve.wait_ge(multiplied.sem, value(multiplied, prior, wrapped, h))
                    nc.vector.tensor_copy(*turned_part(aT, st)).then_inc(aT_made.sem, 1)
                elif st[0] == "finish":
                    g = st[1]
                    dve.wait_ge(multiplied.sem, multiplied.done((g, "m", 0), h))
                    dve.wait_ge(gate_made.sem, gate_made.done(g, h))
                    dve.wait_ge(stored[g % 2], h * 32 + (16 + 16 * ((3 - g) // 2)))
                    nc.vector.tensor_tensor(result[g % 2][:, :], o[g % 2][:, :], gate[:, span(g)], ALU.mult
                                            ).then_inc(finished.sem, 1)

            for st in first_steps:
                step(st, 0)
            with dve.Fori(0, HEADS) as h:
                for st in steps:
                    step(st[1:], h + 1 if st[0] else h)

        @block.tensor
        def _(pe):
            for x in (v_turned, scored, a_turned, multiplied):
                x.credit(pe)

            def wait_turned(st, h):
                prior, rounds = turned_before[st]
                order = v_made if prior[0] == "turn_v" else aT_made
                key = prior[1] if prior[0] == "turn_v" else prior[1:]
                rnd = h if rounds == 0 else h + rounds
                pe.wait_ge(order.sem, order.previous(key, h) if rounds == -1 else order.done(key, rnd))
                chunks = v_made.keys
                if st == first_turn:
                    pe.wait_ge(v_made.sem, v_made.done(1, h))
                elif st == ("turn_v", chunks[0]):
                    pe.wait_ge(v_made.sem, v_made.previous(chunks[-1], h))
                elif st[0] == "turn_v":
                    pe.wait_ge(v_made.sem, v_made.done(chunks[chunks.index(st[1]) - 1], h))

            def step(st, h):
                if st[0] == "turn_v":
                    c = st[1]
                    pe.wait_ge(raw_in[c], h * 16 + 16)
                    wait_turned(st, h)
                    ps = turned[turned_slot[st]]
                    w, cols = (META if c == "m" else P), span(c)
                    for j in tiles_of(c):
                        last = nc.tensor.transpose(ps[0:w, j, :], raw[:, v_i, cols.start + j * P:cols.start + j * P + w],
                                                   common.ident[:, :])
                    last.then_inc(v_turned.sem, 1)
                elif st[0] == "score":
                    _, g, c, i = st
                    pe.wait_ge(q_low_made.sem, q_low_made.done(g, h))
                    pe.wait_ge(k_low_made.sem, k_low_made.done(c, h))
                    prior, wrapped = z_before[(g, c, i)]
                    pe.wait_ge(beta_made.sem, value(beta_made, prior, wrapped, h))
                    nk = META if c == "m" else P * (i + 1) if c == g else 512
                    ks = slice(span(c).start, span(c).start + nk)
                    for t in (range(4) if c == "m" else (i,)):
                        qs = slice(span(g).start + t * P, span(g).start + (t + 1) * P)
                        bank = z[z_slot[(g, c, i)]]
                        to = bank[:, t * META:(t + 1) * META] if c == "m" else bank[:, 0:nk]
                        nc.tensor.matmul(to, q_high[:, qs], k_high[:, ks], start=True, stop=False)
                        nc.tensor.matmul(to, q_high[:, qs], k_low[:, ks], start=False, stop=False)
                        last = nc.tensor.matmul(to, q_low[:, qs], k_high[:, ks], start=False, stop=True)
                    last.then_inc(scored.sem, 1)
                elif st[0] == "turn":
                    _, g, c, j = st
                    pe.wait_ge(a_made.sem, a_made.done((g, c, last_of(c)), h))
                    wait_turned(st, h)
                    of_unit, w = a[a_slot[(g, c)]], (META if c == "m" else P)
                    for i in range(j if c == g else 0, 4):
                        last = nc.tensor.transpose(turned[turned_slot[st]][0:w, i, :], of_unit[:, i, j * P:j * P + w],
                                                   common.ident[:, :])
                    last.then_inc(a_turned.sem, 1)
                elif st[0] == "multiply":
                    _, g, c, j = st
                    key = (g, c, j)
                    pe.wait_ge(aT_made.sem, aT_made.done(key, h))
                    pe.wait_ge(v_made.sem, v_made.done(c, h))
                    if c == g and j == 0:
                        prior, wrapped = o_before[g]
                        pe.wait_ge(finished.sem, value(finished, prior, wrapped, h))
                    i0, w = (j if c == g else 0), (META if c == "m" else P)
                    tile = 0 if c == "m" else 1 + 4 * c + j
                    nc.tensor.matmul(o[g % 2][:, i0 * P:512], v[0:w, tile, :], aT[aT_slot[key]][0:w, i0 * P:512],
                                     start=(c == g and j == 0), stop=(c == "m")).then_inc(multiplied.sem, 1)

            for st in first_steps:
                step(st, 0)
            with pe.Fori(0, HEADS) as h:
                for st in steps:
                    step(st[1:], h + 1 if st[0] else h)



def program(nc, x, meta_tokens, pre_norm, post_norm, hgrn_w_in, hgrn_lb, hgrn_out_norm, hgrn_w_out, sb_w_in, sb_w_out, level_masks, out):
    proj = nc.dram_tensor("proj", (4 * HEADS, P, TOK), F32, kind="Internal").ap()
    mixed = nc.dram_tensor("mixed", (HEADS, P, TOK), F32, kind="Internal").ap()
    h1 = nc.dram_tensor("h1", (TOK, D), F32, kind="Internal").ap()
    rstd_rows = nc.dram_tensor("rstd_rows", (HEADS, 1 + TILES, P), F32, kind="Internal").ap()
    rows = x[0]
    with ExitStack() as ctx:
        s = Space(nc, ctx, "all")
        ident = s.sb("ident", [P, P])
        made = s.sem("made")
        with nc.Block() as block:
            @block.gpsimd
            def _(pool):
                nc.gpsimd.memset(ident[:, :], 1.0).then_inc(made, 1)
                pool.wait_ge(made, 1)
                nc.gpsimd.affine_select(out=ident[:, :], in_=ident[:, :], compare_op=ALU.is_equal, fill=0.0,
                                        base=0, pattern=[[-1, P]], channel_multiplier=1).then_inc(made, 1)
                pool.wait_ge(made, 2)

        common = Common(ident, s.sem("apart"))
        with ExitStack() as yctx:
            y = Space(nc, yctx, "y0")
            yT_high, yT_low = (y.sb(n, [P, KT, TOK], F32R) for n in ("high", "low"))
            with nc.cleanup_on_exit():
                normalise(nc, "n0", meta_tokens, rows, pre_norm[0], common, yT_high, yT_low, hgrn_w_in[0], proj)
            with nc.cleanup_on_exit():
                project(nc, "p0", hgrn_w_in[0], yT_high, yT_low, proj)
        with nc.cleanup_on_exit():
            recurrence(nc, common, "r0", proj, hgrn_lb, hgrn_out_norm[0], level_masks, mixed, rstd_rows)
        with nc.cleanup_on_exit():
            contract(nc, common, "c0", mixed, rstd_rows, hgrn_w_out[0], post_norm[0], meta_tokens, rows, h1[0:META, :], h1[META:TOK, :])
        with ExitStack() as yctx:
            y = Space(nc, yctx, "y1")
            yT_high, yT_low = (y.sb(n, [P, KT, TOK], F32R) for n in ("high", "low"))
            with nc.cleanup_on_exit():
                normalise(nc, "n1", h1[0:META, :], h1[META:TOK, :], pre_norm[1], common, yT_high, yT_low, sb_w_in[0], proj)
            with nc.cleanup_on_exit():
                project(nc, "p1", sb_w_in[0], yT_high, yT_low, proj)
        with nc.cleanup_on_exit():
            attention(nc, common, "a1", proj, mixed)
        with nc.cleanup_on_exit():
            contract(nc, common, "c1", mixed, None, sb_w_out[0], post_norm[1], None, h1[META:TOK, :], None, out[0])


OUT_SHAPE = (1, SEQ, D)
INPUTS = ("x", "meta_tokens", "pre_norm", "post_norm", "hgrn_w_in", "hgrn_lb", "hgrn_out_norm", "hgrn_w_out",
          "sb_w_in", "sb_w_out")


def small_level_masks():
    s, t = np.arange(P)[:, None, None] % 32, np.arange(32)[None, None, :]
    size = 2 ** np.arange(1, 6)[None, :, None]
    level = (s // size == t // size) & (s % size < size // 2) & (t % size >= size // 2)
    own = np.arange(P)[:, None] // 32 == np.arange(4)[None, :]
    return np.concatenate([np.concatenate([s == t, level], axis=1).reshape(P, 6 * 32), own], axis=1).astype(np.float32)


def kernel(**inputs):
    import concourse.bacc as bacc
    from concourse.bass_utils import run_bass_kernel_spmd

    nc = bacc.Bacc("TRN2", target_bir_lowering=False, num_devices=1)
    arrays, args = {}, []
    for name in INPUTS:
        a = np.ascontiguousarray(inputs[name])
        if name == "hgrn_lb":
            a = np.ascontiguousarray(a.reshape(2, HEADS, P).transpose(2, 0, 1))
        arrays[f"in_{name}"] = a
        args.append(nc.dram_tensor(f"in_{name}", a.shape, F32, kind="ExternalInput").ap())
    arrays["level_masks"] = small_level_masks()
    args.append(nc.dram_tensor("level_masks", (P, 6 * 32 + 4), F32, kind="ExternalInput").ap())
    args.append(nc.dram_tensor("out_h", OUT_SHAPE, F32, kind="ExternalOutput").ap())
    program(nc, *args)
    return run_bass_kernel_spmd(nc, [arrays], core_ids=[0]).results[0]["out_h"]
```
